# Optimizing a Trainium2 kernel written in Bass

```python
import math
import jax, jax.numpy as jnp
from jax import lax
import numpy as np

D_MODEL = 1024
BATCH = 1
SEQ = 512
DEPTH = 1
DEC_BATCH = 8
DEC_SEQ = 1
PAST_LEN = 256
PAGE_SIZE = 128

A_HEADS = 4
A_DQK = 64
A_DV = 2 * A_DQK
A_WIDTH = A_HEADS * A_DV
B_HEADS = 4
B_DH = 64
B_WIDTH = B_HEADS * B_DH
DILATED_GROUPS = ((128, 1), (512, 4), (2048, 16))
N_GROUPS = 3
N_MEM = 256
M_HEADS = 4
M_DH = 64
M_WIDTH = M_HEADS * M_DH
N_BRANCH = 3

Q_BLOCK = 128
RMS_EPS = 1e-6
NEG_INF = -1e30

IN_SPLIT_SIZES = (A_HEADS * 2 * A_DQK, A_HEADS * 2 * A_DQK, A_WIDTH, A_WIDTH,
                  N_GROUPS * 3 * B_WIDTH, B_WIDTH, M_WIDTH, M_WIDTH, N_BRANCH * D_MODEL)
IN_WIDTH = sum(IN_SPLIT_SIZES)
IN_SPLIT_POINTS = tuple(int(v) for v in np.cumsum(IN_SPLIT_SIZES)[:-1])

kernel_name = 'hybrid_diffattn_dilated_memory_decode_step'

def rms_norm(x, g):
    xf = x.astype(jnp.float32)
    y = xf * lax.rsqrt(jnp.mean(xf * xf, axis=-1, keepdims=True) + RMS_EPS)
    return (y * g.astype(jnp.float32)).astype(x.dtype)

def alibi_slopes(n_heads):
    return 2.0 ** (-8.0 * jnp.arange(1, n_heads + 1, dtype=jnp.float32) / n_heads)

def lambda_init(layer):
    return 0.8 - 0.6 * math.exp(-0.3 * layer)

def diff_lambda(lq1, lk1, lq2, lk2, lam_init):
    f32 = jnp.float32
    return (jnp.exp(jnp.sum(lq1.astype(f32) * lk1.astype(f32)))
            - jnp.exp(jnp.sum(lq2.astype(f32) * lk2.astype(f32))) + lam_init)

def branch_inputs(x, g_norm, w_in):
    b, t = x.shape[:2]
    h = rms_norm(x, g_norm) @ w_in
    qa, ka, va, za, qkv_b, zb, qm, zm, gates = jnp.split(h, IN_SPLIT_POINTS, axis=-1)
    qa = qa.reshape(b, t, A_HEADS, 2, A_DQK)
    ka = ka.reshape(b, t, A_HEADS, 2, A_DQK)
    va = va.reshape(b, t, A_HEADS, A_DV)
    qkv_b = qkv_b.reshape(b, t, N_GROUPS, 3, B_HEADS, B_DH)
    qm = qm.reshape(b, t, M_HEADS, M_DH)
    return qa, ka, va, za, qkv_b, zb, qm, zm, gates

def diff_attend(q, k, v, q_pos, k_pos, lam, lam_init, g_subln, slopes):
    s = jnp.einsum('bqhcd,bkhcd->bhcqk', q, k).astype(jnp.float32) * (A_DQK ** -0.5)
    dist = (q_pos[:, None] - k_pos[None, :]).astype(jnp.float32)
    s = s - (slopes[:, None, None, None] * dist[None, None])[None]
    s = jnp.where(dist >= 0, s, NEG_INF)
    p = jax.nn.softmax(s, axis=-1)
    a = p[:, :, 0] - lam * p[:, :, 1]
    o = jnp.einsum('bhqk,bkhe->bqhe', a.astype(v.dtype), v)
    return rms_norm(o, g_subln) * (1.0 - lam_init)

def dilated_group(q, k, v, q_idx, window, dil, slopes):
    n_keys = window // dil + 1
    j = jnp.arange(n_keys)
    idx = q_idx[:, None] - dil * j[None, :]
    valid = idx >= 0
    idx = jnp.maximum(idx, 0)
    kg = jnp.take(k, idx, axis=1)
    vg = jnp.take(v, idx, axis=1)
    s = jnp.einsum('bqhd,bqjhd->bhqj', q, kg).astype(jnp.float32) * (B_DH ** -0.5)
    s = s - slopes[:, None, None] * (dil * j).astype(jnp.float32)[None, None, :]
    s = jnp.where(valid[None, None], s, NEG_INF)
    m = jnp.max(s, axis=-1, keepdims=True)
    e = jnp.exp(s - m)
    den = jnp.sum(e, axis=-1, keepdims=True)
    o = jnp.einsum('bhqj,bqjhd->bqhd', e / den, vg.astype(jnp.float32))
    lse = (m + jnp.log(den))[..., 0]
    return o, lse

def dilated_combine(groups):
    w = jax.nn.softmax(jnp.stack([lse for _, lse in groups], axis=0), axis=0)
    w = jnp.swapaxes(w, -1, -2)[..., None]
    return jnp.sum(w * jnp.stack([o for o, _ in groups], axis=0), axis=0)

def memory_kv(mem, g_mem, w_mem_kv):
    b, n = mem.shape[:2]
    return (rms_norm(mem, g_mem) @ w_mem_kv).reshape(b, n, 2, M_HEADS, M_DH)

def memory_attend(q, kv):
    s = jnp.einsum('bqhd,bmhd->bhqm', q, kv[:, :, 0]).astype(jnp.float32) * (M_DH ** -0.5)
    p = jax.nn.softmax(s, axis=-1)
    return jnp.einsum('bhqm,bmhd->bqhd', p.astype(kv.dtype), kv[:, :, 1])

def merge_branches(x, o_a, o_b, o_m, za, zb, zm, gates, w_proj_a, w_proj_b, w_proj_m, w_out):
    b, t = x.shape[:2]
    p_a = (o_a.reshape(b, t, A_WIDTH) * jax.nn.silu(za)) @ w_proj_a
    p_b = (o_b.reshape(b, t, B_WIDTH) * jax.nn.silu(zb)) @ w_proj_b
    p_m = (o_m.reshape(b, t, M_WIDTH) * jax.nn.silu(zm)) @ w_proj_m
    g = jax.nn.sigmoid(gates).reshape(b, t, N_BRANCH, D_MODEL)
    mixed = g[:, :, 0] * p_a + g[:, :, 1] * p_b + g[:, :, 2] * p_m
    return x + mixed @ w_out

def prompt_layer(x, mem, w, layer):
    (g_norm, w_in, g_mem, w_mem_kv, lq1, lk1, lq2, lk2, g_subln,
     w_proj_a, w_proj_b, w_proj_m, w_out) = w
    b, t = x.shape[:2]
    qa, ka, va, za, qkv_b, zb, qm, zm, gates = branch_inputs(x, g_norm, w_in)
    lam_init = lambda_init(layer)
    lam = diff_lambda(lq1, lk1, lq2, lk2, lam_init)
    slopes_a = alibi_slopes(A_HEADS)
    slopes_b = alibi_slopes(B_HEADS)
    k_pos = jnp.arange(t)
    qb = [qkv_b[:, :, g, 0] for g in range(N_GROUPS)]
    kb = [qkv_b[:, :, g, 1] for g in range(N_GROUPS)]
    vb = [qkv_b[:, :, g, 2] for g in range(N_GROUPS)]

    def block(i):
        start = i * Q_BLOCK
        q_pos = start + jnp.arange(Q_BLOCK)
        o_a = diff_attend(lax.dynamic_slice_in_dim(qa, start, Q_BLOCK, axis=1), ka, va,
                          q_pos, k_pos, lam, lam_init, g_subln, slopes_a)
        groups = [dilated_group(lax.dynamic_slice_in_dim(qb[g], start, Q_BLOCK, axis=1),
                                kb[g], vb[g], q_pos, win, dil, slopes_b)
                  for g, (win, dil) in enumerate(DILATED_GROUPS)]
        return o_a, dilated_combine(groups).astype(x.dtype)

    o_a, o_b = lax.map(block, jnp.arange(t // Q_BLOCK))
    o_a = jnp.moveaxis(o_a, 0, 1).reshape(b, t, A_HEADS, A_DV)
    o_b = jnp.moveaxis(o_b, 0, 1).reshape(b, t, B_HEADS, B_DH)
    mem_kv = memory_kv(mem, g_mem, w_mem_kv)
    o_m = memory_attend(qm, mem_kv)
    h = merge_branches(x, o_a, o_b, o_m, za, zb, zm, gates, w_proj_a, w_proj_b, w_proj_m, w_out)
    diff_kv = jnp.stack([ka.reshape(b, t, A_HEADS, A_DV), va], axis=2)
    win_kv = [qkv_b[:, t - min(win, t):, g, 1:] for g, (win, _) in enumerate(DILATED_GROUPS)]
    return h, diff_kv, win_kv, mem_kv

def sample_layer(x, cache_diff_kv_l, page_table, win_caches, cache_mem_kv_l, w, layer):
    (g_norm, w_in, g_mem, w_mem_kv, lq1, lk1, lq2, lk2, g_subln,
     w_proj_a, w_proj_b, w_proj_m, w_out) = w
    del g_mem, w_mem_kv
    b, t = x.shape[:2]
    qa, ka, va, za, qkv_b, zb, qm, zm, gates = branch_inputs(x, g_norm, w_in)
    lam_init = lambda_init(layer)
    lam = diff_lambda(lq1, lk1, lq2, lk2, lam_init)
    past = cache_diff_kv_l[page_table]
    past = past.reshape(b, -1, 2, A_HEADS, A_DV)
    p_len = past.shape[1]
    k_all = jnp.concatenate([past[:, :, 0], ka.reshape(b, t, A_HEADS, A_DV)], axis=1)
    k_all = k_all.reshape(b, p_len + t, A_HEADS, 2, A_DQK)
    v_all = jnp.concatenate([past[:, :, 1], va], axis=1)
    q_pos = p_len + jnp.arange(t)
    k_pos = jnp.arange(p_len + t)
    o_a = diff_attend(qa, k_all, v_all, q_pos, k_pos, lam, lam_init, g_subln, alibi_slopes(A_HEADS))
    slopes_b = alibi_slopes(B_HEADS)
    groups = []
    for g, (win, dil) in enumerate(DILATED_GROUPS):
        buf = win_caches[g]
        lg = buf.shape[1]
        k = jnp.concatenate([buf[:, :, 0], qkv_b[:, :, g, 1]], axis=1)
        v = jnp.concatenate([buf[:, :, 1], qkv_b[:, :, g, 2]], axis=1)
        groups.append(dilated_group(qkv_b[:, :, g, 0], k, v, lg + jnp.arange(t), win, dil, slopes_b))
    o_b = dilated_combine(groups).astype(x.dtype)
    o_m = memory_attend(qm, cache_mem_kv_l)
    h = merge_branches(x, o_a, o_b, o_m, za, zb, zm, gates, w_proj_a, w_proj_b, w_proj_m, w_out)
    diff_kv = jnp.stack([ka.reshape(b, t, A_HEADS, A_DV), va], axis=2)
    win_kv = [qkv_b[:, :, g, 1:] for g in range(N_GROUPS)]
    return h, diff_kv, win_kv

def setup_inputs(seed: int = 0) -> dict:
    key = jax.random.key(seed)
    ks = jax.random.split(key, 24)
    f32 = jnp.float32

    def nrm(k, shape, scale=1.0):
        return scale * jax.random.normal(k, shape, f32)

    n_pages = PAST_LEN // PAGE_SIZE
    n_used = DEC_BATCH * n_pages
    n_pool = n_used + max(1, n_used // 4)
    page_table = jax.random.permutation(ks[0], n_pool)[:n_used].reshape(DEC_BATCH, n_pages).astype(jnp.int32)
    wl = [min(win, PAST_LEN) for win, _ in DILATED_GROUPS]
    return {
        'x_prompt': nrm(ks[1], (BATCH, SEQ, D_MODEL)),
        'x_sample': nrm(ks[2], (DEC_BATCH, DEC_SEQ, D_MODEL)),
        'mem_prompt': nrm(ks[3], (BATCH, N_MEM, D_MODEL)),
        'cache_diff_kv': nrm(ks[4], (DEPTH, n_pool, PAGE_SIZE, 2, A_HEADS, A_DV)),
        'page_table': page_table,
        'cache_win1_kv': nrm(ks[5], (DEPTH, DEC_BATCH, wl[0], 2, B_HEADS, B_DH)),
        'cache_win2_kv': nrm(ks[6], (DEPTH, DEC_BATCH, wl[1], 2, B_HEADS, B_DH)),
        'cache_win3_kv': nrm(ks[7], (DEPTH, DEC_BATCH, wl[2], 2, B_HEADS, B_DH)),
        'cache_mem_kv': nrm(ks[8], (DEPTH, DEC_BATCH, N_MEM, 2, M_HEADS, M_DH)),
        'g_norm': 1.0 + nrm(ks[9], (DEPTH, D_MODEL), 0.02),
        'w_in': nrm(ks[10], (DEPTH, D_MODEL, IN_WIDTH), D_MODEL ** -0.5),
        'g_mem': 1.0 + nrm(ks[11], (DEPTH, D_MODEL), 0.02),
        'w_mem_kv': nrm(ks[12], (DEPTH, D_MODEL, 2 * M_WIDTH), D_MODEL ** -0.5),
        'lambda_q1': nrm(ks[13], (DEPTH, A_DQK), 0.1),
        'lambda_k1': nrm(ks[14], (DEPTH, A_DQK), 0.1),
        'lambda_q2': nrm(ks[15], (DEPTH, A_DQK), 0.1),
        'lambda_k2': nrm(ks[16], (DEPTH, A_DQK), 0.1),
        'g_subln': 1.0 + nrm(ks[17], (DEPTH, A_DV), 0.02),
        'w_proj_a': nrm(ks[18], (DEPTH, A_WIDTH, D_MODEL), A_WIDTH ** -0.5),
        'w_proj_b': nrm(ks[19], (DEPTH, B_WIDTH, D_MODEL), B_WIDTH ** -0.5),
        'w_proj_m': nrm(ks[20], (DEPTH, M_WIDTH, D_MODEL), M_WIDTH ** -0.5),
        'w_out': nrm(ks[21], (DEPTH, D_MODEL, D_MODEL), D_MODEL ** -0.5),
        'g_final': 1.0 + nrm(ks[22], (D_MODEL,), 0.02),
    }

def reference(x_prompt, x_sample, mem_prompt, cache_diff_kv, page_table, cache_win1_kv,
              cache_win2_kv, cache_win3_kv, cache_mem_kv, g_norm, w_in, g_mem, w_mem_kv,
              lambda_q1, lambda_k1, lambda_q2, lambda_k2, g_subln, w_proj_a, w_proj_b,
              w_proj_m, w_out, g_final):
    h_p, h_s = x_prompt, x_sample
    dkv_p, w1_p, w2_p, w3_p, mkv_p = [], [], [], [], []
    dkv_s, w1_s, w2_s, w3_s = [], [], [], []
    for l in range(DEPTH):
        w = (g_norm[l], w_in[l], g_mem[l], w_mem_kv[l], lambda_q1[l], lambda_k1[l],
             lambda_q2[l], lambda_k2[l], g_subln[l], w_proj_a[l], w_proj_b[l],
             w_proj_m[l], w_out[l])
        h_p, d_p, wins_p, m_p = prompt_layer(h_p, mem_prompt, w, l)
        h_s, d_s, wins_s = sample_layer(h_s, cache_diff_kv[l], page_table,
                                        (cache_win1_kv[l], cache_win2_kv[l], cache_win3_kv[l]),
                                        cache_mem_kv[l], w, l)
        dkv_p.append(d_p); w1_p.append(wins_p[0]); w2_p.append(wins_p[1]); w3_p.append(wins_p[2])
        mkv_p.append(m_p)
        dkv_s.append(d_s); w1_s.append(wins_s[0]); w2_s.append(wins_s[1]); w3_s.append(wins_s[2])
    y_prompt = rms_norm(h_p, g_final)
    y_sample = rms_norm(h_s, g_final)
    return (y_prompt, y_sample,
            jnp.stack(dkv_p), jnp.stack(w1_p), jnp.stack(w2_p), jnp.stack(w3_p), jnp.stack(mkv_p),
            jnp.stack(dkv_s), jnp.stack(w1_s), jnp.stack(w2_s), jnp.stack(w3_s))


_drawn_inputs = setup_inputs


def setup_inputs(seed=0):
    import zlib

    import numpy as np

    out = dict(_drawn_inputs(seed))
    spreads = {}
    factors = {'cache_win2_kv': 3.107,
     'cache_win3_kv': 8.0,
     'g_norm': 2.808,
     'g_mem': 8.004,
     'lambda_q1': 3.986,
     'lambda_k1': 6.044,
     'lambda_q2': 3.927,
     'lambda_k2': 5.44,
     'g_subln': 26.549,
     'g_final': 7.945,
     'cache_win1_kv': 8.0}
    for name, (base, spread) in spreads.items():
        noise = np.random.default_rng([zlib.crc32(name.encode()), seed]).standard_normal(out[name].shape)
        drawn = base * np.exp(spread * noise) if base else spread * noise
        out[name] = __import__('jax').numpy.asarray(drawn.astype(out[name].dtype))
    for name, factor in factors.items():
        out[name] = (out[name] * factor).astype(out[name].dtype)
    return out
```

```python
from contextlib import ExitStack

import numpy as np
import concourse.bass as bass
from concourse import mybir

D = 1024
T = 512
NS = 8
TT = T + NS
HALF = TT // 2
KT = D // 128
NMEM = 256
CW = 256
EPS = 1e-6
LAM_INIT = 0.2
SCALE = 0.125
QT = T // 128
W_A = 2 * 128 + 1
G_ROWS = (128, 64, 16)
DIL = (1, 4, 16)
W_B = sum(G_ROWS) + 3


def chunk_sequence():
    first = [("mem", 0), ("mem", 1)] + [("in", j) for j in range(8)]
    second = [("in", 18)] + [("in", j) for j in range(8, 17)] + [("in", 17), ("in", 19)]
    third = []
    for m in range(4):
        third += [("in", 20 + m), ("in", 24 + m), ("in", 28 + m), ("proj", m)]
    return first, second, third, [("out", m) for m in range(4)]


def build_kernel(nc, ins, outs):
    f32, f32r, i32 = mybir.dt.float32, mybir.dt.float32r, mybir.dt.int32
    ACT = mybir.ActivationFunctionType
    ALU = mybir.AluOpType
    AXX = mybir.AxisListType.X

    FIRST, SECOND, THIRD, LAST = chunk_sequence()
    SEQ = FIRST + SECOND + THIRD + LAST
    N_FIRST, N_SECOND = len(FIRST), len(FIRST) + len(SECOND)
    N_THIRD = N_SECOND + len(THIRD)
    POS = {k: n for n, k in enumerate(SEQ)}

    x_p = ins["x_prompt"].rearrange("a t d -> (a t) d")
    x_s = ins["x_sample"].rearrange("b t d -> (b t) d")
    x_m = ins["mem_prompt"].rearrange("a t d -> (a t) d")
    w_in = ins["w_in"].rearrange("l (k p) n -> p (l k) n", p=128)
    w_mem = ins["w_mem_kv"].rearrange("l (k p) n -> p (l k) n", p=128)
    w_pa = ins["w_proj_a"].rearrange("l (k p) n -> p (l k) n", p=128)
    w_pb = ins["w_proj_b"].rearrange("l (k p) n -> p (l k) n", p=128)
    w_pm = ins["w_proj_m"].rearrange("l (k p) n -> p (l k) n", p=128)
    w_out = ins["w_out"].rearrange("l (k p) n -> p (l k) n", p=128)
    cache_a = ins["cache_diff_kv"].rearrange("l n p s h d -> (l n) p s (h d)")
    cache_1 = ins["cache_win1_kv"].rearrange("l b p s h d -> (l b) p s (h d)")
    cache_2 = ins["cache_win2_kv"].rearrange("l b (j r) s h d -> (l b) j r s (h d)", r=DIL[1])
    cache_3 = ins["cache_win3_kv"].rearrange("l b (j r) s h d -> (l b) j r s (h d)", r=DIL[2])
    cache_m = ins["cache_mem_kv"].rearrange("l b (t p) s h d -> (l b) p t s (h d)", p=128)
    diff_p = outs[2].rearrange("l b t s h d -> (l b t) s (h d)")
    win1_p = outs[3].rearrange("l b t s h d -> (l b t) (s h d)")
    win2_p = outs[4].rearrange("l b (j r) s h d -> r (l b j) (s h d)", r=4)
    win3_p = outs[5].rearrange("l b (j r) s h d -> r (l b j) (s h d)", r=4)
    mem_p = outs[6].rearrange("l b t s h d -> (l b t) (s h d)")
    diff_s = outs[7].rearrange("l b t s h d -> (l b t) s (h d)")
    win_s = [o.rearrange("l b t s h d -> (l b t) (s h d)") for o in outs[8:11]]
    y_p = outs[0].rearrange("a t d -> (a t) d")
    y_s = outs[1].rearrange("b t d -> (b t) d")

    ctx = ExitStack()
    early = ExitStack()
    with ctx:
        def sb(name, shape, dt=f32, where=ctx):
            return where.enter_context(nc.sbuf_tensor(name, shape, dt))

        def sem(name):
            return ctx.enter_context(nc.semaphore(name))

        xh = sb("xh", [128, KT, TT], f32r)
        xl = sb("xl", [128, KT, TT], f32r)
        w_raw = sb("w_raw", [128, 3, 4, CW])
        w_hi = sb("w_hi", [128, 2, KT, CW], f32r)
        w_lo = sb("w_lo", [128, 2, KT, CW], f32r)
        oz = sb("oz", [128, KT, TT])
        ident = sb("ident_sb", [128, 128])
        ones = sb("ones", [128, 128])
        ssq = sb("ssq", [128, 16])
        rstd = sb("rstd", [128, 16])
        eps = sb("eps", [128, 1])
        lamv = sb("lamv", [128, 8])
        gs = sb("gs", [128, 2])

        memh = sb("memh", [128, KT, NMEM], f32r, early)
        meml = sb("meml", [128, KT, NMEM], f32r, early)
        early.close()
        work = sb("work", [128, 4 * KT * NMEM // 2], f32, early)
        region = sb("region", [128, 8320], f32, early)
        v_b = sb("v_b", [128, 3, QT, 256], f32, early)
        bias_b = sb("bias_b", [128, 4, 771], f32, early)
        vT = sb("vT", [128, 4, TT], f32, early)
        ring = sb("ring", [128, 2, 2, 512], f32, early)
        prod = sb("prod", [128, 1024], f32, early)
        stage = sb("stage", [128, 2, 512], f32, early)
        kmT = sb("kmT", [128, 2, NMEM], f32, early)
        vm = sb("vm", [128, 2, 256], f32, early)
        small = sb("small", [128, 1100], f32, early)
        pages = sb("pages", [1, 16], i32, early)
        qs_a = sb("qs_a", [8, 512], f32, early)
        qs_m = sb("qs_m", [8, 256], f32, early)
        qs_b = sb("qs_b", [8, 3, 256], f32, early)
        sel_h = sb("sel_h", [128, 4, 4], f32, early)
        row_h = sb("row_h", [4, 4, 128], f32, early)
        early.close()

        mixh = sb("mixh", [128, KT, TT], f32r, early)
        mixl = sb("mixl", [128, KT, TT], f32r, early)
        oh = sb("oh", [128, KT, TT], f32r, early)
        ol = sb("ol", [128, KT, TT], f32r, early)
        gate = sb("gate", [128, 3, 2, TT], f32, early)
        mix_t = sb("mix_t", [128, 2, 3, HALF], f32, early)
        y_nat = sb("y_nat", [128, 5, D], f32, early)
        g_fin = sb("g_fin", [128, D], f32, early)
        early.close()

        xin = [region[:, 1024 * t:1024 * t + 1024] for t in range(7)]
        qaT = region[:, 0:4 * TT].rearrange("p (h t) -> p h t", h=4)
        kaT = region[:, 4 * TT:8 * TT].rearrange("p (h t) -> p h t", h=4)
        v_a = region[:, 8 * TT:8 * TT + 2048].rearrange("p (t c) -> p t c", t=4)
        bias_a = region[:, 8 * TT + 2048:8 * TT + 4096].rearrange("p (h c) -> p h c", h=4)
        qbT = region[:, 0:6 * TT].rearrange("p (g h t) -> p g h t", g=3, h=2)
        kbT = region[:, 6 * TT:12 * TT].rearrange("p (g h t) -> p g h t", g=3, h=2)
        qmT = region[:, 12 * TT:14 * TT].rearrange("p (h t) -> p h t", h=2)
        g_row = ring[:, 0, :, :].rearrange("p a b -> p (a b)")
        g_row_m = ring[:, 1, :, :].rearrange("p a b -> p (a b)")
        sc = {"A": [work[:, 1024 * i:1024 * i + 1024] for i in range(3)],
              "B": [work[:, 768 * i:768 * i + 768] for i in range(3)]}
        pt = {"A": [work[:, 3072 + 512 * i:3584 + 512 * i] for i in range(2)],
              "B": [work[:, 2304 + 768 * i:3072 + 768 * i] for i in range(2)]}
        sc["M"], pt["M"] = sc["B"], pt["B"]
        oraw = vT
        oraw_sq = [work[:, 512 * h:512 * h + 512] for h in range(4)]
        rsq = work[0:4, 2048:2560]

        o = 0

        def cut(n):
            nonlocal o
            o += n
            return small[:, o - n:o]
        mx = cut(8)
        nm = cut(8)
        sm = cut(8)
        rs = cut(8)
        lam_in = cut(256)
        s_a = cut(128)
        s_m = cut(64)
        s_1 = cut(32)
        s_23 = cut(32)
        vn_a = cut(32)
        vn_b = cut(48)
        pm_a = cut(64)
        pm_b = cut(96)
        bias_sa = work[0:64, 0:W_A]
        bias_sb = work[0:32, 272:272 + W_B]
        e_a = work[0:64, 512:512 + W_A]
        e_b = work[0:32, 784:784 + W_B]
        e_m = work[0:32, 1024:1280]
        g_a = work[0:64, 1280:1312]
        g_b = work[0:32, 1312:1344]
        g_m = work[0:32, 1344:1376]
        aT = work[:, 1408:1728]
        t_a = work[:, 1728:1760]
        o_as = work[:, 1760:1792]
        sq_s = work[:, 1792:1824]
        r_s = work[:, 1824:1856]
        t_b = work[:, 1856:1904]
        t_b2 = work[:, 1904:1936]

        pj = [ctx.enter_context(nc.psum_tensor(f"pj{i}", [128, 512], f32)) for i in range(2)]
        ps = [ctx.enter_context(nc.psum_tensor(f"ps{i}", [128, 1024], f32)) for i in range(2)]
        pt_bank = ctx.enter_context(nc.psum_tensor("pt_bank", [128, 512], f32))
        po_bank = ctx.enter_context(nc.psum_tensor("po_bank", [128, 512], f32))
        bank = [ps[0][:, 0:512], ps[0][:, 512:1024], ps[1][:, 0:512], ps[1][:, 512:1024],
                pt_bank[:, :], po_bank[:, :]]

        s_raw = [sem(f"raw_loaded{i}") for i in range(3)]
        s_hi = sem("half_hi")
        s_lo = sem("half_lo")
        s_wfree = sem("chunk_used")
        s_const = sem("const_loaded")
        s_ident = sem("ident_loaded")
        s_gain = sem("gains_loaded")
        s_vn = sem("new_values_kept")
        s_ob = sem("o_bm_gated")
        s_biasa = sem("bias_a_loaded")
        s_biasb = sem("bias_b_loaded")
        s_xin = [sem(f"x_loaded{i}") for i in range(7)]
        s_init = sem("init_done")
        s_dv = sem("dve_step")
        s_ac = sem("act_step")
        s_sq = sem("x_squared")
        s_std = sem("x_std")
        s_xn = sem("x_normed")
        s_xt = sem("x_transposed")
        s_xh = sem("x_hi")
        s_xl = sem("x_lo")
        s_pj = sem("proj_done")
        s_ev = sem("proj_evacuated")
        s_nat = sem("nat_done")
        s_stage = sem("nat_staged")
        s_pc = sem("nat_copied")
        s_out = [sem(f"stage_stored{i}") for i in range(2)]
        s_S = sem("scores")
        s_bm = sem("biased_max")
        s_nm = sem("neg_max")
        s_ex = sem("exps")
        s_cb = sem("probs")
        s_T = sem("probs_transposed")
        s_te = sem("probsT_copied")
        s_pv = sem("pv_done")
        s_oe = sem("o_evacuated")
        s_lexp = sem("lambda_exp")
        s_lsum = sem("lambda_sum")
        s_osq = sem("o_squared")
        s_ov = sem("o_var")
        s_ostd = sem("o_std")
        s_orc = sem("o_rstd")
        s_obc = sem("o_rstd_bc")
        s_oa = sem("o_a_done")
        s_kr = [sem(f"ring_loaded{i}") for i in range(2)]
        s_qb = sem("q_broadcast")
        s_km = sem("k_multiplied")
        s_kd = sem("sample_scores")
        s_new = sem("new_products")
        s_sT = sem("samples_transposed")
        s_snm = sem("samples_neg_max")
        s_sex = sem("samples_exp")
        s_sG = sem("samples_norm")
        s_saT = sem("samples_probsT")
        s_sev = sem("samples_probsT_copied")
        s_spv = sem("samples_pv")
        s_so = sem("samples_o")
        s_sbl = sem("sample_bias_loaded")
        s_oh = sem("o_hi")
        s_ol = sem("o_lo")
        s_pp = sem("branch_projected")
        s_mx = sem("mix_read")
        s_mix = sem("mixed")
        s_mh = sem("mixed_hi")
        s_ml = sem("mixed_lo")
        s_po = sem("out_projected")
        s_y = sem("y_added")
        s_ysq = sem("y_squared")
        s_ystd = sem("y_std")
        s_yo = sem("y_normed")
        s_yl = sem("residual_loaded")
        s_gf = sem("g_final_loaded")
        s_ys = sem("y_stored")
        s_pg = sem("pages_loaded")

        def units_of(kind):
            return {"mem": 2, "in": 4}.get(kind, 0)
        U0 = [0]
        for kind, _ in SEQ:
            U0.append(U0[-1] + units_of(kind))

        def ev_of(key):
            return U0[POS[key] + 1]

        JOBS = []

        def job(after, rows, srcs, need, stores, copies):
            JOBS.append((after, rows, srcs, need, stores, copies))

        def tok(ap, t):
            return ap[:, 128 * t:128 * t + (128 if t < 4 else NS)]

        for t in range(2):
            job(2, 128, [kmT[:, 0, 128 * t:128 * t + 128], kmT[:, 1, 128 * t:128 * t + 128],
                         vT[:, 0, 128 * t:128 * t + 128], vT[:, 1, 128 * t:128 * t + 128]],
                ("mem", 1), [(mem_p[128 * t:128 * t + 128, :], 0, 512)], [(vm[:, t, :], 256, 512)])
        for t in range(5):
            dst = diff_p[128 * t:128 * t + 128, 0, :] if t < 4 else diff_s[:, 0, :]
            job(POS["in", 4], 128 if t < 4 else NS, [tok(kaT[:, h, :], t) for h in range(4)],
                ("in", 3), [(dst, 0, 512)], [])
        job(POS["in", 4], NS, [tok(qaT[:, h, :], 4) for h in range(4)], ("in", 1), [], [(qs_a[:, :], 0, 512)])
        for t in range(5):
            dst = diff_p[128 * t:128 * t + 128, 1, :] if t < 4 else diff_s[:, 1, :]
            job(POS["in", 6], 128 if t < 4 else NS, [tok(vT[:, h, :], t) for h in range(4)],
                ("in", 5), [(dst, 0, 512)], [(v_a[:, t, :], 0, 512)] if t < 4 else [])
        J_FIRST = len(JOBS)
        job(POS["in", 8], NS, [tok(qmT[:, h, :], 4) for h in range(2)], ("in", 18), [], [(qs_m[:, :], 0, 256)])
        J_QM = len(JOBS)
        for g in range(3):
            vt = [vT[:, (2 * g) % 4 + h, :] for h in range(2)]
            after = POS["in", 11 + 3 * g] if g < 2 else POS["in", 17]
            job(after, NS, [tok(qbT[:, g, h, :], 4) for h in range(2)], ("in", 8 + 3 * g), [],
                [(qs_b[:, g, :], 0, 256)])
            for t in range(4):
                if g == 0:
                    if t < 3:
                        job(after, 128, [tok(v, t) for v in vt], ("in", 10), [], [(v_b[:, 0, t, :], 0, 256)])
                        continue
                    srcs = [tok(kbT[:, 0, h, :], t) for h in range(2)] + [tok(v, t) for v in vt]
                    dst = win1_p
                else:
                    srcs = [kbT[:, g, h, t:T:4] for h in range(2)] + [v[:, t:T:4] for v in vt]
                    dst = (win2_p, win3_p)[g - 1][t]
                job(after, 128, srcs, ("in", 10 + 3 * g), [(dst, 0, 512)], [(v_b[:, g, t, :], 256, 512)])
            job(after, NS, [tok(kbT[:, g, h, :], 4) for h in range(2)] + [tok(v, 4) for v in vt],
                ("in", 10 + 3 * g), [(win_s[g], 0, 512)], [])
        NJ = len(JOBS)
        PC = [0]
        OUTC = [0, 0]
        OUT_AT = []
        for J, (_, _, _, _, stores, copies) in enumerate(JOBS):
            PC.append(PC[-1] + len(copies))
            OUTC[J % 2] += 16 * len(stores)
            OUT_AT.append(OUTC[J % 2])

        def jobs_after(n):
            return [J for J in range(NJ) if JOBS[J][0] == n]

        V_GUARD = {("in", 4): 2, ("in", 5): 2, ("in", 10): J_FIRST, ("in", 13): J_FIRST,
                   ("in", 16): [J for J in range(NJ) if JOBS[J][3] == ("in", 10)][-1] + 1}

        RINGS = []
        RING_AT = {}
        for b in range(NS):
            step = POS["in", 9 + b] if b < 8 else None
            RINGS += [("A", b), ("M", b)]
            RING_AT.setdefault(step, []).extend([2 * b, 2 * b + 1])
        for b in range(NS):
            RING_AT.setdefault(POS["in", 19], []).append(len(RINGS))
            RINGS.append(("B", b))
        NK = len(RINGS)
        RINGS += [(k, b) for k in "AMB" for b in range(NS)]
        LOADS = {"A": 2, "M": 1, "B": 3}
        KR = []
        cum = [0, 0]
        for k, (kind, _) in enumerate(RINGS):
            cum[k % 2] += 16 * LOADS[kind]
            KR.append(cum[k % 2])
        OA_UNITS = 4 * QT
        OB_UNITS = 4 * 4
        OM_UNITS = QT * 2
        NU = OA_UNITS + OB_UNITS + OM_UNITS

        block = ctx.enter_context(nc.Block())

        @block.sync
        def _(sp):
            sp.dma_start(xin[5], x_m[0:128, :]).then_inc(s_xin[5], 16)
            sp.dma_start(xin[6], x_m[128:256, :]).then_inc(s_xin[6], 16)
            sp.dma_start(g_row_m, ins["g_mem"].partition_broadcast(128).rearrange("p a d -> p (a d)")).then_inc(s_gain, 16)
            sp.dma_start(ident[:, :], ins["c_ident"]).then_inc(s_ident, 16)
            sp.dma_start(g_row, ins["g_norm"].partition_broadcast(128).rearrange("p a d -> p (a d)")).then_inc(s_gain, 16)
            for t in range(4):
                sp.dma_start(xin[t], x_p[128 * t:128 * t + 128, :]).then_inc(s_xin[t], 16)
            sp.dma_start(xin[4][0:NS, :], x_s).then_inc(s_xin[4], 16)
            for i, n in enumerate(("lambda_q1", "lambda_k1", "lambda_q2", "lambda_k2")):
                sp.dma_start(lam_in[:, 64 * i:64 * i + 64],
                             ins[n].partition_broadcast(128).rearrange("p a d -> p (a d)")).then_inc(s_const, 16)
            sp.dma_start(gs[:, 0:1], ins["g_subln"].rearrange("l d -> d l")).then_inc(s_const, 16)
            sp.dma_start(sel_h[:, :, :], ins["c_selh"]).then_inc(s_const, 16)
            sp.dma_start(row_h[:, :, :], ins["c_rowh"]).then_inc(s_const, 16)
            sp.dma_start(bias_b[:, :, :], ins["c_bias_b"]).then_inc(s_biasb, 16)
            for m in range(2 * len(SEQ)):
                n, s = divmod(m, 2)
                kind, j = SEQ[n]
                if m >= 3:
                    sp.wait_ge(s_lo, m - 2)
                if kind == "proj" and s == 1:
                    sp.dma_start(w_raw[:, m % 3, 0:2, :], w_pb[:, :, CW * j:CW * j + CW]).then_inc(s_raw[m % 3], 16)
                    sp.dma_start(w_raw[:, m % 3, 2:4, :], w_pm[:, :, CW * j:CW * j + CW]).then_inc(s_raw[m % 3], 16)
                    continue
                src = {"mem": w_mem, "in": w_in, "proj": w_pa, "out": w_out}[kind]
                sp.dma_start(w_raw[:, m % 3, :, :],
                             src[:, 4 * s:4 * s + 4, CW * j:CW * j + CW]).then_inc(s_raw[m % 3], 16)

        RAWC = [0, 0, 0]
        RAW_AT = []
        for m in range(2 * len(SEQ)):
            RAWC[m % 3] += 32 if (SEQ[m // 2][0] == "proj" and m % 2) else 16
            RAW_AT.append(RAWC[m % 3])

        @block.gpsimd
        def _(pool):
            pool.memset(ones[:, :], 1.0).then_inc(s_init, 1)
            pool.memset(eps[:, :], EPS).then_inc(s_init, 1)
            pool.memset(ssq[:, :], 1.0).then_inc(s_init, 1)
            pool.memset(pm_a, 0.0).then_inc(s_init, 1)
            pool.memset(pm_b, 0.0).then_inc(s_init, 1)
            pool.dma_start(pages[:, :], ins["page_table"].rearrange("b n -> (b n)").unsqueeze(0)).then_inc(s_pg, 16)

            def store_job(J):
                _, rows, _, _, stores, copies = JOBS[J]
                pool.wait_ge(s_stage, J + 1)
                for dst, a, b in copies:
                    pool.tensor_copy(dst, stage[0:rows, J % 2, a:b]).then_inc(s_pc, 1)
                for dst, a, b in stores:
                    pool.dma_start(dst, stage[0:rows, J % 2, a:b]).then_inc(s_out[J % 2], 16)

            def load_ring(k):
                kind, b = RINGS[k]
                s = 0 if k < NK else 1
                if k >= 2 and k - 2 < NK:
                    pool.wait_ge(s_km, k - 1)
                elif k >= 2:
                    pool.wait_ge(s_spv, k - 2 - NK + 1)
                slot = ring[:, k % 2, :, :]
                if kind == "A":
                    for t in range(2):
                        page = pool.value_load(pages[0:1, 2 * b + t:2 * b + t + 1], min_val=0,
                                               max_val=cache_a.shape[0] - 1)
                        pool.dma_start(slot[:, t, :], cache_a[bass.ds(page, 1), :, s, :].rearrange("a p c -> (a p) c")).then_inc(s_kr[k % 2], 16)
                elif kind == "M":
                    pool.dma_start(slot[:, :, 0:256], cache_m[b, :, :, s, :]).then_inc(s_kr[k % 2], 16)
                else:
                    pool.dma_start(slot[:, 0, 0:256], cache_1[b, :, s, :]).then_inc(s_kr[k % 2], 16)
                    pool.dma_start(slot[0:64, 1, 0:256], cache_2[b, :, 0, s, :]).then_inc(s_kr[k % 2], 16)
                    pool.dma_start(slot[64:80, 1, 0:256], cache_3[b, :, 0, s, :]).then_inc(s_kr[k % 2], 16)

            for n in range(N_FIRST):
                for J in jobs_after(n):
                    store_job(J)
                if n == 3:
                    pool.wait_ge(s_xt, 14)
                    pool.wait_ge(s_xn, 7)
                    pool.dma_start(bias_a, ins["c_bias_a"]).then_inc(s_biasa, 16)
            pool.wait_ge(s_pg, 16)
            pool.wait_ge(s_xn, 7)
            load_ring(0)
            load_ring(1)
            for n in range(N_FIRST, N_SECOND):
                for k in RING_AT.get(n, []):
                    if k + 2 < NK:
                        load_ring(k + 2)
                for J in jobs_after(n):
                    store_job(J)
            pool.wait_ge(s_cb, NU)
            pool.wait_ge(s_te, NU)
            pool.wait_ge(s_pv, NU)
            pool.dma_start(bias_sa, ins["c_bias_sa"]).then_inc(s_sbl, 16)
            pool.dma_start(bias_sb, ins["c_bias_sb"]).then_inc(s_sbl, 16)
            for k in range(NK, 2 * NK):
                load_ring(k)
            pool.wait_ge(s_so, 2)
            for i in range(2):
                pool.wait_ge(s_out[i], OUTC[i])
            for t in range(4):
                pool.dma_start(y_nat[:, t, :], x_p[128 * t:128 * t + 128, :]).then_inc(s_yl, 16)
            pool.dma_start(y_nat[0:NS, 4, :], x_s).then_inc(s_yl, 16)
            pool.dma_start(g_fin[:, :], ins["g_final"].unsqueeze(0).partition_broadcast(128).rearrange("p a d -> p (a d)")).then_inc(s_gf, 16)
            for t in range(5):
                pool.wait_ge(s_yo, t + 1)
                rows = 128 if t < 4 else NS
                dst = y_p[128 * t:128 * t + 128, :] if t < 4 else y_s
                pool.dma_start(dst, y_nat[0:rows, t, :]).then_inc(s_ys, 16)
            pool.wait_ge(s_ys, 80)

        XORDER = [5, 6, 0, 1, 2, 3, 4]

        def rows_of(t):
            return NS if t == 4 else 128

        def x_dst(buf_x, buf_m, t, kg):
            if t < 5:
                return buf_x[:, 4 * kg:4 * kg + 4, 128 * t:128 * t + rows_of(t)]
            return buf_m[:, 4 * kg:4 * kg + 4, 128 * (t - 5):128 * (t - 5) + 128]

        def attn_slot(u):
            if u < OA_UNITS:
                return "A", u // QT, u % QT
            u -= OA_UNITS
            if u < OB_UNITS:
                return "B", u // 4, u % 4
            u -= OB_UNITS
            return "M", u // 2, u % 2

        RANGES = {"A": (0, OA_UNITS), "BM": (OA_UNITS, NU)}

        @block.tensor
        def _(pe):
            pe.wait_ge(s_ident, 16)
            pe.wait_ge(s_init, 5)
            for i, t in enumerate(XORDER):
                pe.wait_ge(s_xn, i + 1)
                for kg in range(2):
                    g = 2 * i + kg
                    if g >= 4:
                        pe.wait_ge(s_xl, g - 3)
                    for c in range(4):
                        last = pe.transpose(bank[g % 4][:, 128 * c:128 * c + rows_of(t)],
                                            xin[t][0:rows_of(t), 512 * kg + 128 * c:512 * kg + 128 * c + 128],
                                            ident[0:rows_of(t), 0:rows_of(t)])
                    last.then_inc(s_xt, 1)

            def product(out, parts, hi_m, lo_m):
                n = len(parts)
                for i, (slot, kt, c0, cn, kx, a, b) in enumerate(parts):
                    wh = w_hi[:, slot, kt, c0:c0 + cn]
                    wl = w_lo[:, slot, kt, c0:c0 + cn]
                    mh, ml = hi_m[:, kx, a:b], lo_m[:, kx, a:b]
                    pe.matmul(out, wh, mh, start=(i == 0), stop=False)
                    pe.matmul(out, wl, mh, start=False, stop=False)
                    last = pe.matmul(out, wh, ml, start=False, stop=(i == n - 1))
                return last

            def nat_job(J):
                _, rows, srcs, need, _, _ = JOBS[J]
                pe.wait_ge(s_ev, ev_of(need))
                if J >= 2:
                    pe.wait_ge(s_stage, J - 1)
                for c, src in enumerate(srcs):
                    last = pe.transpose(bank[J % 2][0:rows, 128 * c:128 * c + 128], src, ident[:, :])
                last.then_inc(s_nat, 1)

            def project_chunk(n):
                kind, j = SEQ[n]
                pe.wait_ge(s_lo, 2 * n + 2)
                hi_m, lo_m = (memh, meml) if kind == "mem" else (xh, xl)
                spans = [(0, NMEM)] if kind == "mem" else [(0, HALF), (HALF, TT)]
                u = U0[n]
                for tile in range(2):
                    for a, b in spans:
                        if n == N_SECOND - 1:
                            k = 16 + 2 * (u - U0[n])
                            broadcast_q(k)
                            broadcast_q(k + 1)
                        if u >= 2:
                            pe.wait_ge(s_ev, u - 1)
                        last = product(pj[u % 2][:, 0:b - a],
                                       [(n % 2, kt, 128 * tile, 128, kt, a, b) for kt in range(KT)], hi_m, lo_m)
                        last.then_inc(s_pj, 1)
                        u += 1
                for J in jobs_after(n):
                    nat_job(J)

            def broadcast_q(k):
                kind, b = RINGS[k]
                if k >= 2:
                    pe.wait_ge(s_km, k - 1)
                out = bank[2 + k % 2]
                pick = ident[0:NS, b:b + 1]
                if kind == "A":
                    last = pe.matmul(out, pick.to_broadcast([NS, 128]), qs_a[:, :], start=True, stop=True)
                elif kind == "M":
                    last = pe.matmul(out[:, 0:256], pick.to_broadcast([NS, 128]), qs_m[:, :], start=True, stop=True)
                else:
                    pe.matmul(out[:, 0:256], pick.to_broadcast([NS, 128]), qs_b[:, 0, :], start=True, stop=True)
                    pe.matmul(out[0:64, 256:512], pick.to_broadcast([NS, 64]), qs_b[:, 1, :], start=True, stop=True)
                    last = pe.matmul(out[64:80, 256:512], pick.to_broadcast([NS, 16]), qs_b[:, 2, :], start=True, stop=True)
                last.then_inc(s_qb, 1)

            def scores(u):
                br, p, q = attn_slot(u)
                S = ps[u % 2]
                if u >= 2:
                    pe.wait_ge(s_bm, u - 1)
                    if attn_slot(u - 2)[0] == "M":
                        pe.wait_ge(s_ex, u - 1)
                if br == "A":
                    for c in range(2):
                        rows = slice(64 * c, 64 * c + 64)
                        last = pe.matmul(S[:, 512 * c:512 * c + 128 * (q + 1)],
                                         qaT[rows, p, 128 * q:128 * q + 128],
                                         kaT[rows, p, 0:128 * (q + 1)], start=True, stop=True)
                elif br == "B":
                    hp, hh = divmod(q, 2)
                    rows = slice(64 * hh, 64 * hh + 64)
                    pe.matmul(S[:, 0:512], qbT[rows, 0, hp, p:T:4], kbT[rows, 0, hp, 0:T], start=True, stop=True)
                    pe.matmul(S[:, 512:640], qbT[rows, 1, hp, p:T:4], kbT[rows, 1, hp, p:T:4], start=True, stop=True)
                    last = pe.matmul(S[:, 640:768], qbT[rows, 2, hp, p:T:4], kbT[rows, 2, hp, p:T:4],
                                     start=True, stop=True)
                else:
                    for hh in range(2):
                        rows = slice(64 * hh, 64 * hh + 64)
                        last = pe.matmul(S[:, 512 * hh:512 * hh + 256], qmT[rows, q, 128 * p:128 * p + 128],
                                         kmT[rows, q, :], start=True, stop=True)
                last.then_inc(s_S, 1)

            def transposes(u):
                br, p, q = attn_slot(u)
                pe.wait_ge(s_cb, u + 1)
                pe.wait_ge(s_te, u)
                blocks = {"A": q + 1, "B": 6, "M": 4}[br]
                for k in range(blocks):
                    dst = pt_bank[:, 128 * k:128 * k + 128] if k < 4 else po_bank[:, 128 * k - 512:128 * k - 384]
                    last = pe.transpose(dst, sc[br][u % 3][:, 128 * k:128 * k + 128], ident[:, :])
                last.then_inc(s_T, 1)

            def values(u):
                br, p, q = attn_slot(u)
                pe.wait_ge(s_te, u + 1)
                P = pt[br][u % 2]
                if br == "A":
                    out = po_bank[:, 128 * q:128 * q + 128]
                    if q == 0 and p > 0:
                        pe.wait_ge(s_oe, p)
                    for k in range(q + 1):
                        last = pe.matmul(out, v_a[:, k, 128 * p:128 * p + 128], P[:, 128 * k:128 * k + 128],
                                         start=(k == 0), stop=(k == q))
                else:
                    v = u - OA_UNITS
                    pair = v // 2 if br == "B" else OB_UNITS // 2 + (v - OB_UNITS)
                    heads = [(q // 2, q % 2)] if br == "B" else [(q, 0), (q, 1)]
                    if pair >= 2 and (br == "M" or q % 2 == 0):
                        pe.wait_ge(s_ob, pair - 1)
                    for hp, hh in heads:
                        out = pj[pair % 2][64 * hh:64 * hh + 64, 0:128]
                        cols = slice(128 * hp + 64 * hh, 128 * hp + 64 * hh + 64)
                        if br == "B":
                            vs = [v_b[:, 0, k, cols] for k in range(4)] + [v_b[:, 1, p, cols], v_b[:, 2, p, cols]]
                            ks = range(6)
                        else:
                            vs = [vm[:, k, cols] for k in range(2)]
                            ks = [2 * hh, 2 * hh + 1]
                        for i, k in enumerate(ks):
                            last = pe.matmul(out, vs[i], P[:, 128 * k:128 * k + 128],
                                             start=(i == 0), stop=(i == len(vs) - 1))
                last.then_inc(s_pv, 1)

            def attention(which):
                a, b = RANGES[which]
                for s in range(a, b + 3):
                    if s < b:
                        scores(s)
                    if a <= s - 2 < b:
                        transposes(s - 2)
                    if a <= s - 3:
                        values(s - 3)

            for n in range(N_FIRST):
                if n == 0:
                    pe.wait_ge(s_xl, 4)
                if n == 2:
                    pe.wait_ge(s_xl, 14)
                project_chunk(n)
            pe.wait_ge(s_stage, J_FIRST)
            pe.wait_ge(s_pc, PC[J_FIRST])
            pe.wait_ge(s_ev, U0[N_FIRST])
            attention("A")
            pe.wait_ge(s_bm, OA_UNITS)
            pe.wait_ge(s_te, OA_UNITS)
            for n in range(N_FIRST, N_SECOND):
                if n == N_FIRST + 1:
                    pe.wait_ge(s_const, 16 * 7)
                    for h in range(4):
                        pe.wait_ge(s_osq, h + 1)
                        last = pe.matmul(pt_bank[0:4, 0:512], sel_h[:, h, :], oraw_sq[h], start=(h == 0), stop=(h == 3))
                    last.then_inc(s_ov, 1)
                if n == POS["in", 10]:
                    pe.wait_ge(s_orc, 1)
                    for h in range(4):
                        if h >= 2:
                            pe.wait_ge(s_oa, h - 1)
                        dst = (pt_bank, po_bank)[h % 2][:, 0:512]
                        pe.matmul(dst, row_h[:, h, :], rsq, start=True, stop=True).then_inc(s_obc, 1)
                if n == POS["in", 9]:
                    pe.wait_ge(s_pc, PC[J_QM])
                if n == POS["in", 19]:
                    pe.wait_ge(s_pc, PC[NJ])
                elif n in RING_AT:
                    for k in RING_AT[n]:
                        broadcast_q(k)
                project_chunk(n)
            pe.wait_ge(s_stage, NJ)
            pe.wait_ge(s_pc, PC[NJ])
            pe.wait_ge(s_km, NK)
            pe.wait_ge(s_ev, U0[N_SECOND])
            pe.wait_ge(s_oa, 4)
            attention("BM")

            pe.wait_ge(s_bm, NU)
            pe.wait_ge(s_te, NU)
            pe.wait_ge(s_ex, NU)
            pe.wait_ge(s_kd, NK)
            pe.wait_ge(s_new, 4)
            sa = s_a.rearrange("p (t r) -> p t r", t=2)
            smt = s_m.rearrange("p (t r) -> p t r", t=2)
            for t in range(2):
                pe.transpose(bank[0][0:64, 128 * t:128 * t + 128], sa[:, t, :], ident[:, :])
            pe.matmul(bank[0][0:64, 256:257], pm_a, ones[:, 0:1], start=True, stop=True).then_inc(s_sT, 1)
            pe.transpose(bank[1][0:32, 0:128], s_1, ident[:, :])
            pe.transpose(bank[1][0:32, 128:208], s_23[0:80, :], ident[0:80, 0:80])
            for g in range(3):
                last = pe.matmul(bank[1][0:32, 208 + g:209 + g], pm_b[:, 32 * g:32 * g + 32], ones[:, 0:1],
                                 start=True, stop=True)
            last.then_inc(s_sT, 1)
            for t in range(2):
                last = pe.transpose(bank[2][0:32, 128 * t:128 * t + 128], smt[:, t, :], ident[:, :])
            last.then_inc(s_sT, 1)
            pe.wait_ge(s_sG, 3)
            out = bank[3]
            for t in range(2):
                pe.matmul(out[:, 32 * t:32 * t + 32], e_a[:, 128 * t:128 * t + 128], g_a, start=True, stop=True)
            pe.matmul(out[:, 64:96], e_a[:, 256:257].to_broadcast([64, 128]), g_a, start=True, stop=True)
            pe.matmul(out[:, 96:128], e_b[:, 0:128], g_b, start=True, stop=True)
            for g in range(3):
                pe.matmul(out[:, 128 + 32 * g:160 + 32 * g], e_b[:, 208 + g:209 + g].to_broadcast([32, 128]), g_b,
                          start=True, stop=True)
            for t in range(2):
                pe.matmul(out[:, 224 + 32 * t:256 + 32 * t], e_m[:, 128 * t:128 * t + 128], g_m, start=True, stop=True)
            pe.matmul(out[0:80, 288:320], e_b[:, 128:208], g_b, start=True, stop=True).then_inc(s_saT, 1)
            pe.wait_ge(s_sev, 1)
            for k in range(NK, 2 * NK):
                kind, b = RINGS[k]
                pe.wait_ge(s_kr[k % 2], KR[k])
                slot = ring[:, k % 2, :, :]
                if kind == "A":
                    for h in range(4):
                        for t in range(2):
                            last = pe.matmul(bank[4][:, 8 * h + b:8 * h + b + 1], slot[:, t, 128 * h:128 * h + 128],
                                             aT[:, 32 * t + 8 * h + b:32 * t + 8 * h + b + 1],
                                             start=(t == 0), stop=(t == 1))
                else:
                    dst = bank[4] if kind == "M" else bank[5]
                    for hp in range(2):
                        o2 = dst[:, 64 + 16 * hp + 2 * b:64 + 16 * hp + 2 * b + 2]
                        tiles = ([(slot[:, 0, 0:256], aT[:, 96:128], 128), (slot[0:80, 1, 0:256], aT[0:80, 288:320], 80)]
                                 if kind == "B" else
                                 [(slot[:, t, 0:256], aT[:, 224 + 32 * t:256 + 32 * t], 128) for t in range(2)])
                        for i, (vv, pp, rows) in enumerate(tiles):
                            rhs = pp.rearrange("p (h b) -> p h b", h=4)[:, 2 * hp:2 * hp + 2, b]
                            last = pe.matmul(o2, vv[:, 128 * hp:128 * hp + 128], rhs, start=(i == 0), stop=(i == 1))
                last.then_inc(s_spv, 1)
            pe.wait_ge(s_so, 1)
            pe.matmul(bank[0][:, 0:32], ones[:, :], sq_s, start=True, stop=True).then_inc(s_saT, 1)

            pe.wait_ge(s_ob, OB_UNITS // 2 + OM_UNITS)
            for m in range(4):
                for g in range(3):
                    project_chunk(N_SECOND + 4 * m + g)
                n = N_SECOND + 4 * m + 3
                pe.wait_ge(s_lo, 2 * n + 2)
                if m == 0:
                    pe.wait_ge(s_ol, 2)
                    pe.wait_ge(s_so, 2)
                for tile in range(2):
                    for hf in range(2):
                        i = 4 * m + 2 * tile + hf
                        a, b = HALF * hf, HALF * hf + HALF
                        if i >= 2:
                            pe.wait_ge(s_mx, i - 1)
                        for br, kts in enumerate(((0, 1, 2, 3), (4, 5), (6, 7))):
                            last = product(bank[3 * (i % 2) + br][:, 0:HALF],
                                           [(n % 2, kt, 128 * tile, 128, kt, a, b) for kt in kts], oh, ol)
                        last.then_inc(s_pp, 1)
            pe.wait_ge(s_ml, 16)
            for m in range(4):
                n = N_THIRD + m
                pe.wait_ge(s_lo, 2 * n + 2)
                for t in range(5):
                    i = 5 * m + t
                    rows = rows_of(t)
                    if i >= 2:
                        pe.wait_ge(s_y, i - 1)
                    out = pj[i % 2][0:rows, 0:CW]
                    for kt in range(KT):
                        mh = mixh[:, kt, 128 * t:128 * t + rows]
                        ml = mixl[:, kt, 128 * t:128 * t + rows]
                        pe.matmul(out, mh, w_hi[:, n % 2, kt, :], start=(kt == 0), stop=False)
                        pe.matmul(out, ml, w_hi[:, n % 2, kt, :], start=False, stop=False)
                        last = pe.matmul(out, mh, w_lo[:, n % 2, kt, :], start=False, stop=(kt == KT - 1))
                    last.then_inc(s_po, 1)

        def wait_chunk_used(eng, n):
            kind, j = SEQ[n]
            if kind == "proj":
                eng.wait_ge(s_pp, 4 * (j + 1))
            elif kind == "out":
                eng.wait_ge(s_po, 5 * (j + 1))
            else:
                eng.wait_ge(s_pj, U0[n + 1])

        @block.scalar
        def _(act):
            def hi_split(n):
                if n >= len(SEQ):
                    return
                if n >= 2:
                    wait_chunk_used(act, n - 2)
                for s in range(2):
                    m = 2 * n + s
                    act.wait_ge(s_raw[m % 3], RAW_AT[m])
                    act.activation(w_hi[:, n % 2, 4 * s:4 * s + 4, :], w_raw[:, m % 3, :, :], ACT.Copy).then_inc(s_hi, 1)

            for i, t in enumerate(XORDER):
                act.wait_ge(s_xin[t], 16)
                if i == 0:
                    act.wait_ge(s_init, 5)
                else:
                    act.wait_ge(s_sq, i)
                r = rows_of(t)
                act.activation(prod[0:r, :], xin[t][0:r, :], ACT.Square, accum_out=ssq[0:r, t:t + 1]).then_inc(s_sq, 1)
            act.wait_ge(s_sq, 7)
            act.activation(rstd[:, 0:7], ssq[:, 0:7], ACT.Sqrt, scale=1.0 / D, bias=eps[:, :]).then_inc(s_std, 1)
            hi_split(0)
            for i, t in enumerate(XORDER):
                for kg in range(2):
                    g = 2 * i + kg
                    act.wait_ge(s_xt, g + 1)
                    src = bank[g % 4].rearrange("p (c t) -> p c t", c=4)[:, :, 0:rows_of(t)]
                    act.activation(x_dst(xh, memh, t, kg), src, ACT.Copy).then_inc(s_xh, 1)
                if i == 2:
                    hi_split(1)

            act.wait_ge(s_lsum, 1)
            act.activation(lamv[:, 2:4], lamv[:, 0:2], ACT.Exp).then_inc(s_lexp, 1)

            def evac_dest(key, tile, a, b):
                kind, j = key
                if kind == "mem":
                    return (kmT if j == 0 else vT)[:, tile, a:b]
                c = 2 * j + tile
                if j < 2:
                    return qaT[:, c, a:b]
                if j < 4:
                    return kaT[:, c - 4, a:b]
                if j < 6:
                    return vT[:, c - 8, a:b]
                if j < 8:
                    return oz[:, c - 12, a:b]
                if j < 17:
                    g, r = divmod(j - 8, 3)
                    if r == 2:
                        return vT[:, (2 * g) % 4 + tile, a:b]
                    return (qbT, kbT)[r][:, g, tile, a:b]
                if j == 17:
                    return oz[:, 4 + tile, a:b]
                if j == 18:
                    return qmT[:, tile, a:b]
                if j == 19:
                    return oz[:, 6 + tile, a:b]
                return gate[:, (j - 20) // 4, tile, a:b]

            def evacuate(n):
                key = SEQ[n]
                kind, j = key
                spans = [(0, NMEM)] if kind == "mem" else [(0, HALF), (HALF, TT)]
                if kind == "in" and j >= 20:
                    func = ACT.Sigmoid
                elif kind == "in" and j in (6, 7, 17, 19):
                    func = ACT.Silu
                else:
                    func = ACT.Copy
                if key in V_GUARD:
                    act.wait_ge(s_nat, V_GUARD[key])
                if key == ("in", 10):
                    act.wait_ge(s_oa, 4)
                if key == ("in", 8):
                    act.wait_ge(s_new, 2)
                if kind == "in" and j == 20:
                    act.wait_ge(s_so, 2)
                u = U0[n]
                for tile in range(2):
                    for a, b in spans:
                        act.wait_ge(s_pj, u + 1)
                        if kind == "in" and j >= 20 and (j - 20) % 4:
                            act.wait_ge(s_mx, 4 * ((j - 21) % 4) + 2 * tile + (1 if a else 0) + 1)
                        act.activation(evac_dest(key, tile, a, b), pj[u % 2][:, 0:b - a], func).then_inc(s_ev, 1)
                        if kind == "in" and a and (j in (4, 5) or j in (10, 13, 16)):
                            if j < 6:
                                dst = vn_a[:, 8 * (2 * j - 8 + tile):8 * (2 * j - 8 + tile) + 8]
                            else:
                                g = (j - 10) // 3
                                dst = vn_b[:, 16 * g + 8 * tile:16 * g + 8 * tile + 8]
                            act.wait_ge(s_ev, u + 1)
                            act.activation(dst, evac_dest(key, tile, 512, TT), ACT.Copy).then_inc(s_vn, 1)
                        u += 1

            def exps(u):
                br, p, q = attn_slot(u)
                act.wait_ge(s_nm, u + 1)
                k4 = 2 * (u % 4)
                buf = sc[br][u % 3]
                if br == "A":
                    kn = 128 * (q + 1)
                    act.activation(buf[:, 0:kn], buf[:, 0:kn], ACT.Exp, bias=nm[:, k4:k4 + 1],
                                   accum_out=sm[:, k4:k4 + 1])
                    act.activation(buf[:, 512:512 + kn], buf[:, 512:512 + kn], ACT.Exp, bias=nm[:, k4 + 1:k4 + 2],
                                   accum_out=sm[:, k4 + 1:k4 + 2]).then_inc(s_ex, 1)
                elif br == "B":
                    act.activation(buf[:, 0:768], buf[:, 0:768], ACT.Exp, bias=nm[:, k4:k4 + 1],
                                   accum_out=sm[:, k4:k4 + 1]).then_inc(s_ex, 1)
                else:
                    for hh in range(2):
                        last = act.activation(buf[:, 256 * hh:256 * hh + 256], ps[u % 2][:, 512 * hh:512 * hh + 256],
                                              ACT.Exp, bias=nm[:, k4 + hh:k4 + hh + 1], scale=SCALE,
                                              accum_out=sm[:, k4 + hh:k4 + hh + 1])
                    last.then_inc(s_ex, 1)

            def copy_probs(u):
                br, p, q = attn_slot(u)
                act.wait_ge(s_T, u + 1)
                if u >= 2:
                    act.wait_ge(s_pv, u - 1)
                P = pt[br][u % 2]
                if br == "B":
                    act.activation(P[:, 0:512], pt_bank[:, :], ACT.Copy)
                    act.activation(P[:, 512:768], po_bank[:, 0:256], ACT.Copy).then_inc(s_te, 1)
                else:
                    w = 128 * (q + 1) if br == "A" else 512
                    act.activation(P[:, 0:w], pt_bank[:, 0:w], ACT.Copy).then_inc(s_te, 1)

            def attention(which):
                a, b = RANGES[which]
                for s in range(a, b + 4):
                    v = s - 4
                    if which == "A" and a <= v < b and attn_slot(v)[2] == QT - 1:
                        h = attn_slot(v)[1]
                        act.wait_ge(s_pv, v + 1)
                        act.activation(oraw[:, h, 0:T], po_bank[:, :], ACT.Copy).then_inc(s_oe, 1)
                    if s < b:
                        exps(s)
                    if a <= s - 2 < b:
                        copy_probs(s - 2)

            for n in range(N_FIRST):
                evacuate(n)
                hi_split(n + 2)
            act.wait_ge(s_nat, J_FIRST)
            act.wait_ge(s_xl, 14)
            attention("A")
            act.wait_ge(s_oe, 4)
            for h in range(4):
                act.activation(oraw_sq[h], oraw[:, h, 0:T], ACT.Square).then_inc(s_osq, 1)
            for n in range(N_FIRST, N_SECOND):
                evacuate(n)
                hi_split(n + 2)
                if n == N_FIRST + 1:
                    act.wait_ge(s_ov, 1)
                    act.activation(rsq, pt_bank[0:4, 0:512], ACT.Sqrt, bias=eps[0:4, :]).then_inc(s_ostd, 1)
            attention("BM")

            act.wait_ge(s_snm, 1)
            act.activation(e_a, e_a, ACT.Exp, bias=nm[0:64, 0:1], accum_out=sm[0:64, 0:1]).then_inc(s_sex, 1)
            act.wait_ge(s_snm, 2)
            act.activation(e_b, e_b, ACT.Exp, bias=nm[0:32, 1:2], accum_out=sm[0:32, 1:2]).then_inc(s_sex, 1)
            act.wait_ge(s_snm, 3)
            act.activation(e_m, bank[2][0:32, 0:256], ACT.Exp, bias=nm[0:32, 2:3], scale=SCALE,
                           accum_out=sm[0:32, 2:3]).then_inc(s_sex, 1)
            act.wait_ge(s_saT, 2)
            act.activation(r_s, bank[0][:, 0:32], ACT.Sqrt, scale=1.0 / 128, bias=eps[:, :]).then_inc(s_sex, 1)

            act.wait_ge(s_so, 2)
            for s in range(2):
                act.activation(oh[:, 4 * s:4 * s + 4, :], oz[:, 4 * s:4 * s + 4, :], ACT.Copy).then_inc(s_oh, 1)
            for m in range(4):
                for g in range(3):
                    n = N_SECOND + 4 * m + g
                    evacuate(n)
                    hi_split(n + 2)
                for i in range(4 * m, 4 * m + 4):
                    c, hf = divmod(i, 2)
                    act.wait_ge(s_mix, i + 1)
                    act.activation(mixh[:, c, HALF * hf:HALF * hf + HALF], mix_t[:, i % 2, 0, :], ACT.Copy).then_inc(s_mh, 1)
                hi_split(N_SECOND + 4 * m + 3 + 2)
            for m in range(4):
                hi_split(N_THIRD + m + 2)
            for t in range(5):
                r = rows_of(t)
                act.wait_ge(s_y, 15 + t + 1)
                if t:
                    act.wait_ge(s_ysq, t)
                act.activation(gate[0:r, 0:2, :, 0:256].rearrange("p a b c -> p (a b) c"),
                               y_nat[0:r, t, :].rearrange("p (a c) -> p a c", c=256), ACT.Square,
                               accum_out=ssq[0:r, 8 + t:9 + t]).then_inc(s_ysq, 1)
                act.wait_ge(s_ysq, t + 1)
                act.activation(rstd[0:r, 8 + t:9 + t], ssq[0:r, 8 + t:9 + t], ACT.Sqrt, scale=1.0 / D,
                               bias=eps[0:r, :]).then_inc(s_ystd, 1)

        @block.vector
        def _(dve):
            own = [0]

            def link(ins):
                own[0] += 1
                ins.then_inc(s_dv, 1)
                dve.wait_ge(s_dv, own[0])

            def lo_split(n):
                if n >= len(SEQ):
                    return
                for s in range(2):
                    m = 2 * n + s
                    dve.wait_ge(s_hi, m + 1)
                    dve.tensor_tensor(w_lo[:, n % 2, 4 * s:4 * s + 4, :], w_raw[:, m % 3, :, :],
                                      w_hi[:, n % 2, 4 * s:4 * s + 4, :].bitcast(f32), ALU.subtract).then_inc(s_lo, 1)

            def split_x(i):
                t = XORDER[i]
                for kg in range(2):
                    g = 2 * i + kg
                    dve.wait_ge(s_xh, g + 1)
                    src = bank[g % 4].rearrange("p (c t) -> p c t", c=4)[:, :, 0:rows_of(t)]
                    dve.tensor_tensor(x_dst(xl, meml, t, kg), src, x_dst(xh, memh, t, kg).bitcast(f32),
                                      ALU.subtract).then_inc(s_xl, 1)

            dve.wait_ge(s_std, 1)
            link(dve.reciprocal(ssq[:, 0:7], rstd[:, 0:7]))
            dve.wait_ge(s_gain, 32)
            for i, t in enumerate(XORDER):
                r = rows_of(t)
                dve.scalar_tensor_tensor(xin[t][0:r, :], xin[t][0:r, :], ssq[0:r, t:t + 1],
                                         (g_row if t < 5 else g_row_m)[0:r, :], ALU.mult, ALU.mult).then_inc(s_xn, 1)
                if i == 2:
                    lo_split(0)
                if i >= 1:
                    split_x(i - 1)
            split_x(6)
            dve.wait_ge(s_const, 16 * 7)
            for i in range(2):
                link(dve.tensor_tensor(s_a[:, 64 * i:64 * i + 64], lam_in[:, 128 * i:128 * i + 64],
                                       lam_in[:, 128 * i + 64:128 * i + 128], ALU.mult))
            dve.tensor_reduce(lamv[:, 0:2], s_a.rearrange("p (i d) -> p i d", i=2), AXX, ALU.add).then_inc(s_lsum, 1)
            dve.tensor_scalar(gs[:, 1:2], gs[:, 0:1], 1.0 - LAM_INIT, None, ALU.mult)
            lo_split(1)
            dve.wait_ge(s_lexp, 1)
            link(dve.tensor_tensor(lamv[:, 4:5], lamv[:, 3:4], lamv[:, 2:3], ALU.subtract))
            link(dve.tensor_scalar(lamv[:, 5:6], lamv[:, 4:5], -LAM_INIT, None, ALU.add))

            def stage_job(J):
                _, rows, srcs, _, _, _ = JOBS[J]
                dve.wait_ge(s_nat, J + 1)
                if J >= 2:
                    dve.wait_ge(s_out[J % 2], OUT_AT[J - 2])
                    dve.wait_ge(s_pc, PC[J - 1])
                w = 128 * len(srcs)
                dve.tensor_copy(stage[0:rows, J % 2, 0:w], bank[J % 2][0:rows, 0:w]).then_inc(s_stage, 1)

            def sample_scores(k):
                kind, b = RINGS[k]
                dve.wait_ge(s_kr[k % 2], KR[k])
                dve.wait_ge(s_qb, k + 1)
                if k:
                    dve.wait_ge(s_kd, k)
                slot = ring[:, k % 2, :, :]
                q = bank[2 + k % 2]
                if kind == "A":
                    dve.tensor_tensor(prod.rearrange("p (t c) -> p t c", t=2), slot,
                                      q.unsqueeze(1).to_broadcast([128, 2, 512]), ALU.mult).then_inc(s_km, 1)
                    dve.wait_ge(s_km, k + 1)
                    dve.tensor_reduce(s_a.rearrange("p (t c h b) -> p b t h c", t=2, c=2, h=4)[:, b],
                                      prod.rearrange("p (t h c d) -> p t h c d", t=2, h=4, c=2), AXX,
                                      ALU.add).then_inc(s_kd, 1)
                elif kind == "M":
                    dve.tensor_tensor(prod[:, 0:512].rearrange("p (t c) -> p t c", t=2), slot[:, :, 0:256],
                                      q[:, 0:256].unsqueeze(1).to_broadcast([128, 2, 256]), ALU.mult).then_inc(s_km, 1)
                    dve.wait_ge(s_km, k + 1)
                    dve.tensor_reduce(s_m.rearrange("p (t h b) -> p b t h", t=2, h=4)[:, b],
                                      prod[:, 0:512].rearrange("p (t h d) -> p t h d", t=2, h=4), AXX,
                                      ALU.add).then_inc(s_kd, 1)
                else:
                    dve.tensor_tensor(prod[:, 0:256], slot[:, 0, 0:256], q[:, 0:256], ALU.mult)
                    dve.tensor_tensor(prod[0:80, 256:512], slot[0:80, 1, 0:256], q[0:80, 256:512],
                                      ALU.mult).then_inc(s_km, 1)
                    dve.wait_ge(s_km, k + 1)
                    dve.tensor_reduce(s_1.rearrange("p (h b) -> p b h", h=4)[:, b],
                                      prod[:, 0:256].rearrange("p (h d) -> p h d", h=4), AXX, ALU.add)
                    dve.tensor_reduce(s_23[0:80, :].rearrange("p (h b) -> p b h", h=4)[:, b],
                                      prod[0:80, 256:512].rearrange("p (h d) -> p h d", h=4), AXX,
                                      ALU.add).then_inc(s_kd, 1)

            LOWEST = -3.0e38

            def biased_max(u):
                br, p, q = attn_slot(u)
                dve.wait_ge(s_S, u + 1)
                if u >= 3:
                    dve.wait_ge(s_T, u - 2)
                buf, S, k4 = sc[br][u % 3], ps[u % 2], 2 * (u % 4)
                if br == "A":
                    kn = 128 * (q + 1)
                    for c in range(2):
                        last = dve.tensor_tensor_reduce(
                            out=buf[:, 512 * c:512 * c + kn], in0=S[:, 512 * c:512 * c + kn],
                            in1=bias_a[:, p, 512 - kn:512], scale=SCALE, scalar=LOWEST, op0=ALU.add, op1=ALU.max,
                            accum_out=mx[:, k4 + c:k4 + c + 1])
                    last.then_inc(s_bm, 1)
                    n, f = 2, -1.0
                elif br == "B":
                    link(dve.tensor_tensor_reduce(
                        out=buf[:, 0:512], in0=S[:, 0:512], in1=bias_b[:, q, 3 - p:515 - p], scale=SCALE,
                        scalar=LOWEST, op0=ALU.add, op1=ALU.max, accum_out=mx[:, k4 + 1:k4 + 2]))
                    dve.tensor_tensor_reduce(
                        out=buf[:, 512:768], in0=S[:, 512:768], in1=bias_b[:, q, 515:771], scale=SCALE,
                        scalar=mx[:, k4 + 1:k4 + 2], op0=ALU.add, op1=ALU.max,
                        accum_out=mx[:, k4:k4 + 1]).then_inc(s_bm, 1)
                    n, f = 1, -1.0
                else:
                    dve.tensor_reduce(mx[:, k4:k4 + 2], S[:, :].rearrange("p (h c) -> p h c", h=2)[:, :, 0:256], AXX,
                                      ALU.max).then_inc(s_bm, 1)
                    n, f = 2, -SCALE
                dve.wait_ge(s_bm, u + 1)
                dve.tensor_scalar(nm[:, k4:k4 + n], mx[:, k4:k4 + n], f, None, ALU.mult).then_inc(s_nm, 1)

            def normalise(u):
                br, p, q = attn_slot(u)
                buf, k4 = sc[br][u % 3], 2 * (u % 4)
                n = 1 if br == "B" else 2
                dve.wait_ge(s_ex, u + 1)
                link(dve.reciprocal(rs[:, k4:k4 + n], sm[:, k4:k4 + n]))
                if br == "A":
                    kn = 128 * (q + 1)
                    link(dve.tensor_scalar(buf[:, 512:512 + kn], buf[:, 512:512 + kn], rs[:, k4 + 1:k4 + 2],
                                           lamv[:, 5:6], ALU.mult, ALU.mult))
                    dve.scalar_tensor_tensor(buf[:, 0:kn], buf[:, 0:kn], rs[:, k4:k4 + 1], buf[:, 512:512 + kn],
                                             ALU.mult, ALU.add).then_inc(s_cb, 1)
                elif br == "B":
                    dve.tensor_scalar(buf[:, 0:768], buf[:, 0:768], rs[:, k4:k4 + 1], None, ALU.mult).then_inc(s_cb, 1)
                else:
                    for hh in range(2):
                        w = buf[:, 256 * hh:256 * hh + 256]
                        last = dve.tensor_scalar(w, w, rs[:, k4 + hh:k4 + hh + 1], None, ALU.mult)
                    last.then_inc(s_cb, 1)

            def gate_output(u):
                br, p, q = attn_slot(u)
                if br == "A" or (br == "B" and q % 2 == 0):
                    return
                v = u - OA_UNITS
                pair = v // 2 if br == "B" else OB_UNITS // 2 + (v - OB_UNITS)
                dve.wait_ge(s_pv, u + 1)
                z = oz[:, 4 + q // 2, p:T:4] if br == "B" else oz[:, 6 + q, 128 * p:128 * p + 128]
                dve.tensor_tensor(z, pj[pair % 2][:, 0:128], z, ALU.mult).then_inc(s_ob, 1)

            def attention(which):
                a, b = RANGES[which]
                for s in range(a, b + 4):
                    if a <= s - 4:
                        gate_output(s - 4)
                    if s < b:
                        biased_max(s)
                    if a <= s - 1 < b:
                        normalise(s - 1)

            for n in range(N_FIRST):
                for J in jobs_after(n):
                    stage_job(J)
                lo_split(n + 2)
            dve.wait_ge(s_ev, ev_of(("in", 3)))
            for c in range(2):
                r = slice(64 * c, 64 * c + 64)
                dve.tensor_tensor(pm_a[r, 32 * c:32 * c + 32].rearrange("p (h b) -> p h b", h=4),
                                  qaT[r, :, T:TT], kaT[r, :, T:TT], ALU.mult).then_inc(s_new, 1)
            dve.wait_ge(s_biasa, 16)
            attention("A")
            for n in range(N_FIRST, N_SECOND):
                if n == POS["in", 10]:
                    for h in range(4):
                        dve.wait_ge(s_obc, h + 1)
                        link(dve.scalar_tensor_tensor(oraw[:, h, 0:T], oraw[:, h, 0:T], gs[:, 1:2],
                                                      (pt_bank, po_bank)[h % 2][:, 0:512], ALU.mult, ALU.mult))
                        dve.tensor_tensor(oz[:, h, 0:T], oz[:, h, 0:T], oraw[:, h, 0:T], ALU.mult).then_inc(s_oa, 1)
                for k in RING_AT.get(n, []):
                    sample_scores(k)
                for J in jobs_after(n):
                    stage_job(J)
                lo_split(n + 2)
                if n == N_FIRST + 1:
                    dve.wait_ge(s_ostd, 1)
                    dve.reciprocal(rsq, rsq).then_inc(s_orc, 1)
            dve.wait_ge(s_ev, ev_of(("in", 15)))
            for hh in range(2):
                r = slice(64 * hh, 64 * hh + 64)
                dve.tensor_tensor(pm_b[r, :].rearrange("p (g k h b) -> p g k h b", g=3, k=2, h=2)[:, :, :, hh, :],
                                  qbT[r, :, :, T:TT], kbT[r, :, :, T:TT], ALU.mult).then_inc(s_new, 1)
            dve.wait_ge(s_biasb, 16)
            attention("BM")

            dve.wait_ge(s_sbl, 32)
            dve.wait_ge(s_sT, 1)
            link(dve.tensor_tensor_reduce(out=e_a, in0=bank[0][0:64, 0:W_A], in1=bias_sa, scale=SCALE, scalar=LOWEST,
                                          op0=ALU.add, op1=ALU.max, accum_out=mx[0:64, 0:1]))
            dve.tensor_scalar(nm[0:64, 0:1], mx[0:64, 0:1], -1.0, None, ALU.mult).then_inc(s_snm, 1)
            dve.wait_ge(s_sT, 2)
            link(dve.tensor_tensor_reduce(out=e_b, in0=bank[1][0:32, 0:W_B], in1=bias_sb, scale=SCALE, scalar=LOWEST,
                                          op0=ALU.add, op1=ALU.max, accum_out=mx[0:32, 1:2]))
            dve.tensor_scalar(nm[0:32, 1:2], mx[0:32, 1:2], -1.0, None, ALU.mult).then_inc(s_snm, 1)
            dve.wait_ge(s_sT, 3)
            link(dve.tensor_reduce(mx[0:32, 2:3], bank[2][0:32, 0:256], AXX, ALU.max))
            dve.tensor_scalar(nm[0:32, 2:3], mx[0:32, 2:3], -SCALE, None, ALU.mult).then_inc(s_snm, 1)
            dve.wait_ge(s_sex, 1)
            link(dve.reciprocal(rs[0:64, 0:1], sm[0:64, 0:1]))
            dve.tensor_scalar(g_a[0:32, :], ident[0:32, 0:32], rs[0:32, 0:1], None, ALU.mult)
            dve.tensor_scalar(g_a[32:64, :], ident[32:64, 32:64], rs[32:64, 0:1], lamv[32:64, 5:6],
                              ALU.mult, ALU.mult).then_inc(s_sG, 1)
            for i, g in ((1, g_b), (2, g_m)):
                dve.wait_ge(s_sex, i + 1)
                link(dve.reciprocal(rs[0:32, i:i + 1], sm[0:32, i:i + 1]))
                dve.tensor_scalar(g, ident[0:32, 0:32], rs[0:32, i:i + 1], None, ALU.mult).then_inc(s_sG, 1)
            dve.wait_ge(s_saT, 1)
            dve.tensor_copy(aT[:, 0:288], bank[3][:, 0:288])
            dve.tensor_copy(aT[0:80, 288:320], bank[3][0:80, 288:320]).then_inc(s_sev, 1)
            dve.wait_ge(s_vn, 10)
            dve.wait_ge(s_sev, 1)
            link(dve.tensor_tensor(t_a, vn_a, aT[:, 64:96], ALU.mult))
            dve.wait_ge(s_spv, 3 * NS)
            link(dve.tensor_tensor(o_as, bank[4][:, 0:32], t_a, ALU.add))
            dve.tensor_tensor(sq_s, o_as, o_as, ALU.mult).then_inc(s_so, 1)
            for hh in range(2):
                r = slice(64 * hh, 64 * hh + 64)
                z = oz[r, 6:8, T:TT]
                dve.tensor_tensor(z, bank[4][r, 64:96].rearrange("p (k b h) -> p k b h", k=2, h=2)[:, :, :, hh], z, ALU.mult)
                link(dve.tensor_tensor(t_b[r, :].rearrange("p (g k b) -> p g k b", g=3, k=2),
                                       aT[r, 128:224].rearrange("p (g k h b) -> p g k h b", g=3, k=2, h=2)[:, :, :, hh, :],
                                       vn_b[r, :].rearrange("p (g k b) -> p g k b", g=3, k=2), ALU.mult))
            link(dve.tensor_reduce(t_b2[:, 0:16], t_b.rearrange("p (g x) -> p x g", g=3), AXX, ALU.add))
            for hh in range(2):
                r = slice(64 * hh, 64 * hh + 64)
                w = t_b2[r, 0:16].rearrange("p (k b) -> p k b", k=2)
                link(dve.tensor_tensor(w, bank[5][r, 64:96].rearrange("p (k b h) -> p k b h", k=2, h=2)[:, :, :, hh], w, ALU.add))
            z = oz[:, 4:6, T:TT]
            dve.tensor_tensor(z, z, t_b2[:, 0:16].rearrange("p (k b) -> p k b", k=2), ALU.mult)
            dve.wait_ge(s_sex, 4)
            link(dve.reciprocal(r_s, r_s))
            link(dve.scalar_tensor_tensor(t_a, o_as, gs[:, 1:2], r_s, ALU.mult, ALU.mult))
            z = oz[:, 0:4, T:TT]
            dve.tensor_tensor(z, z, t_a.rearrange("p (h b) -> p h b", h=4), ALU.mult).then_inc(s_so, 1)

            for s in range(2):
                dve.wait_ge(s_oh, s + 1)
                dve.tensor_tensor(ol[:, 4 * s:4 * s + 4, :], oz[:, 4 * s:4 * s + 4, :],
                                  oh[:, 4 * s:4 * s + 4, :].bitcast(f32), ALU.subtract).then_inc(s_ol, 1)

            def mixed_lo(i):
                c, hf = divmod(i, 2)
                dve.wait_ge(s_mh, i + 1)
                cols = slice(HALF * hf, HALF * hf + HALF)
                dve.tensor_tensor(mixl[:, c, cols], mix_t[:, i % 2, 0, :], mixh[:, c, cols].bitcast(f32),
                                  ALU.subtract).then_inc(s_ml, 1)

            for m in range(4):
                for g in range(3):
                    lo_split(N_SECOND + 4 * m + g + 2)
                dve.wait_ge(s_ev, ev_of(("in", 28 + m)))
                for i in range(4 * m, 4 * m + 4):
                    tile, hf = (i // 2) % 2, i % 2
                    cols = slice(HALF * hf, HALF * hf + HALF)
                    dve.wait_ge(s_pp, i + 1)
                    if i >= 2:
                        dve.wait_ge(s_ml, i - 1)
                    for br in range(3):
                        last = dve.tensor_tensor(mix_t[:, i % 2, br, :], bank[3 * (i % 2) + br][:, 0:HALF],
                                                 gate[:, br, tile, cols], ALU.mult)
                    last.then_inc(s_mx, 1)
                    dve.wait_ge(s_mx, i + 1)
                    t0 = mix_t[:, i % 2, 0, :]
                    link(dve.tensor_tensor(t0, t0, mix_t[:, i % 2, 1, :], ALU.add))
                    dve.tensor_tensor(t0, t0, mix_t[:, i % 2, 2, :], ALU.add).then_inc(s_mix, 1)
                    if i % 4:
                        mixed_lo(i - 1)
                mixed_lo(4 * m + 3)
                lo_split(N_SECOND + 4 * m + 3 + 2)
            dve.wait_ge(s_yl, 80)
            for m in range(4):
                for t in range(5):
                    i = 5 * m + t
                    r = rows_of(t)
                    dve.wait_ge(s_po, i + 1)
                    y = y_nat[0:r, t, CW * m:CW * m + CW]
                    dve.tensor_tensor(y, pj[i % 2][0:r, 0:CW], y, ALU.add).then_inc(s_y, 1)
                lo_split(N_THIRD + m + 2)
            dve.wait_ge(s_gf, 16)
            for t in range(5):
                r = rows_of(t)
                dve.wait_ge(s_ystd, t + 1)
                link(dve.reciprocal(rstd[0:r, 8 + t:9 + t], rstd[0:r, 8 + t:9 + t]))
                dve.scalar_tensor_tensor(y_nat[0:r, t, :], y_nat[0:r, t, :], rstd[0:r, 8 + t:9 + t],
                                         g_fin[0:r, :], ALU.mult, ALU.mult).then_inc(s_yo, 1)


def constants():
    f = np.float32
    slope = [2.0 ** (-2.0 * (h + 1)) for h in range(4)]
    neg = -1e30 / SCALE

    def bias(dist, ok, h):
        return np.where(ok, -slope[h] * dist / SCALE, neg)

    p = np.arange(128)[:, None]
    y = np.arange(512)[None, :] - 384
    bias_a = np.stack([bias(p - y, p >= y, h) for h in range(4)], 1)
    d1 = 4 * p - (np.arange(515)[None, :] - 3)
    d2 = 4 * (p - np.arange(128)[None, :])
    bias_b = np.stack([np.concatenate([bias(d1, (d1 >= 0) & (d1 <= 128), h), bias(d2, d2 >= 0, h),
                                       bias(d2, (d2 >= 0) & (d2 % 16 == 0), h)], 1) for h in range(4)], 1)
    rows = np.arange(64)
    ha = (rows // 8) % 4
    bias_sa = np.stack([bias(256 - np.arange(W_A), np.ones(W_A, bool), h) for h in ha])
    cached = [d * (n - np.arange(n)) for n, d in zip(G_ROWS, DIL)]
    dist_b = np.concatenate(cached + [np.zeros(3)])
    bias_sb = np.stack([bias(dist_b, np.ones(W_B, bool), h) for h in ha[:32]])
    sel = np.zeros((128, 4, 4))
    row = np.zeros((4, 4, 128))
    for h in range(4):
        sel[:, h, h] = 1.0 / 128
        row[h, h, :] = 1.0
    return {"c_ident": np.eye(128, dtype=f), "c_bias_a": bias_a.astype(f), "c_bias_b": bias_b.astype(f),
            "c_bias_sa": bias_sa.astype(f), "c_bias_sb": bias_sb.astype(f), "c_selh": sel.astype(f),
            "c_rowh": row.astype(f)}


_INS = ["x_prompt", "x_sample", "mem_prompt", "cache_diff_kv", "page_table", "cache_win1_kv", "cache_win2_kv",
        "cache_win3_kv", "cache_mem_kv", "g_norm", "w_in", "g_mem", "w_mem_kv", "lambda_q1", "lambda_k1",
        "lambda_q2", "lambda_k2", "g_subln", "w_proj_a", "w_proj_b", "w_proj_m", "w_out", "g_final"]
_OUTS = [(1, 512, 1024), (8, 1, 1024), (1, 1, 512, 2, 4, 128), (1, 1, 128, 2, 4, 64), (1, 1, 512, 2, 4, 64),
         (1, 1, 512, 2, 4, 64), (1, 1, 256, 2, 4, 64), (1, 8, 1, 2, 4, 128), (1, 8, 1, 2, 4, 64),
         (1, 8, 1, 2, 4, 64), (1, 8, 1, 2, 4, 64)]


def kernel(**inputs):
    import concourse.bacc as bacc
    from concourse.bass_utils import run_bass_kernel_spmd

    nc = bacc.Bacc("TRN2", target_bir_lowering=False, num_devices=1)
    arrays = {f"in_{n}": np.ascontiguousarray(inputs[n]) for n in _INS}
    arrays.update({f"in_{n}": a for n, a in constants().items()})
    ins = {n[3:]: nc.dram_tensor(n, a.shape, mybir.dt.from_np(a.dtype), kind="ExternalInput").ap()
           for n, a in arrays.items()}
    outs = [nc.dram_tensor(f"out_{i}", s, mybir.dt.float32, kind="ExternalOutput").ap() for i, s in enumerate(_OUTS)]
    build_kernel(nc, ins, outs)
    r = run_bass_kernel_spmd(nc, [arrays], core_ids=[0])
    return tuple(r.results[0][f"out_{i}"] for i in range(len(_OUTS)))
```

```python
from contextlib import ExitStack

import numpy as np
import concourse.bass as bass
from concourse import mybir

D = 1024
T = 512
NS = 8
TT = T + NS
HALF = TT // 2
KT = D // 128
NMEM = 256
CW = 256
EPS = 1e-6
LAM_INIT = 0.2
SCALE = 0.125
QT = T // 128
W_A = 2 * 128 + 1
G_ROWS = (128, 64, 16)
DIL = (1, 4, 16)
W_B = sum(G_ROWS) + 3


def chunk_sequence():
    first = [("mem", 0), ("mem", 1)] + [("in", j) for j in (4, 5, 2, 3, 0, 1)]
    beside_a = [("in", j) for j in (6, 7, 17)]
    second = [("in", j) for j in (18, 8, 11, 14, 10, 9, 13, 12, 16, 15, 19)]
    beside_bm = [("in", 20), ("in", 24)]
    third = [("in", 28), ("proj", 0)]
    for m in range(1, 4):
        third += [("in", 20 + m), ("in", 24 + m), ("in", 28 + m), ("proj", m)]
    return first, beside_a, second, beside_bm, third, [("out", m) for m in range(4)]


def build_kernel(nc, ins, outs):
    f32, f32r, i32 = mybir.dt.float32, mybir.dt.float32r, mybir.dt.int32
    ACT = mybir.ActivationFunctionType
    ALU = mybir.AluOpType
    AXX = mybir.AxisListType.X

    PARTS = chunk_sequence()
    SEQ = sum(PARTS, [])
    N_A, N_SECOND, N_BM, N_THIRD, N_OUT = (sum(map(len, PARTS[:i])) for i in range(1, 6))
    POS = {k: n for n, k in enumerate(SEQ)}

    x_p = ins["x_prompt"].rearrange("a t d -> (a t) d")
    x_s = ins["x_sample"].rearrange("b t d -> (b t) d")
    x_m = ins["mem_prompt"].rearrange("a t d -> (a t) d")
    w_in = ins["w_in"].rearrange("l (k p) n -> p (l k) n", p=128)
    w_mem = ins["w_mem_kv"].rearrange("l (k p) n -> p (l k) n", p=128)
    w_pa = ins["w_proj_a"].rearrange("l (k p) n -> p (l k) n", p=128)
    w_pb = ins["w_proj_b"].rearrange("l (k p) n -> p (l k) n", p=128)
    w_pm = ins["w_proj_m"].rearrange("l (k p) n -> p (l k) n", p=128)
    w_out = ins["w_out"].rearrange("l (k p) n -> p (l k) n", p=128)
    cache_a = ins["cache_diff_kv"].rearrange("l n p s h d -> (l n) p s (h d)")
    cache_1 = ins["cache_win1_kv"].rearrange("l b p s h d -> (l b) p s (h d)")
    cache_2 = ins["cache_win2_kv"].rearrange("l b (j r) s h d -> (l b) j r s (h d)", r=DIL[1])
    cache_3 = ins["cache_win3_kv"].rearrange("l b (j r) s h d -> (l b) j r s (h d)", r=DIL[2])
    cache_m = ins["cache_mem_kv"].rearrange("l b (t p) s h d -> (l b) p t s (h d)", p=128)
    diff_p = outs[2].rearrange("l b t s h d -> (l b t) s (h d)")
    win1_p = outs[3].rearrange("l b t s h d -> (l b t) (s h d)")
    win2_p = outs[4].rearrange("l b (j r) s h d -> r (l b j) (s h d)", r=4)
    win3_p = outs[5].rearrange("l b (j r) s h d -> r (l b j) (s h d)", r=4)
    mem_p = outs[6].rearrange("l b t s h d -> (l b t) (s h d)")
    diff_s = outs[7].rearrange("l b t s h d -> (l b t) s (h d)")
    win_s = [o.rearrange("l b t s h d -> (l b t) (s h d)") for o in outs[8:11]]
    y_p = outs[0].rearrange("a t d -> (a t) d")
    y_s = outs[1].rearrange("b t d -> (b t) d")

    ctx = ExitStack()
    early = ExitStack()
    with ctx:
        def sb(name, shape, dt=f32, where=ctx):
            return where.enter_context(nc.sbuf_tensor(name, shape, dt))

        def sem(name):
            return ctx.enter_context(nc.semaphore(name))

        xh = sb("xh", [128, KT, TT], f32r)
        xl = sb("xl", [128, KT, TT], f32r)
        w_raw = sb("w_raw", [128, 3, 4, CW])
        w_hi = sb("w_hi", [128, 2, KT, CW], f32r)
        w_lo = sb("w_lo", [128, 2, KT, CW], f32r)
        oz = sb("oz", [128, KT, TT])
        ident = sb("ident_sb", [128, 128])
        ones = sb("ones", [128, 128])
        ssq = sb("ssq", [128, 16])
        rstd = sb("rstd", [128, 16])
        eps = sb("eps", [128, 1])
        lamv = sb("lamv", [128, 8])
        gs = sb("gs", [128, 2])

        prod = sb("prod", [128, 1024], f32, early)
        stage = sb("stage", [128, 2, 512], f32, early)
        qs_a = sb("qs_a", [8, 512], f32, early)
        qs_m = sb("qs_m", [8, 256], f32, early)
        qs_b = sb("qs_b", [8, 3, 256], f32, early)
        row_h = sb("row_h", [4, 4, 128], f32, early)
        early.close()
        gate = sb("gate", [128, 3, 2, TT])
        g_fin = sb("g_fin", [128, D])

        memh = sb("memh", [128, KT, NMEM], f32r, early)
        meml = sb("meml", [128, KT, NMEM], f32r, early)
        early.close()
        work = sb("work", [128, 4 * KT * NMEM // 2], f32, early)
        region = sb("region", [128, 8320], f32, early)
        v_b = sb("v_b", [128, 3, QT, 256], f32, early)
        bias_b = sb("bias_b", [128, 4, 771], f32, early)
        vT = sb("vT", [128, 4, TT], f32, early)
        ring = sb("ring", [128, 2, 2, 512], f32, early)
        kmT = sb("kmT", [128, 2, NMEM], f32, early)
        vm = sb("vm", [128, 2, 256], f32, early)
        small = sb("small", [128, 1100], f32, early)
        pages = sb("pages", [1, 16], i32, early)
        sel_h = sb("sel_h", [128, 4, 4], f32, early)
        early.close()

        mixh = sb("mixh", [128, KT, TT], f32r, early)
        mixl = sb("mixl", [128, KT, TT], f32r, early)
        oh = sb("oh", [128, KT, TT], f32r, early)
        ol = sb("ol", [128, KT, TT], f32r, early)
        mix_t = sb("mix_t", [128, 2, 3, HALF], f32, early)
        y_nat = sb("y_nat", [128, 5, D], f32, early)
        early.close()

        xin = [region[:, 1024 * t:1024 * t + 1024] for t in range(7)]
        qaT = region[:, 0:4 * TT].rearrange("p (h t) -> p h t", h=4)
        kaT = region[:, 4 * TT:8 * TT].rearrange("p (h t) -> p h t", h=4)
        v_a = region[:, 8 * TT:8 * TT + 2048].rearrange("p (t c) -> p t c", t=4)
        bias_a = region[:, 8 * TT + 2048:8 * TT + 4096].rearrange("p (h c) -> p h c", h=4)
        qbT = region[:, 0:6 * TT].rearrange("p (g h t) -> p g h t", g=3, h=2)
        kbT = region[:, 6 * TT:12 * TT].rearrange("p (g h t) -> p g h t", g=3, h=2)
        qmT = region[:, 12 * TT:14 * TT].rearrange("p (h t) -> p h t", h=2)
        g_row = ring[:, 0, :, :].rearrange("p a b -> p (a b)")
        g_row_m = ring[:, 1, :, :].rearrange("p a b -> p (a b)")
        sc = {"A": [work[:, 1024 * i:1024 * i + 1024] for i in range(3)],
              "B": [work[:, 768 * i:768 * i + 768] for i in range(3)]}
        pt = {"A": [work[:, 3072 + 512 * i:3584 + 512 * i] for i in range(2)],
              "B": [work[:, 2304 + 768 * i:3072 + 768 * i] for i in range(2)]}
        sc["M"], pt["M"] = sc["B"], pt["B"]
        oraw = vT
        oraw_sq = [work[:, 512 * h:512 * h + 512] for h in range(4)]
        rsq = work[0:4, 2048:2560]

        o = 0

        def cut(n):
            nonlocal o
            o += n
            return small[:, o - n:o]
        mx = cut(8)
        nm = cut(8)
        sm = cut(8)
        rs = cut(8)
        smx, snm, ssm, srs = cut(4), cut(4), cut(4), cut(4)
        lam_in = cut(256)
        s_a = cut(128)
        s_m = cut(64)
        s_1 = cut(32)
        s_23 = cut(32)
        vn_a = cut(32)
        vn_b = cut(48)
        pm_a = cut(64)
        pm_b = cut(96)
        bias_sa = work[0:64, 2560:2560 + W_A]
        e_a = work[0:64, 2832:2832 + W_A]
        e_m = work[0:32, 3104:3360]
        g_a = work[0:64, 3360:3392]
        g_m = work[0:32, 3392:3424]
        swork = vT[:, :, :].rearrange("p a b -> p (a b)")
        g_b = swork[0:32, 992:1024]
        aT = swork[:, 1040:1360]
        t_a = swork[:, 1360:1392]
        o_as = swork[:, 1392:1424]
        sq_s = swork[:, 1424:1456]
        r_s = swork[:, 1456:1488]
        t_b = swork[:, 1488:1536]
        t_b2 = swork[:, 1536:1568]
        bias_sb = swork[0:32, 1568:1568 + W_B]
        e_b = swork[0:32, 1840:1840 + W_B]
        own_a, own_m = region[:, 7280:7792], region[:, 7792:8304]
        own_b = swork[:, 0:512]
        ov_sa = swork[0:32, 512:1024]
        ov_sb = swork[64:96, 512:1024]

        pj = [ctx.enter_context(nc.psum_tensor(f"pj{i}", [128, 512], f32)) for i in range(2)]
        ps = [ctx.enter_context(nc.psum_tensor(f"ps{i}", [128, 1024], f32)) for i in range(2)]
        pt_bank = ctx.enter_context(nc.psum_tensor("pt_bank", [128, 512], f32))
        po_bank = ctx.enter_context(nc.psum_tensor("po_bank", [128, 512], f32))
        bank = [ps[0][:, 0:512], ps[0][:, 512:1024], ps[1][:, 0:512], ps[1][:, 512:1024],
                pt_bank[:, :], po_bank[:, :]]

        s_raw = [sem(f"raw_loaded{i}") for i in range(3)]
        s_hi = sem("half_hi")
        s_lo = sem("half_lo")
        s_wfree = sem("chunk_used")
        s_const = sem("const_loaded")
        s_ident = sem("ident_loaded")
        s_gain = [sem(f"gain_loaded{i}") for i in range(2)]
        s_vn = sem("new_values_kept")
        s_ob = sem("o_bm_gated")
        s_biasa = sem("bias_a_loaded")
        s_biasb = sem("bias_b_loaded")
        s_xin = [sem(f"x_loaded{i}") for i in range(7)]
        s_init = sem("init_done")
        s_dv = sem("dve_step")
        s_ac = sem("act_step")
        s_sq = sem("x_squared")
        s_std = sem("x_std")
        s_xn = sem("x_normed")
        s_xt = sem("x_transposed")
        s_xh = sem("x_hi")
        s_xl = sem("x_lo")
        s_pj = sem("proj_done")
        s_ev = sem("proj_evacuated")
        s_nat = sem("nat_done")
        s_stage = sem("nat_staged")
        s_pc = sem("nat_copied")
        s_out = [sem(f"stage_stored{i}") for i in range(2)]
        s_S = sem("scores")
        s_bm = sem("biased_max")
        s_nm = sem("neg_max")
        s_ex = sem("exps")
        s_cb = sem("probs")
        s_T = sem("probs_transposed")
        s_te = sem("probsT_copied")
        s_pv = sem("pv_done")
        s_oe = sem("o_evacuated")
        s_lexp = sem("lambda_exp")
        s_lsum = sem("lambda_sum")
        s_osq = sem("o_squared")
        s_ov = sem("o_var")
        s_ostd = sem("o_std")
        s_orc = sem("o_rstd")
        s_obc = sem("o_rstd_bc")
        s_oa = sem("o_a_done")
        s_kr = [sem(f"ring_loaded{i}") for i in range(2)]
        s_qb = sem("q_broadcast")
        s_km = sem("k_multiplied")
        s_kd = sem("sample_scores")
        s_new = sem("new_products")
        s_sT = sem("samples_transposed")
        s_snm = sem("samples_neg_max")
        s_sex = sem("samples_exp")
        s_sG = sem("samples_norm")
        s_saT = sem("samples_probsT")
        s_sev = sem("samples_probsT_copied")
        s_spv = sem("samples_pv")
        s_own = sem("samples_masked_zeroed")
        s_sov = sem("samples_pv_copied")
        s_sot = sem("samples_o_transposed")
        s_silu = sem("silu_done")
        s_sig = sem("sigmoid_done")
        s_so = sem("samples_o")
        s_sbl = [sem(f"sample_bias_loaded{i}") for i in range(2)]
        s_oh = sem("o_hi")
        s_ol = sem("o_lo")
        s_pp = sem("branch_projected")
        s_mx = sem("mix_read")
        s_mix = sem("mixed")
        s_mh = sem("mixed_hi")
        s_ml = sem("mixed_lo")
        s_po = sem("out_projected")
        s_y = sem("y_added")
        s_ysq = sem("y_squared")
        s_ystd = sem("y_std")
        s_yo = sem("y_normed")
        s_yl = sem("residual_loaded")
        s_gf = sem("g_final_loaded")
        s_ys = sem("y_stored")
        s_pg = sem("pages_loaded")

        def units_of(kind):
            return {"mem": 2, "in": 4}.get(kind, 0)

        def pj_of(u):
            return pj[0] if U0[N_BM] <= u < U0[N_THIRD] else pj[u % 2]

        def sole_bank(u):
            return U0[N_BM] <= u <= U0[N_THIRD]
        U0 = [0]
        for kind, _ in SEQ:
            U0.append(U0[-1] + units_of(kind))

        def ev_of(key):
            return U0[POS[key] + 1]

        JOBS = []

        def job(need, rows, srcs, stores, copies):
            JOBS.append((POS[need], rows, srcs, stores, copies))

        def tok(ap, t):
            return ap[:, 128 * t:128 * t + (128 if t < 4 else NS)]

        for t in range(2):
            job(("mem", 1), 128, [kmT[:, 0, 128 * t:128 * t + 128], kmT[:, 1, 128 * t:128 * t + 128],
                                  vT[:, 2, 128 * t:128 * t + 128], vT[:, 3, 128 * t:128 * t + 128]],
                [(mem_p[128 * t:128 * t + 128, :], 0, 512)], [(vm[:, t, :], 256, 512)])
        J_MEM = len(JOBS)
        for t in range(5):
            dst = diff_p[128 * t:128 * t + 128, 1, :] if t < 4 else diff_s[:, 1, :]
            job(("in", 5), 128 if t < 4 else NS, [tok(vT[:, h, :], t) for h in range(4)],
                [(dst, 0, 512)], [(v_a[:, t, :], 0, 512)] if t < 4 else [])
        for t in range(5):
            dst = diff_p[128 * t:128 * t + 128, 0, :] if t < 4 else diff_s[:, 0, :]
            job(("in", 3), 128 if t < 4 else NS, [tok(kaT[:, h, :], t) for h in range(4)],
                [(dst, 0, 512)], [])
        J_A = len(JOBS)
        job(("in", 17), NS, [tok(qaT[:, h, :], 4) for h in range(4)], [], [(qs_a[:, :], 0, 512)])
        J_QA = len(JOBS)
        job(("in", 18), NS, [tok(qmT[:, h, :], 4) for h in range(2)], [], [(qs_m[:, :], 0, 256)])
        J_QM = len(JOBS)
        for g in range(3):
            job(("in", 8 + 3 * g), NS, [tok(qbT[:, g, h, :], 4) for h in range(2)], [], [(qs_b[:, g, :], 0, 256)])
        J_QB = len(JOBS)
        J_G = []
        for g in range(3):
            vt = [vT[:, (2 * g) % 4 + h, :] for h in range(2)]
            need = ("in", 9 + 3 * g)
            for t in range(4):
                if g == 0 and t < 3:
                    job(need, 128, [tok(v, t) for v in vt], [], [(v_b[:, 0, t, :], 0, 256)])
                    continue
                if g == 0:
                    srcs = [tok(kbT[:, 0, h, :], t) for h in range(2)] + [tok(v, t) for v in vt]
                    dst = win1_p
                else:
                    srcs = [kbT[:, g, h, t:T:4] for h in range(2)] + [v[:, t:T:4] for v in vt]
                    dst = (win2_p, win3_p)[g - 1][t]
                job(need, 128, srcs, [(dst, 0, 512)], [(v_b[:, g, t, :], 256, 512)])
            job(need, NS, [tok(kbT[:, g, h, :], 4) for h in range(2)] + [tok(v, 4) for v in vt],
                [(win_s[g], 0, 512)], [])
            J_G.append(len(JOBS))
        NJ = len(JOBS)
        PC = [0]
        OUTC = [0, 0]
        OUT_AT = []
        for J, (_, _, _, stores, copies) in enumerate(JOBS):
            PC.append(PC[-1] + len(copies))
            OUTC[J % 2] += 16 * len(stores)
            OUT_AT.append(OUTC[J % 2])

        V_GUARD = {("in", 5): J_MEM, ("in", 10): J_A, ("in", 13): J_A, ("in", 16): J_G[0]}

        RINGS = [(k, b) for b in range(NS) for k in "AM"] + [("B", b) for b in range(NS)]
        NK = len(RINGS)
        RINGS += [(k, b) for k in "BAM" for b in range(NS)]

        BESIDE = {}
        seen = [0] * len(SEQ)
        for J, (n, *_) in enumerate(JOBS):
            BESIDE.setdefault((n + 1, seen[n] // 2), []).append(("job", J))
            seen[n] += 1
        for k in range(NK):
            if k < 2 * NS:
                at = (N_SECOND + 1 + k // 2, k % 2)
            else:
                at = (N_BM - 2 + (k - 2 * NS) // 4, (0, 1, 2, 2)[k % 4])
            BESIDE.setdefault(at, []).append(("ring", k))

        def beside(n, k=None):
            return [e for i in (range(4) if k is None else [k]) for e in BESIDE.get((n, i), [])]

        LOADS = {"A": 2, "M": 1, "B": 3}
        KR = []
        cum = [0, 0]
        for k, (kind, _) in enumerate(RINGS):
            cum[k % 2] += 16 * LOADS[kind]
            KR.append(cum[k % 2])
        OA_UNITS = 4 * QT
        OB_UNITS = 4 * 4
        OM_UNITS = QT * 2
        NU = OA_UNITS + OB_UNITS + OM_UNITS

        SLOTS = {"A": [s for s in range(16) if s % 4 < 3], "BM": list(range(4, 20, 2))}
        FILL, SPLIT = {}, {}
        for which, n0 in (("A", N_A), ("BM", N_BM)):
            FILL[which] = {s: (n0 + i // 4, i % 4) for i, s in enumerate(SLOTS[which])}
            SPLIT[which] = {}
            for s, (n, k) in FILL[which].items():
                if k == 3:
                    SPLIT[which].setdefault(s, []).append((n + 2, 0))
                    SPLIT[which].setdefault(s + 1, []).append((n + 2, 1))

        RAWC = [0, 0, 0]
        RAW_AT = []
        for m in range(2 * len(SEQ)):
            RAWC[m % 3] += 32 if (SEQ[m // 2][0] == "proj" and m % 2) else 16
            RAW_AT.append(RAWC[m % 3])

        block = ctx.enter_context(nc.Block())

        @block.sync
        def _(sp):
            def load_weights(m):
                n, s = divmod(m, 2)
                kind, j = SEQ[n]
                if m >= 3:
                    sp.wait_ge(s_lo, m - 2)
                if kind == "proj" and s == 1:
                    sp.dma_start(w_raw[:, m % 3, 0:2, :], w_pb[:, :, CW * j:CW * j + CW]).then_inc(s_raw[m % 3], 16)
                    sp.dma_start(w_raw[:, m % 3, 2:4, :], w_pm[:, :, CW * j:CW * j + CW]).then_inc(s_raw[m % 3], 16)
                    return
                src = {"mem": w_mem, "in": w_in, "proj": w_pa, "out": w_out}[kind]
                sp.dma_start(w_raw[:, m % 3, :, :],
                             src[:, 4 * s:4 * s + 4, CW * j:CW * j + CW]).then_inc(s_raw[m % 3], 16)

            sp.dma_start(xin[5], x_m[0:128, :]).then_inc(s_xin[5], 16)
            sp.dma_start(g_row_m, ins["g_mem"].partition_broadcast(128).rearrange("p a d -> p (a d)")).then_inc(s_gain[1], 16)
            sp.dma_start(ident[:, :], ins["c_ident"]).then_inc(s_ident, 16)
            sp.dma_start(xin[6], x_m[128:256, :]).then_inc(s_xin[6], 16)
            load_weights(0)
            load_weights(1)
            sp.dma_start(g_row, ins["g_norm"].partition_broadcast(128).rearrange("p a d -> p (a d)")).then_inc(s_gain[0], 16)
            sp.dma_start(xin[0], x_p[0:128, :]).then_inc(s_xin[0], 16)
            sp.dma_start(xin[1], x_p[128:256, :]).then_inc(s_xin[1], 16)
            load_weights(2)
            sp.dma_start(xin[2], x_p[256:384, :]).then_inc(s_xin[2], 16)
            sp.dma_start(xin[3], x_p[384:512, :]).then_inc(s_xin[3], 16)
            sp.dma_start(xin[4][0:NS, :], x_s).then_inc(s_xin[4], 16)
            for m in range(3, 2 * len(SEQ)):
                load_weights(m)

        @block.gpsimd
        def _(pool):
            pool.memset(ones[:, :], 1.0).then_inc(s_init, 1)
            pool.memset(eps[:, :], EPS).then_inc(s_init, 1)
            pool.memset(ssq[:, :], 1.0).then_inc(s_init, 1)
            pool.memset(pm_a, 0.0).then_inc(s_init, 1)
            pool.memset(pm_b, 0.0).then_inc(s_init, 1)
            for i, n in enumerate(("lambda_q1", "lambda_k1", "lambda_q2", "lambda_k2")):
                pool.dma_start(lam_in[:, 64 * i:64 * i + 64],
                               ins[n].partition_broadcast(128).rearrange("p a d -> p (a d)")).then_inc(s_const, 16)
            pool.dma_start(gs[:, 0:1], ins["g_subln"].rearrange("l d -> d l")).then_inc(s_const, 16)
            pool.dma_start(sel_h[:, :, :], ins["c_selh"]).then_inc(s_const, 16)
            pool.dma_start(row_h[:, :, :], ins["c_rowh"]).then_inc(s_const, 16)
            pool.dma_start(pages[:, :], ins["page_table"].rearrange("b n -> (b n)").unsqueeze(0)).then_inc(s_pg, 16)

            def store_job(J):
                _, rows, _, stores, copies = JOBS[J]
                pool.wait_ge(s_stage, J + 1)
                for dst, a, b in copies:
                    pool.tensor_copy(dst, stage[0:rows, J % 2, a:b]).then_inc(s_pc, 1)
                for dst, a, b in stores:
                    pool.dma_start(dst, stage[0:rows, J % 2, a:b]).then_inc(s_out[J % 2], 16)

            def load_ring(k):
                kind, b = RINGS[k]
                s = 0 if k < NK else 1
                if k >= 2 and k - 2 < NK:
                    pool.wait_ge(s_km, k - 1)
                elif k >= 2:
                    pool.wait_ge(s_spv, k - 2 - NK + 1)
                slot = ring[:, k % 2, :, :]
                if kind == "A":
                    for t in range(2):
                        page = pool.value_load(pages[0:1, 2 * b + t:2 * b + t + 1], min_val=0,
                                               max_val=cache_a.shape[0] - 1)
                        pool.dma_start(slot[:, t, :], cache_a[bass.ds(page, 1), :, s, :].rearrange("a p c -> (a p) c")).then_inc(s_kr[k % 2], 16)
                elif kind == "M":
                    pool.dma_start(slot[:, :, 0:256], cache_m[b, :, :, s, :]).then_inc(s_kr[k % 2], 16)
                else:
                    pool.dma_start(slot[:, 0, 0:256], cache_1[b, :, s, :]).then_inc(s_kr[k % 2], 16)
                    pool.dma_start(slot[0:64, 1, 0:256], cache_2[b, :, 0, s, :]).then_inc(s_kr[k % 2], 16)
                    pool.dma_start(slot[64:80, 1, 0:256], cache_3[b, :, 0, s, :]).then_inc(s_kr[k % 2], 16)

            def run_beside(n):
                for what, i in beside(n):
                    if what == "job":
                        store_job(i)
                    else:
                        load_ring(i + 2)

            for n in range(N_SECOND):
                if n == 3:
                    pool.wait_ge(s_xt, 14)
                    pool.dma_start(bias_a, ins["c_bias_a"]).then_inc(s_biasa, 16)
                run_beside(n)
            pool.dma_start(bias_b[:, :, :], ins["c_bias_b"]).then_inc(s_biasb, 16)
            pool.wait_ge(s_pg, 16)
            pool.wait_ge(s_xn, 7)
            load_ring(0)
            load_ring(1)
            pool.wait_ge(s_pv, OA_UNITS)
            pool.dma_start(bias_sa, ins["c_bias_sa"]).then_inc(s_sbl[0], 16)
            for n in range(N_SECOND, N_BM):
                run_beside(n)
                if n == N_BM - 2:
                    pool.wait_ge(s_nat, J_G[1])
                    pool.wait_ge(s_vn, 10)
                    pool.dma_start(bias_sb, ins["c_bias_sb"]).then_inc(s_sbl[1], 16)
            for k in range(NK + 2, 2 * NK):
                load_ring(k)
            pool.wait_ge(s_so, 2)
            for i in range(2):
                pool.wait_ge(s_out[i], OUTC[i])
            for t in range(4):
                pool.dma_start(y_nat[:, t, :], x_p[128 * t:128 * t + 128, :]).then_inc(s_yl, 16)
            pool.dma_start(y_nat[0:NS, 4, :], x_s).then_inc(s_yl, 16)
            pool.dma_start(g_fin[:, :], ins["g_final"].unsqueeze(0).partition_broadcast(128).rearrange("p a d -> p (a d)")).then_inc(s_gf, 16)
            for t in range(5):
                pool.wait_ge(s_yo, t + 1)
                rows = 128 if t < 4 else NS
                dst = y_p[128 * t:128 * t + 128, :] if t < 4 else y_s
                pool.dma_start(dst, y_nat[0:rows, t, :]).then_inc(s_ys, 16)
            pool.wait_ge(s_ys, 80)

        XORDER = [5, 6, 0, 1, 2, 3, 4]

        def rows_of(t):
            return NS if t == 4 else 128

        def x_dst(buf_x, buf_m, t, kg):
            if t < 5:
                return buf_x[:, 4 * kg:4 * kg + 4, 128 * t:128 * t + rows_of(t)]
            return buf_m[:, 4 * kg:4 * kg + 4, 128 * (t - 5):128 * (t - 5) + 128]

        def attn_slot(u):
            if u < OA_UNITS:
                return "A", u // QT, u % QT
            u -= OA_UNITS
            if u < OB_UNITS:
                return "B", u // 4, u % 4
            u -= OB_UNITS
            return "M", u // 2, u % 2

        def pairs_through(u):
            v = u - OA_UNITS + 1
            return max(0, v // 2 if v <= OB_UNITS else v - OB_UNITS // 2)

        RANGES = {"A": (0, OA_UNITS), "BM": (OA_UNITS, NU)}

        @block.tensor
        def _(pe):
            def transpose_input(i):
                t = XORDER[i]
                pe.wait_ge(s_xn, i + 1)
                for kg in range(2):
                    g = 2 * i + kg
                    if g >= 4:
                        pe.wait_ge(s_xl, g - 3)
                    for c in range(4):
                        last = pe.transpose(bank[g % 4][:, 128 * c:128 * c + rows_of(t)],
                                            xin[t][0:rows_of(t), 512 * kg + 128 * c:512 * kg + 128 * c + 128],
                                            ident[0:rows_of(t), 0:rows_of(t)])
                    last.then_inc(s_xt, 1)

            def product(out, parts, hi_m, lo_m):
                n = len(parts)
                for i, (slot, kt, c0, cn, kx, a, b) in enumerate(parts):
                    wh = w_hi[:, slot, kt, c0:c0 + cn]
                    wl = w_lo[:, slot, kt, c0:c0 + cn]
                    mh, ml = hi_m[:, kx, a:b], lo_m[:, kx, a:b]
                    pe.matmul(out, wh, mh, start=(i == 0), stop=False)
                    pe.matmul(out, wl, mh, start=False, stop=False)
                    last = pe.matmul(out, wh, ml, start=False, stop=(i == n - 1))
                return last

            def nat_job(J):
                need, rows, srcs, _, _ = JOBS[J]
                pe.wait_ge(s_ev, U0[need + 1])
                if J >= 2:
                    pe.wait_ge(s_stage, J - 1)
                for c, src in enumerate(srcs):
                    last = pe.transpose(bank[J % 2][0:rows, 128 * c:128 * c + 128], src, ident[:, :])
                last.then_inc(s_nat, 1)

            def project_unit(n, k):
                kind, j = SEQ[n]
                if k == 0:
                    pe.wait_ge(s_lo, 2 * n + 2)
                hi_m, lo_m = (memh, meml) if kind == "mem" else (xh, xl)
                tile, (a, b) = (k, (0, NMEM)) if kind == "mem" else (k // 2, ((0, HALF), (HALF, TT))[k % 2])
                u = U0[n] + k
                if u >= 2:
                    pe.wait_ge(s_ev, u if sole_bank(u) else u - 1)
                product(pj_of(u)[:, 0:b - a],
                        [(n % 2, kt, 128 * tile, 128, kt, a, b) for kt in range(KT)], hi_m, lo_m).then_inc(s_pj, 1)

            def project_chunk(n):
                for k in range(units_of(SEQ[n][0])):
                    project_unit(n, k)
                    for what, i in beside(n, k):
                        (nat_job if what == "job" else broadcast_q)(i)

            def broadcast_q(k):
                kind, b = RINGS[k]
                pe.wait_ge(s_pc, PC[{"A": J_QA, "M": J_QM, "B": J_QB}[kind]])
                if k >= 2:
                    pe.wait_ge(s_km, k - 1)
                out = bank[2 + k % 2]
                pick = ident[0:NS, b:b + 1]
                if kind == "A":
                    last = pe.matmul(out, pick.to_broadcast([NS, 128]), qs_a[:, :], start=True, stop=True)
                elif kind == "M":
                    last = pe.matmul(out[:, 0:256], pick.to_broadcast([NS, 128]), qs_m[:, :], start=True, stop=True)
                else:
                    pe.matmul(out[:, 0:256], pick.to_broadcast([NS, 128]), qs_b[:, 0, :], start=True, stop=True)
                    pe.matmul(out[0:64, 256:512], pick.to_broadcast([NS, 64]), qs_b[:, 1, :], start=True, stop=True)
                    last = pe.matmul(out[64:80, 256:512], pick.to_broadcast([NS, 16]), qs_b[:, 2, :], start=True, stop=True)
                last.then_inc(s_qb, 1)

            def scores(u):
                br, p, q = attn_slot(u)
                S = ps[u % 2]
                if u >= 2:
                    pe.wait_ge(s_bm, u - 1)
                    if attn_slot(u - 2)[0] == "M":
                        pe.wait_ge(s_ex, u - 1)
                if br == "A":
                    for c in range(2):
                        rows = slice(64 * c, 64 * c + 64)
                        last = pe.matmul(S[:, 512 * c:512 * c + 128 * (q + 1)],
                                         qaT[rows, p, 128 * q:128 * q + 128],
                                         kaT[rows, p, 0:128 * (q + 1)], start=True, stop=True)
                elif br == "B":
                    hp, hh = divmod(q, 2)
                    rows = slice(64 * hh, 64 * hh + 64)
                    pe.matmul(S[:, 0:512], qbT[rows, 0, hp, p:T:4], kbT[rows, 0, hp, 0:T], start=True, stop=True)
                    pe.matmul(S[:, 512:640], qbT[rows, 1, hp, p:T:4], kbT[rows, 1, hp, p:T:4], start=True, stop=True)
                    last = pe.matmul(S[:, 640:768], qbT[rows, 2, hp, p:T:4], kbT[rows, 2, hp, p:T:4],
                                     start=True, stop=True)
                else:
                    for hh in range(2):
                        rows = slice(64 * hh, 64 * hh + 64)
                        last = pe.matmul(S[:, 512 * hh:512 * hh + 256], qmT[rows, q, 128 * p:128 * p + 128],
                                         kmT[rows, q, :], start=True, stop=True)
                last.then_inc(s_S, 1)

            def transposes(u):
                br, p, q = attn_slot(u)
                pe.wait_ge(s_cb, u + 1)
                pe.wait_ge(s_te, u)
                if u == OA_UNITS:
                    pe.wait_ge(s_sev, 3)
                if u > OA_UNITS:
                    pe.wait_ge(s_ob, pairs_through(u - 1))
                blocks = {"A": q + 1, "B": 6, "M": 4}[br]
                for k in range(blocks):
                    dst = pt_bank[:, 128 * k:128 * k + 128] if k < 4 else po_bank[:, 128 * k - 512:128 * k - 384]
                    last = pe.transpose(dst, sc[br][u % 3][:, 128 * k:128 * k + 128], ident[:, :])
                last.then_inc(s_T, 1)

            def values(u):
                br, p, q = attn_slot(u)
                pe.wait_ge(s_te, u + 1)
                P = pt[br][u % 2]
                if br == "A":
                    out = po_bank[:, 128 * q:128 * q + 128]
                    if q == 0 and p > 0:
                        pe.wait_ge(s_oe, p)
                    for k in range(q + 1):
                        last = pe.matmul(out, v_a[:, k, 128 * p:128 * p + 128], P[:, 128 * k:128 * k + 128],
                                         start=(k == 0), stop=(k == q))
                else:
                    v = u - OA_UNITS
                    pair = v // 2 if br == "B" else OB_UNITS // 2 + (v - OB_UNITS)
                    heads = [(q // 2, q % 2)] if br == "B" else [(q, 0), (q, 1)]
                    if pair and (br == "M" or q % 2 == 0):
                        pe.wait_ge(s_ob, pair)
                    for hp, hh in heads:
                        out = po_bank[64 * hh:64 * hh + 64, 256:384]
                        cols = slice(128 * hp + 64 * hh, 128 * hp + 64 * hh + 64)
                        if br == "B":
                            vs = [v_b[:, 0, k, cols] for k in range(4)] + [v_b[:, 1, p, cols], v_b[:, 2, p, cols]]
                            ks = range(6)
                        else:
                            vs = [vm[:, k, cols] for k in range(2)]
                            ks = [2 * hh, 2 * hh + 1]
                        for i, k in enumerate(ks):
                            last = pe.matmul(out, vs[i], P[:, 128 * k:128 * k + 128],
                                             start=(i == 0), stop=(i == len(vs) - 1))
                last.then_inc(s_pv, 1)

            def attention(which):
                a, b = RANGES[which]
                for s in range(a, b + 3):
                    if s < b:
                        scores(s)
                    if which == "BM" and s == a + 1:
                        samples_probs_b()
                    if which == "BM" and s >= a + 3:
                        sample_values(NK + s - a - 3)
                    if a <= s - 3:
                        values(s - 3)
                    if s - a in FILL[which]:
                        project_unit(*FILL[which][s - a])
                    if a <= s - 2 < b:
                        transposes(s - 2)

            sa = s_a.rearrange("p (t r) -> p t r", t=2)
            smt = s_m.rearrange("p (t r) -> p t r", t=2)

            def samples_rows_am():
                pe.wait_ge(s_kd, 2 * NS)
                pe.wait_ge(s_new, 2)
                pe.wait_ge(s_oa, 4)
                for t in range(2):
                    pe.transpose(pt_bank[0:64, 128 * t:128 * t + 128], sa[:, t, :], ident[:, :])
                pe.matmul(pt_bank[0:64, 256:257], pm_a, ones[:, 0:1], start=True, stop=True).then_inc(s_sT, 1)
                for t in range(2):
                    last = pe.transpose(po_bank[0:32, 128 * t:128 * t + 128], smt[:, t, :], ident[:, :])
                last.then_inc(s_sT, 1)

            def samples_probs_am():
                pe.wait_ge(s_sG, 2)
                out = pt_bank[:, 288:448]
                for t in range(2):
                    pe.matmul(out[:, 32 * t:32 * t + 32], e_a[:, 128 * t:128 * t + 128], g_a, start=True, stop=True)
                pe.matmul(out[:, 64:96], e_a[:, 256:257].to_broadcast([64, 128]), g_a, start=True, stop=True)
                for t in range(2):
                    last = pe.matmul(out[:, 96 + 32 * t:128 + 32 * t], e_m[:, 128 * t:128 * t + 128], g_m,
                                     start=True, stop=True)
                last.then_inc(s_saT, 1)

            def samples_rows_b():
                pe.wait_ge(s_kd, NK)
                pe.wait_ge(s_new, 4)
                pe.wait_ge(s_sev, 1)
                pe.transpose(po_bank[0:32, 0:128], s_1, ident[:, :])
                pe.transpose(po_bank[0:32, 128:208], s_23[0:80, :], ident[0:80, 0:80])
                for g in range(3):
                    last = pe.matmul(po_bank[0:32, 208 + g:209 + g], pm_b[:, 32 * g:32 * g + 32], ones[:, 0:1],
                                     start=True, stop=True)
                last.then_inc(s_sT, 1)

            def samples_probs_b():
                pe.wait_ge(s_sG, 3)
                out = po_bank[:, 256:416]
                pe.matmul(out[:, 0:32], e_b[:, 0:128], g_b, start=True, stop=True)
                for g in range(3):
                    pe.matmul(out[:, 32 + 32 * g:64 + 32 * g], e_b[:, 208 + g:209 + g].to_broadcast([32, 128]), g_b,
                              start=True, stop=True)
                pe.matmul(out[0:80, 128:160], e_b[:, 128:208], g_b, start=True, stop=True).then_inc(s_saT, 1)

            def sample_values(k):
                kind, b = RINGS[k]
                pe.wait_ge(s_kr[k % 2], KR[k])
                if k == NK:
                    pe.wait_ge(s_sev, 3)
                slot = ring[:, k % 2, :, :]
                for t in range(2):
                    cols = slice(256 * t + 32 * b, 256 * t + 32 * b + 32)
                    first, end = b == 0 and t == 0, b == NS - 1 and t == 1
                    if kind == "A":
                        last = pe.matmul(pj[1][0:32, 0:512], own_a[:, cols], slot[:, t, :], start=first, stop=end)
                    elif kind == "M":
                        last = pe.matmul(pj[1][64:96, 0:256], own_m[:, cols], slot[:, t, 0:256], start=first, stop=end)
                    else:
                        r = 128 if t == 0 else 80
                        last = pe.matmul(pj[1][64:96, 256:512], own_b[0:r, cols], slot[0:r, t, 0:256],
                                         start=first, stop=end)
                last.then_inc(s_spv, 1)

            def samples_outputs():
                pe.wait_ge(s_sov, 2)
                pe.wait_ge(s_pv, NU)
                for h in range(4):
                    last = pe.transpose(po_bank[:, 32 * h:32 * h + 32], ov_sa[:, 128 * h:128 * h + 128], ident[0:32, 0:32])
                last.then_inc(s_sot, 1)
                for c in range(4):
                    last = pe.transpose(pt_bank[:, 32 * c:32 * c + 32], ov_sb[:, 128 * c:128 * c + 128],
                                        ident[64:96, 64:96])
                last.then_inc(s_sot, 1)

            pe.wait_ge(s_ident, 16)
            pe.wait_ge(s_init, 5)
            for i in range(3):
                transpose_input(i)
            pe.wait_ge(s_xl, 4)
            project_chunk(0)
            transpose_input(3)
            transpose_input(4)
            project_chunk(1)
            transpose_input(5)
            transpose_input(6)
            pe.wait_ge(s_xl, 14)
            for n in range(2, N_A):
                project_chunk(n)
            pe.wait_ge(s_stage, J_A)
            pe.wait_ge(s_pc, PC[J_A])
            pe.wait_ge(s_ev, U0[N_A])
            attention("A")
            pe.wait_ge(s_bm, OA_UNITS)
            pe.wait_ge(s_te, OA_UNITS)
            for n in range(N_SECOND, N_BM):
                if n == N_SECOND + 1:
                    pe.wait_ge(s_const, 16 * 7)
                    for h in range(4):
                        pe.wait_ge(s_osq, h + 1)
                        last = pe.matmul(pt_bank[0:4, 0:512], sel_h[:, h, :], oraw_sq[h], start=(h == 0), stop=(h == 3))
                    last.then_inc(s_ov, 1)
                if n == N_SECOND + 3:
                    pe.wait_ge(s_orc, 1)
                    for h in range(4):
                        if h >= 2:
                            pe.wait_ge(s_oa, h - 1)
                        dst = (pt_bank, po_bank)[h % 2][:, 0:512]
                        pe.matmul(dst, row_h[:, h, :], rsq, start=True, stop=True).then_inc(s_obc, 1)
                if n == N_BM - 2:
                    samples_rows_am()
                if n == N_BM - 1:
                    samples_probs_am()
                project_chunk(n)
            pe.wait_ge(s_stage, NJ)
            pe.wait_ge(s_pc, PC[NJ])
            pe.wait_ge(s_ev, U0[N_BM])
            pe.wait_ge(s_km, NK)
            samples_rows_b()
            attention("BM")
            pe.wait_ge(s_bm, NU)
            pe.wait_ge(s_ex, NU)

            for m in range(4):
                for g in range(3):
                    if m == 0 and g < 2:
                        continue
                    for k in range(4):
                        project_unit(POS["in", 20 + 4 * g + m], k)
                        if m == 0 and k == 0:
                            samples_outputs()
                        if m == 0 and k == 1:
                            pe.wait_ge(s_so, 1)
                            pe.matmul(bank[3][:, 0:32], ones[:, :], sq_s, start=True, stop=True).then_inc(s_saT, 1)
                n = POS["proj", m]
                pe.wait_ge(s_lo, 2 * n + 2)
                for tile in range(2):
                    for hf in range(2):
                        i = 4 * m + 2 * tile + hf
                        a, b = HALF * hf, HALF * hf + HALF
                        if i >= 2:
                            pe.wait_ge(s_mx, i - 1)
                        else:
                            pe.wait_ge(s_ol, 2 + i)
                        for br, kts in enumerate(((0, 1, 2, 3), (4, 5), (6, 7))):
                            last = product(bank[3 * (i % 2) + br][:, 0:HALF],
                                           [(n % 2, kt, 128 * tile, 128, kt, a, b) for kt in kts], oh, ol)
                        last.then_inc(s_pp, 1)
            pe.wait_ge(s_ev, U0[-1])
            for m in range(4):
                n = N_OUT + m
                pe.wait_ge(s_lo, 2 * n + 2)
                for t in range(5):
                    i = 5 * m + t
                    rows = rows_of(t)
                    if i >= 2:
                        pe.wait_ge(s_y, i - 1)
                    out = pj[i % 2][0:rows, 0:CW]
                    for kt in range(KT):
                        if m == 0 and t < 3:
                            pe.wait_ge(s_ml, 2 * kt + (1 if t < 2 else 2))
                        mh = mixh[:, kt, 128 * t:128 * t + rows]
                        ml = mixl[:, kt, 128 * t:128 * t + rows]
                        pe.matmul(out, mh, w_hi[:, n % 2, kt, :], start=(kt == 0), stop=False)
                        pe.matmul(out, ml, w_hi[:, n % 2, kt, :], start=False, stop=False)
                        last = pe.matmul(out, mh, w_lo[:, n % 2, kt, :], start=False, stop=(kt == KT - 1))
                    last.then_inc(s_po, 1)

        def wait_chunk_used(eng, n):
            kind, j = SEQ[n]
            if kind == "proj":
                eng.wait_ge(s_pp, 4 * (j + 1))
            elif kind == "out":
                eng.wait_ge(s_po, 5 * (j + 1))
            else:
                eng.wait_ge(s_pj, U0[n + 1])

        @block.scalar
        def _(act):
            def hi_split(n, halves=(0, 1)):
                if n >= len(SEQ):
                    return
                if n >= 2:
                    wait_chunk_used(act, n - 2)
                for s in halves:
                    m = 2 * n + s
                    act.wait_ge(s_raw[m % 3], RAW_AT[m])
                    act.activation(w_hi[:, n % 2, 4 * s:4 * s + 4, :], w_raw[:, m % 3, :, :], ACT.Copy).then_inc(s_hi, 1)

            def evac_dest(key, tile, a, b):
                kind, j = key
                if kind == "mem":
                    return kmT[:, tile, a:b] if j == 0 else vT[:, 2 + tile, a:b]
                c = 2 * j + tile
                if j < 2:
                    return qaT[:, c, a:b]
                if j < 4:
                    return kaT[:, c - 4, a:b]
                if j < 6:
                    return vT[:, c - 8, a:b]
                if j < 8:
                    return oz[:, c - 12, a:b]
                if j < 17:
                    g, r = divmod(j - 8, 3)
                    if r == 2:
                        return vT[:, (2 * g) % 4 + tile, a:b]
                    return (qbT, kbT)[r][:, g, tile, a:b]
                if j == 17:
                    return oz[:, 4 + tile, a:b]
                if j == 18:
                    return qmT[:, tile, a:b]
                if j == 19:
                    return oz[:, 6 + tile, a:b]
                return gate[:, (j - 20) // 4, tile, a:b]

            def evacuate_unit(n, k):
                key = SEQ[n]
                kind, j = key
                if N_A <= n < N_SECOND or N_BM <= n < N_THIRD:
                    func = ACT.Copy
                elif kind == "in" and j >= 20:
                    func = ACT.Sigmoid
                elif kind == "in" and j in (6, 7, 17, 19):
                    func = ACT.Silu
                else:
                    func = ACT.Copy
                if k == 0:
                    if key in V_GUARD:
                        act.wait_ge(s_nat, V_GUARD[key])
                    if key == ("in", 10):
                        act.wait_ge(s_oa, 4)
                    if key == ("in", 8):
                        act.wait_ge(s_new, 2)
                        act.wait_ge(s_nat, J_QA)
                    if key == ("in", 20):
                        act.wait_ge(s_kd, NK)
                        act.wait_ge(s_qb, NK)
                        for i in range(2):
                            act.wait_ge(s_out[i], OUTC[i])
                tile, (a, b) = (k, (0, NMEM)) if kind == "mem" else (k // 2, ((0, HALF), (HALF, TT))[k % 2])
                u = U0[n] + k
                act.wait_ge(s_pj, u + 1)
                if kind == "in" and j >= 20 and (j - 20) % 4:
                    act.wait_ge(s_mx, 4 * ((j - 21) % 4) + 2 * tile + (1 if a else 0) + 1)
                act.activation(evac_dest(key, tile, a, b), pj_of(u)[:, 0:b - a], func).then_inc(s_ev, 1)
                if kind == "in" and a and (j in (4, 5) or j in (10, 13, 16)):
                    if j < 6:
                        dst = vn_a[:, 8 * (2 * j - 8 + tile):8 * (2 * j - 8 + tile) + 8]
                    else:
                        g = (j - 10) // 3
                        dst = vn_b[:, 16 * g + 8 * tile:16 * g + 8 * tile + 8]
                    act.wait_ge(s_ev, u + 1)
                    act.activation(dst, evac_dest(key, tile, 512, TT), ACT.Copy).then_inc(s_vn, 1)

            def evacuate(n):
                for k in range(units_of(SEQ[n][0])):
                    evacuate_unit(n, k)

            def exps(u):
                br, p, q = attn_slot(u)
                act.wait_ge(s_nm, u + 1)
                k4 = 2 * (u % 4)
                buf = sc[br][u % 3]
                if br == "A":
                    kn = 128 * (q + 1)
                    act.activation(buf[:, 0:kn], buf[:, 0:kn], ACT.Exp, bias=nm[:, k4:k4 + 1],
                                   accum_out=sm[:, k4:k4 + 1])
                    act.activation(buf[:, 512:512 + kn], buf[:, 512:512 + kn], ACT.Exp, bias=nm[:, k4 + 1:k4 + 2],
                                   accum_out=sm[:, k4 + 1:k4 + 2]).then_inc(s_ex, 1)
                elif br == "B":
                    act.activation(buf[:, 0:768], buf[:, 0:768], ACT.Exp, bias=nm[:, k4:k4 + 1],
                                   accum_out=sm[:, k4:k4 + 1]).then_inc(s_ex, 1)
                else:
                    for hh in range(2):
                        last = act.activation(buf[:, 256 * hh:256 * hh + 256], ps[u % 2][:, 512 * hh:512 * hh + 256],
                                              ACT.Exp, bias=nm[:, k4 + hh:k4 + hh + 1], scale=SCALE,
                                              accum_out=sm[:, k4 + hh:k4 + hh + 1])
                    last.then_inc(s_ex, 1)

            def copy_probs(u):
                br, p, q = attn_slot(u)
                act.wait_ge(s_T, u + 1)
                if u >= 2:
                    act.wait_ge(s_pv, u - 1)
                P = pt[br][u % 2]
                if br == "B":
                    act.activation(P[:, 0:512], pt_bank[:, :], ACT.Copy)
                    act.activation(P[:, 512:768], po_bank[:, 0:256], ACT.Copy).then_inc(s_te, 1)
                else:
                    w = 128 * (q + 1) if br == "A" else 512
                    act.activation(P[:, 0:w], pt_bank[:, 0:w], ACT.Copy).then_inc(s_te, 1)

            def attention(which):
                a, b = RANGES[which]
                for s in range(a, b + 4):
                    v = s - 4
                    if which == "A" and a <= v < b and attn_slot(v)[2] == QT - 1:
                        h = attn_slot(v)[1]
                        act.wait_ge(s_pv, v + 1)
                        act.activation(oraw[:, h, 0:T], po_bank[:, :], ACT.Copy).then_inc(s_oe, 1)
                    fill = FILL[which].get(s - a)
                    if a <= s - 2 < b and not fill:
                        copy_probs(s - 2)
                    if which == "BM" and s == a:
                        samples_exp_b()
                    if s < b:
                        exps(s)
                    if fill:
                        evacuate_unit(*fill)
                        if a <= s - 2 < b:
                            copy_probs(s - 2)
                    for n, half in SPLIT[which].get(s - a, ()):
                        hi_split(n, (half,))

            def samples_exp_am():
                act.wait_ge(s_snm, 1)
                act.activation(e_a, e_a, ACT.Exp, bias=snm[0:64, 0:1], accum_out=ssm[0:64, 0:1]).then_inc(s_sex, 1)
                act.wait_ge(s_snm, 2)
                act.activation(e_m, po_bank[0:32, 0:256], ACT.Exp, bias=snm[0:32, 1:2], scale=SCALE,
                               accum_out=ssm[0:32, 1:2]).then_inc(s_sex, 1)

            def samples_exp_b():
                act.wait_ge(s_snm, 3)
                act.activation(e_b, e_b, ACT.Exp, bias=snm[0:32, 2:3], accum_out=ssm[0:32, 2:3]).then_inc(s_sex, 1)

            act.wait_ge(s_init, 5)
            for i in range(9):
                if i < 7:
                    t = XORDER[i]
                    r = rows_of(t)
                    act.wait_ge(s_xin[t], 16)
                    if i:
                        act.wait_ge(s_sq, i)
                    act.activation(prod[0:r, :], xin[t][0:r, :], ACT.Square,
                                   accum_out=ssq[0:r, t:t + 1]).then_inc(s_sq, 1)
                    act.wait_ge(s_sq, i + 1)
                    act.activation(rstd[0:r, t:t + 1], ssq[0:r, t:t + 1], ACT.Sqrt, scale=1.0 / D,
                                   bias=eps[0:r, :]).then_inc(s_std, 1)
                if i == 2:
                    hi_split(0)
                if i >= 2:
                    t = XORDER[i - 2]
                    for kg in range(2):
                        g = 2 * (i - 2) + kg
                        act.wait_ge(s_xt, g + 1)
                        src = bank[g % 4].rearrange("p (c t) -> p c t", c=4)[:, :, 0:rows_of(t)]
                        act.activation(x_dst(xh, memh, t, kg), src, ACT.Copy).then_inc(s_xh, 1)
                if i == 4:
                    hi_split(1)
                if i == 5:
                    evacuate(0)
            hi_split(2)
            act.wait_ge(s_lsum, 1)
            act.activation(lamv[:, 2:4], lamv[:, 0:2], ACT.Exp).then_inc(s_lexp, 1)
            for n in range(1, N_A):
                evacuate(n)
                hi_split(n + 2)
            act.wait_ge(s_nat, J_A)
            attention("A")
            act.wait_ge(s_oe, 4)
            for h in range(4):
                act.activation(oraw_sq[h], oraw[:, h, 0:T], ACT.Square).then_inc(s_osq, 1)
            for n in range(N_SECOND, N_BM):
                for k in range(4):
                    evacuate_unit(n, k)
                    if n == N_BM - 2 and k == 1:
                        samples_exp_am()
                hi_split(n + 2)
                if n == N_SECOND:
                    act.wait_ge(s_ev, U0[N_SECOND])
                    act.activation(oz[:, 0:6, :], oz[:, 0:6, :], ACT.Silu).then_inc(s_silu, 1)
                if n == N_SECOND + 1:
                    act.wait_ge(s_ov, 1)
                    act.activation(rsq, pt_bank[0:4, 0:512], ACT.Sqrt, bias=eps[0:4, :]).then_inc(s_ostd, 1)
            attention("BM")

            evacuate_unit(N_THIRD, 0)
            act.wait_ge(s_ob, OB_UNITS // 2 + OM_UNITS)
            act.wait_ge(s_spv, 3 * NS)
            for i in range(2):
                act.activation(oh[:, 4 * i:4 * i + 4, 0:T], oz[:, 4 * i:4 * i + 4, 0:T], ACT.Copy).then_inc(s_oh, 1)
                evacuate_unit(N_THIRD, 1 + i)
            evacuate_unit(N_THIRD, 3)
            act.wait_ge(s_saT, 3)
            act.activation(r_s, bank[3][:, 0:32], ACT.Sqrt, scale=1.0 / 128, bias=eps[:, :]).then_inc(s_sex, 1)
            act.wait_ge(s_so, 2)
            act.activation(oh[:, :, T:TT], oz[:, :, T:TT], ACT.Copy).then_inc(s_oh, 1)
            act.activation(gate[:, 0:2, :, :], gate[:, 0:2, :, :], ACT.Sigmoid).then_inc(s_sig, 1)
            hi_split(N_THIRD + 2)
            for m in range(4):
                for g in range(3 if m else 0):
                    n = POS["in", 20 + 4 * g + m]
                    evacuate(n)
                    hi_split(n + 2)
                for i in range(4 * m, 4 * m + 4):
                    c, hf = divmod(i, 2)
                    act.wait_ge(s_mix, i + 1)
                    act.activation(mixh[:, c, HALF * hf:HALF * hf + HALF], mix_t[:, i % 2, 0, :], ACT.Copy).then_inc(s_mh, 1)
                hi_split(POS["proj", m] + 2)
            for m in range(4):
                hi_split(N_OUT + m + 2)
            for t in range(5):
                r = rows_of(t)
                act.wait_ge(s_y, 15 + t + 1)
                if t:
                    act.wait_ge(s_ysq, t)
                act.activation(gate[0:r, 0:2, :, 0:256].rearrange("p a b c -> p (a b) c"),
                               y_nat[0:r, t, :].rearrange("p (a c) -> p a c", c=256), ACT.Square,
                               accum_out=ssq[0:r, 8 + t:9 + t]).then_inc(s_ysq, 1)
                act.wait_ge(s_ysq, t + 1)
                act.activation(rstd[0:r, 8 + t:9 + t], ssq[0:r, 8 + t:9 + t], ACT.Sqrt, scale=1.0 / D,
                               bias=eps[0:r, :]).then_inc(s_ystd, 1)

        @block.vector
        def _(dve):
            own = [0]

            def link(ins):
                own[0] += 1
                ins.then_inc(s_dv, 1)
                dve.wait_ge(s_dv, own[0])

            def lo_split(n, halves=(0, 1)):
                if n >= len(SEQ):
                    return
                for s in halves:
                    m = 2 * n + s
                    dve.wait_ge(s_hi, m + 1)
                    dve.tensor_tensor(w_lo[:, n % 2, 4 * s:4 * s + 4, :], w_raw[:, m % 3, :, :],
                                      w_hi[:, n % 2, 4 * s:4 * s + 4, :].bitcast(f32), ALU.subtract).then_inc(s_lo, 1)

            def split_x(i):
                t = XORDER[i]
                for kg in range(2):
                    g = 2 * i + kg
                    dve.wait_ge(s_xh, g + 1)
                    src = bank[g % 4].rearrange("p (c t) -> p c t", c=4)[:, :, 0:rows_of(t)]
                    dve.tensor_tensor(x_dst(xl, meml, t, kg), src, x_dst(xh, memh, t, kg).bitcast(f32),
                                      ALU.subtract).then_inc(s_xl, 1)

            for i in range(9):
                if i < 7:
                    t = XORDER[i]
                    r = rows_of(t)
                    dve.wait_ge(s_std, i + 1)
                    link(dve.reciprocal(rstd[0:r, t:t + 1], rstd[0:r, t:t + 1]))
                    dve.wait_ge(s_gain[t // 5], 16)
                    dve.scalar_tensor_tensor(xin[t][0:r, :], xin[t][0:r, :], rstd[0:r, t:t + 1],
                                             (g_row if t < 5 else g_row_m)[0:r, :], ALU.mult,
                                             ALU.mult).then_inc(s_xn, 1)
                if i >= 2:
                    split_x(i - 2)
                if i == 2:
                    lo_split(0)
                if i == 4:
                    lo_split(1)
            dve.wait_ge(s_const, 16 * 7)
            for i in range(2):
                link(dve.tensor_tensor(s_a[:, 64 * i:64 * i + 64], lam_in[:, 128 * i:128 * i + 64],
                                       lam_in[:, 128 * i + 64:128 * i + 128], ALU.mult))
            dve.tensor_reduce(lamv[:, 0:2], s_a.rearrange("p (i d) -> p i d", i=2), AXX, ALU.add).then_inc(s_lsum, 1)
            dve.tensor_scalar(gs[:, 1:2], gs[:, 0:1], 1.0 - LAM_INIT, None, ALU.mult)
            lo_split(2)
            dve.wait_ge(s_lexp, 1)
            link(dve.tensor_tensor(lamv[:, 4:5], lamv[:, 3:4], lamv[:, 2:3], ALU.subtract))
            link(dve.tensor_scalar(lamv[:, 5:6], lamv[:, 4:5], -LAM_INIT, None, ALU.add))

            def stage_job(J):
                _, rows, srcs, _, _ = JOBS[J]
                dve.wait_ge(s_nat, J + 1)
                if J >= 2:
                    dve.wait_ge(s_out[J % 2], OUT_AT[J - 2])
                    dve.wait_ge(s_pc, PC[J - 1])
                w = 128 * len(srcs)
                dve.tensor_copy(stage[0:rows, J % 2, 0:w], bank[J % 2][0:rows, 0:w]).then_inc(s_stage, 1)

            def sample_scores(k):
                kind, b = RINGS[k]
                dve.wait_ge(s_kr[k % 2], KR[k])
                dve.wait_ge(s_qb, k + 1)
                if k:
                    dve.wait_ge(s_kd, k)
                slot = ring[:, k % 2, :, :]
                q = bank[2 + k % 2]
                if kind == "A":
                    dve.tensor_tensor(prod.rearrange("p (t c) -> p t c", t=2), slot,
                                      q.unsqueeze(1).to_broadcast([128, 2, 512]), ALU.mult).then_inc(s_km, 1)
                    dve.wait_ge(s_km, k + 1)
                    dve.tensor_reduce(s_a.rearrange("p (t c h b) -> p b t h c", t=2, c=2, h=4)[:, b],
                                      prod.rearrange("p (t h c d) -> p t h c d", t=2, h=4, c=2), AXX,
                                      ALU.add).then_inc(s_kd, 1)
                elif kind == "M":
                    dve.tensor_tensor(prod[:, 0:512].rearrange("p (t c) -> p t c", t=2), slot[:, :, 0:256],
                                      q[:, 0:256].unsqueeze(1).to_broadcast([128, 2, 256]), ALU.mult).then_inc(s_km, 1)
                    dve.wait_ge(s_km, k + 1)
                    dve.tensor_reduce(s_m.rearrange("p (t h b) -> p b t h", t=2, h=4)[:, b],
                                      prod[:, 0:512].rearrange("p (t h d) -> p t h d", t=2, h=4), AXX,
                                      ALU.add).then_inc(s_kd, 1)
                else:
                    dve.tensor_tensor(prod[:, 0:256], slot[:, 0, 0:256], q[:, 0:256], ALU.mult)
                    dve.tensor_tensor(prod[0:80, 256:512], slot[0:80, 1, 0:256], q[0:80, 256:512],
                                      ALU.mult).then_inc(s_km, 1)
                    dve.wait_ge(s_km, k + 1)
                    dve.tensor_reduce(s_1.rearrange("p (h b) -> p b h", h=4)[:, b],
                                      prod[:, 0:256].rearrange("p (h d) -> p h d", h=4), AXX, ALU.add)
                    dve.tensor_reduce(s_23[0:80, :].rearrange("p (h b) -> p b h", h=4)[:, b],
                                      prod[0:80, 256:512].rearrange("p (h d) -> p h d", h=4), AXX,
                                      ALU.add).then_inc(s_kd, 1)

            LOWEST = -3.0e38

            def biased_max(u):
                br, p, q = attn_slot(u)
                dve.wait_ge(s_S, u + 1)
                if u >= 3:
                    dve.wait_ge(s_T, u - 2)
                buf, S, k4 = sc[br][u % 3], ps[u % 2], 2 * (u % 4)
                if br == "A":
                    kn = 128 * (q + 1)
                    for c in range(2):
                        last = dve.tensor_tensor_reduce(
                            out=buf[:, 512 * c:512 * c + kn], in0=S[:, 512 * c:512 * c + kn],
                            in1=bias_a[:, p, 512 - kn:512], scale=SCALE, scalar=LOWEST, op0=ALU.add, op1=ALU.max,
                            accum_out=mx[:, k4 + c:k4 + c + 1])
                    last.then_inc(s_bm, 1)
                    n, f = 2, -1.0
                elif br == "B":
                    link(dve.tensor_tensor_reduce(
                        out=buf[:, 0:512], in0=S[:, 0:512], in1=bias_b[:, q, 3 - p:515 - p], scale=SCALE,
                        scalar=LOWEST, op0=ALU.add, op1=ALU.max, accum_out=mx[:, k4 + 1:k4 + 2]))
                    dve.tensor_tensor_reduce(
                        out=buf[:, 512:768], in0=S[:, 512:768], in1=bias_b[:, q, 515:771], scale=SCALE,
                        scalar=mx[:, k4 + 1:k4 + 2], op0=ALU.add, op1=ALU.max,
                        accum_out=mx[:, k4:k4 + 1]).then_inc(s_bm, 1)
                    n, f = 1, -1.0
                else:
                    dve.tensor_reduce(mx[:, k4:k4 + 2], S[:, :].rearrange("p (h c) -> p h c", h=2)[:, :, 0:256], AXX,
                                      ALU.max).then_inc(s_bm, 1)
                    n, f = 2, -SCALE
                dve.wait_ge(s_bm, u + 1)
                dve.tensor_scalar(nm[:, k4:k4 + n], mx[:, k4:k4 + n], f, None, ALU.mult).then_inc(s_nm, 1)

            def normalise(u):
                br, p, q = attn_slot(u)
                buf, k4 = sc[br][u % 3], 2 * (u % 4)
                n = 1 if br == "B" else 2
                dve.wait_ge(s_ex, u + 1)
                link(dve.reciprocal(rs[:, k4:k4 + n], sm[:, k4:k4 + n]))
                if br == "A":
                    kn = 128 * (q + 1)
                    link(dve.tensor_scalar(buf[:, 512:512 + kn], buf[:, 512:512 + kn], rs[:, k4 + 1:k4 + 2],
                                           lamv[:, 5:6], ALU.mult, ALU.mult))
                    dve.scalar_tensor_tensor(buf[:, 0:kn], buf[:, 0:kn], rs[:, k4:k4 + 1], buf[:, 512:512 + kn],
                                             ALU.mult, ALU.add).then_inc(s_cb, 1)
                elif br == "B":
                    dve.tensor_scalar(buf[:, 0:768], buf[:, 0:768], rs[:, k4:k4 + 1], None, ALU.mult).then_inc(s_cb, 1)
                else:
                    for hh in range(2):
                        w = buf[:, 256 * hh:256 * hh + 256]
                        last = dve.tensor_scalar(w, w, rs[:, k4 + hh:k4 + hh + 1], None, ALU.mult)
                    last.then_inc(s_cb, 1)

            def gate_output(u):
                br, p, q = attn_slot(u)
                if br == "A" or (br == "B" and q % 2 == 0):
                    return
                v = u - OA_UNITS
                pair = v // 2 if br == "B" else OB_UNITS // 2 + (v - OB_UNITS)
                dve.wait_ge(s_pv, u + 1)
                z = oz[:, 4 + q // 2, p:T:4] if br == "B" else oz[:, 6 + q, 128 * p:128 * p + 128]
                dve.tensor_tensor(z, po_bank[:, 256:384], z, ALU.mult).then_inc(s_ob, 1)

            def attention(which):
                a, b = RANGES[which]
                for s in range(a, b + 3):
                    if s < b:
                        biased_max(s)
                    if a <= s - 3:
                        gate_output(s - 3)
                    if which == "BM" and s == a:
                        samples_norm(2, g_b)
                    if a <= s - 1 < b:
                        normalise(s - 1)
                    if which == "BM" and s == a + 1:
                        dve.wait_ge(s_saT, 2)
                        dve.tensor_copy(aT[:, 192:288], po_bank[:, 288:384]).then_inc(s_sev, 1)
                        dve.wait_ge(s_own, 3)
                        own_columns(swork, 0, 0, po_bank[:, 256:288])
                        own_columns(swork, 0, 1, po_bank[:, 384:416], 80).then_inc(s_sev, 1)
                    for n, half in SPLIT[which].get(s - a, ()):
                        lo_split(n, (half,))

            def samples_max(i, e, scores_, bias, rows):
                m1 = smx[0:rows, i:i + 1]
                if bias is None:
                    link(dve.tensor_reduce(m1, scores_, AXX, ALU.max))
                else:
                    link(dve.tensor_tensor_reduce(out=e, in0=scores_, in1=bias, scale=SCALE, scalar=LOWEST,
                                                  op0=ALU.add, op1=ALU.max, accum_out=m1))
                dve.tensor_scalar(snm[0:rows, i:i + 1], m1, -1.0 if bias is not None else -SCALE, None,
                                  ALU.mult).then_inc(s_snm, 1)

            def own_columns(buf, at, t, src, rows=128):
                w = buf[0:rows, at + 256 * t:at + 256 * t + 264]
                return dve.tensor_copy(w.rearrange("p (b x) -> p b x", x=33)[:, :, 0:32:8],
                                       src[0:rows, :].rearrange("p (h b) -> p b h", h=4))

            def samples_norm(i, g):
                dve.wait_ge(s_sex, i + 1)
                link(dve.reciprocal(srs[0:32, i:i + 1], ssm[0:32, i:i + 1]))
                dve.tensor_scalar(g, ident[0:32, 0:32], srs[0:32, i:i + 1], None, ALU.mult).then_inc(s_sG, 1)

            def run_beside(n):
                for what, i in beside(n):
                    (stage_job if what == "job" else sample_scores)(i)

            for n in range(1, N_A):
                run_beside(n)
                lo_split(n + 2)
            dve.wait_ge(s_ev, ev_of(("in", 1)))
            for c in range(2):
                r = slice(64 * c, 64 * c + 64)
                dve.tensor_tensor(pm_a[r, 32 * c:32 * c + 32].rearrange("p (h b) -> p h b", h=4),
                                  qaT[r, :, T:TT], kaT[r, :, T:TT], ALU.mult).then_inc(s_new, 1)
            dve.wait_ge(s_biasa, 16)
            attention("A")
            for n in range(N_SECOND, N_BM):
                if n == N_SECOND + 3:
                    for h in range(4):
                        dve.wait_ge(s_obc, h + 1)
                        dve.wait_ge(s_silu, 1)
                        link(dve.scalar_tensor_tensor(oraw[:, h, 0:T], oraw[:, h, 0:T], gs[:, 1:2],
                                                      (pt_bank, po_bank)[h % 2][:, 0:512], ALU.mult, ALU.mult))
                        dve.tensor_tensor(oz[:, h, 0:T], oz[:, h, 0:T], oraw[:, h, 0:T], ALU.mult).then_inc(s_oa, 1)
                if n == N_BM - 1:
                    dve.wait_ge(s_saT, 1)
                    dve.wait_ge(s_own, 2)
                    dve.tensor_copy(aT[:, 64:96], pt_bank[:, 352:384])
                    for t in range(2):
                        own_columns(region, 7280, t, pt_bank[:, 288 + 32 * t:320 + 32 * t])
                    own_columns(region, 7792, 0, pt_bank[:, 384:416])
                    own_columns(region, 7792, 1, pt_bank[:, 416:448]).then_inc(s_sev, 1)
                if n == N_BM - 2:
                    dve.wait_ge(s_sbl[0], 16)
                    dve.wait_ge(s_sT, 1)
                    samples_max(0, e_a, pt_bank[0:64, 0:W_A], bias_sa, 64)
                    dve.wait_ge(s_sT, 2)
                    samples_max(1, e_m, po_bank[0:32, 0:256], None, 32)
                run_beside(n)
                lo_split(n + 2)
                if n == N_BM - 3:
                    dve.memset(own_a, 0.0).then_inc(s_own, 1)
                    dve.memset(own_m, 0.0).then_inc(s_own, 1)
                if n == N_SECOND + 1:
                    dve.wait_ge(s_ostd, 1)
                    dve.reciprocal(rsq, rsq).then_inc(s_orc, 1)
                if n == N_BM - 2:
                    dve.wait_ge(s_sex, 1)
                    link(dve.reciprocal(srs[0:64, 0:1], ssm[0:64, 0:1]))
                    dve.tensor_scalar(g_a[0:32, :], ident[0:32, 0:32], srs[0:32, 0:1], None, ALU.mult)
                    dve.tensor_scalar(g_a[32:64, :], ident[32:64, 32:64], srs[32:64, 0:1], lamv[32:64, 5:6],
                                      ALU.mult, ALU.mult).then_inc(s_sG, 1)
                    samples_norm(1, g_m)
            for hh in range(2):
                r = slice(64 * hh, 64 * hh + 64)
                dve.tensor_tensor(pm_b[r, :].rearrange("p (g k h b) -> p g k h b", g=3, k=2, h=2)[:, :, :, hh, :],
                                  qbT[r, :, :, T:TT], kbT[r, :, :, T:TT], ALU.mult).then_inc(s_new, 1)
            dve.wait_ge(s_sbl[1], 16)
            dve.wait_ge(s_sT, 3)
            samples_max(2, e_b, po_bank[0:32, 0:W_B], bias_sb, 32)
            dve.memset(own_b, 0.0).then_inc(s_own, 1)
            dve.wait_ge(s_biasb, 16)
            attention("BM")

            def split_outputs(i):
                dve.wait_ge(s_oh, i + 1)
                dve.tensor_tensor(ol[:, 4 * i:4 * i + 4, 0:T], oz[:, 4 * i:4 * i + 4, 0:T],
                                  oh[:, 4 * i:4 * i + 4, 0:T].bitcast(f32), ALU.subtract).then_inc(s_ol, 1)

            dve.wait_ge(s_spv, 3 * NS)
            dve.tensor_copy(ov_sa, pj[1][0:32, :]).then_inc(s_sov, 1)
            dve.tensor_copy(ov_sb, pj[1][64:96, :]).then_inc(s_sov, 1)
            link(dve.tensor_tensor(t_a, vn_a, aT[:, 64:96], ALU.mult))
            for hh in range(2):
                r = slice(64 * hh, 64 * hh + 64)
                link(dve.tensor_tensor(t_b[r, :].rearrange("p (g k b) -> p g k b", g=3, k=2),
                                       aT[r, 192:288].rearrange("p (g k h b) -> p g k h b", g=3, k=2, h=2)[:, :, :, hh, :],
                                       vn_b[r, :].rearrange("p (g k b) -> p g k b", g=3, k=2), ALU.mult))
            link(dve.tensor_reduce(t_b2[:, 0:16], t_b.rearrange("p (g x) -> p x g", g=3), AXX, ALU.add))
            dve.wait_ge(s_sot, 1)
            link(dve.tensor_tensor(o_as.rearrange("p (h b) -> p h b", h=4),
                                   po_bank[:, 0:160].rearrange("p (h x) -> p h x", x=40)[:, :, 0:8],
                                   t_a.rearrange("p (h b) -> p h b", h=4), ALU.add))
            dve.tensor_tensor(sq_s, o_as, o_as, ALU.mult).then_inc(s_so, 1)
            split_outputs(0)
            dve.wait_ge(s_sot, 2)
            for hh in range(2):
                r = slice(64 * hh, 64 * hh + 64)

                def heads(c):
                    return pt_bank[r, c:c + 96].rearrange("p (k x) -> p k x", x=48)[:, :, 8 * hh:8 * hh + 8]
                z = oz[r, 6:8, T:TT]
                dve.tensor_tensor(z, heads(0), z, ALU.mult)
                w = t_b2[r, 0:16].rearrange("p (k b) -> p k b", k=2)
                link(dve.tensor_tensor(w, heads(64), w, ALU.add))
            z = oz[:, 4:6, T:TT]
            dve.tensor_tensor(z, z, t_b2[:, 0:16].rearrange("p (k b) -> p k b", k=2), ALU.mult)
            split_outputs(1)
            dve.wait_ge(s_sex, 4)
            link(dve.reciprocal(r_s, r_s))
            link(dve.scalar_tensor_tensor(t_a, o_as, gs[:, 1:2], r_s, ALU.mult, ALU.mult))
            z = oz[:, 0:4, T:TT]
            dve.tensor_tensor(z, z, t_a.rearrange("p (h b) -> p h b", h=4), ALU.mult).then_inc(s_so, 1)
            dve.wait_ge(s_oh, 3)
            dve.tensor_tensor(ol[:, :, T:TT], oz[:, :, T:TT], oh[:, :, T:TT].bitcast(f32), ALU.subtract).then_inc(s_ol, 1)
            lo_split(N_THIRD + 2)

            def mixed_lo(i):
                c, hf = divmod(i, 2)
                dve.wait_ge(s_mh, i + 1)
                cols = slice(HALF * hf, HALF * hf + HALF)
                dve.tensor_tensor(mixl[:, c, cols], mix_t[:, i % 2, 0, :], mixh[:, c, cols].bitcast(f32),
                                  ALU.subtract).then_inc(s_ml, 1)

            for m in range(4):
                for g in range(3 if m else 0):
                    lo_split(POS["in", 20 + 4 * g + m] + 2)
                dve.wait_ge(s_ev, ev_of(("in", 28 + m)))
                if m == 0:
                    dve.wait_ge(s_sig, 1)
                for i in range(4 * m, 4 * m + 4):
                    tile, hf = (i // 2) % 2, i % 2
                    cols = slice(HALF * hf, HALF * hf + HALF)
                    dve.wait_ge(s_pp, i + 1)
                    if i >= 2:
                        dve.wait_ge(s_ml, i - 1)
                    for br in range(3):
                        last = dve.tensor_tensor(mix_t[:, i % 2, br, :], bank[3 * (i % 2) + br][:, 0:HALF],
                                                 gate[:, br, tile, cols], ALU.mult)
                    last.then_inc(s_mx, 1)
                    dve.wait_ge(s_mx, i + 1)
                    t0 = mix_t[:, i % 2, 0, :]
                    link(dve.tensor_tensor(t0, t0, mix_t[:, i % 2, 1, :], ALU.add))
                    dve.tensor_tensor(t0, t0, mix_t[:, i % 2, 2, :], ALU.add).then_inc(s_mix, 1)
                    if i % 4:
                        mixed_lo(i - 1)
                mixed_lo(4 * m + 3)
                lo_split(POS["proj", m] + 2)
            dve.wait_ge(s_yl, 80)
            for m in range(4):
                for t in range(5):
                    i = 5 * m + t
                    r = rows_of(t)
                    dve.wait_ge(s_po, i + 1)
                    y = y_nat[0:r, t, CW * m:CW * m + CW]
                    dve.tensor_tensor(y, pj[i % 2][0:r, 0:CW], y, ALU.add).then_inc(s_y, 1)
                lo_split(N_OUT + m + 2)
            dve.wait_ge(s_gf, 16)
            for t in range(5):
                r = rows_of(t)
                dve.wait_ge(s_ystd, t + 1)
                link(dve.reciprocal(rstd[0:r, 8 + t:9 + t], rstd[0:r, 8 + t:9 + t]))
                dve.scalar_tensor_tensor(y_nat[0:r, t, :], y_nat[0:r, t, :], rstd[0:r, 8 + t:9 + t],
                                         g_fin[0:r, :], ALU.mult, ALU.mult).then_inc(s_yo, 1)


def constants():
    f = np.float32
    slope = [2.0 ** (-2.0 * (h + 1)) for h in range(4)]
    neg = -1e30 / SCALE

    def bias(dist, ok, h):
        return np.where(ok, -slope[h] * dist / SCALE, neg)

    p = np.arange(128)[:, None]
    y = np.arange(512)[None, :] - 384
    bias_a = np.stack([bias(p - y, p >= y, h) for h in range(4)], 1)
    d1 = 4 * p - (np.arange(515)[None, :] - 3)
    d2 = 4 * (p - np.arange(128)[None, :])
    bias_b = np.stack([np.concatenate([bias(d1, (d1 >= 0) & (d1 <= 128), h), bias(d2, d2 >= 0, h),
                                       bias(d2, (d2 >= 0) & (d2 % 16 == 0), h)], 1) for h in range(4)], 1)
    rows = np.arange(64)
    ha = (rows // 8) % 4
    bias_sa = np.stack([bias(256 - np.arange(W_A), np.ones(W_A, bool), h) for h in ha])
    cached = [d * (n - np.arange(n)) for n, d in zip(G_ROWS, DIL)]
    dist_b = np.concatenate(cached + [np.zeros(3)])
    bias_sb = np.stack([bias(dist_b, np.ones(W_B, bool), h) for h in ha[:32]])
    sel = np.zeros((128, 4, 4))
    row = np.zeros((4, 4, 128))
    for h in range(4):
        sel[:, h, h] = 1.0 / 128
        row[h, h, :] = 1.0
    return {"c_ident": np.eye(128, dtype=f), "c_bias_a": bias_a.astype(f), "c_bias_b": bias_b.astype(f),
            "c_bias_sa": bias_sa.astype(f), "c_bias_sb": bias_sb.astype(f), "c_selh": sel.astype(f),
            "c_rowh": row.astype(f)}


_INS = ["x_prompt", "x_sample", "mem_prompt", "cache_diff_kv", "page_table", "cache_win1_kv", "cache_win2_kv",
        "cache_win3_kv", "cache_mem_kv", "g_norm", "w_in", "g_mem", "w_mem_kv", "lambda_q1", "lambda_k1",
        "lambda_q2", "lambda_k2", "g_subln", "w_proj_a", "w_proj_b", "w_proj_m", "w_out", "g_final"]
_OUTS = [(1, 512, 1024), (8, 1, 1024), (1, 1, 512, 2, 4, 128), (1, 1, 128, 2, 4, 64), (1, 1, 512, 2, 4, 64),
         (1, 1, 512, 2, 4, 64), (1, 1, 256, 2, 4, 64), (1, 8, 1, 2, 4, 128), (1, 8, 1, 2, 4, 64),
         (1, 8, 1, 2, 4, 64), (1, 8, 1, 2, 4, 64)]


def kernel(**inputs):
    import concourse.bacc as bacc
    from concourse.bass_utils import run_bass_kernel_spmd

    nc = bacc.Bacc("TRN2", target_bir_lowering=False, num_devices=1)
    arrays = {f"in_{n}": np.ascontiguousarray(inputs[n]) for n in _INS}
    arrays.update({f"in_{n}": a for n, a in constants().items()})
    ins = {n[3:]: nc.dram_tensor(n, a.shape, mybir.dt.from_np(a.dtype), kind="ExternalInput").ap()
           for n, a in arrays.items()}
    outs = [nc.dram_tensor(f"out_{i}", s, mybir.dt.float32, kind="ExternalOutput").ap() for i, s in enumerate(_OUTS)]
    build_kernel(nc, ins, outs)
    r = run_bass_kernel_spmd(nc, [arrays], core_ids=[0])
    return tuple(r.results[0][f"out_{i}"] for i in range(len(_OUTS)))
```

```python
from contextlib import ExitStack

import numpy as np
import concourse.bass as bass
from concourse import mybir

D = 1024
T = 512
NS = 8
TT = T + NS
HALF = TT // 2
KT = D // 128
NMEM = 256
CW = 256
EPS = 1e-6
LAM_INIT = 0.2
SCALE = 0.125
QT = T // 128
W_A = 2 * 128 + 1
G_ROWS = (128, 64, 16)
DIL = (1, 4, 16)
W_B = sum(G_ROWS) + 3


def chunk_sequence():
    first = [("mem", 0), ("mem", 1)] + [("in", j) for j in (4, 5, 2, 3, 0, 1)]
    beside_a = [("in", j) for j in (6, 7, 17)]
    second = [("in", j) for j in (18, 8, 11, 14, 10, 9, 13, 12, 16, 15, 19)]
    beside_bm = [("in", 20), ("in", 24)]
    third = [("in", 28), ("proj", 0)]
    for m in range(1, 4):
        third += [("in", 20 + m), ("in", 24 + m), ("in", 28 + m), ("proj", m)]
    return first, beside_a, second, beside_bm, third, [("out", m) for m in range(4)]


def build_kernel(nc, ins, outs):
    f32, f32r, i32 = mybir.dt.float32, mybir.dt.float32r, mybir.dt.int32
    ACT = mybir.ActivationFunctionType
    ALU = mybir.AluOpType
    AXX = mybir.AxisListType.X

    PARTS = chunk_sequence()
    SEQ = sum(PARTS, [])
    N_A, N_SECOND, N_BM, N_THIRD, N_OUT = (sum(map(len, PARTS[:i])) for i in range(1, 6))
    POS = {k: n for n, k in enumerate(SEQ)}

    x_p = ins["x_prompt"].rearrange("a t d -> (a t) d")
    x_s = ins["x_sample"].rearrange("b t d -> (b t) d")
    x_m = ins["mem_prompt"].rearrange("a t d -> (a t) d")
    w_in = ins["w_in"].rearrange("l (k p) n -> p (l k) n", p=128)
    w_mem = ins["w_mem_kv"].rearrange("l (k p) n -> p (l k) n", p=128)
    w_pa = ins["w_proj_a"].rearrange("l (k p) n -> p (l k) n", p=128)
    w_pb = ins["w_proj_b"].rearrange("l (k p) n -> p (l k) n", p=128)
    w_pm = ins["w_proj_m"].rearrange("l (k p) n -> p (l k) n", p=128)
    w_out = ins["w_out"].rearrange("l (k p) n -> p (l k) n", p=128)
    cache_a = ins["cache_diff_kv"].rearrange("l n p s h d -> (l n) p s (h d)")
    cache_1 = ins["cache_win1_kv"].rearrange("l b p s h d -> (l b) p s (h d)")
    cache_2 = ins["cache_win2_kv"].rearrange("l b (j r) s h d -> (l b) j r s (h d)", r=DIL[1])
    cache_3 = ins["cache_win3_kv"].rearrange("l b (j r) s h d -> (l b) j r s (h d)", r=DIL[2])
    cache_m = ins["cache_mem_kv"].rearrange("l b (t p) s h d -> (l b) p t s (h d)", p=128)
    diff_p = outs[2].rearrange("l b t s h d -> (l b t) s (h d)")
    win1_p = outs[3].rearrange("l b t s h d -> (l b t) (s h d)")
    win2_p = outs[4].rearrange("l b (j r) s h d -> r (l b j) (s h d)", r=4)
    win3_p = outs[5].rearrange("l b (j r) s h d -> r (l b j) (s h d)", r=4)
    mem_p = outs[6].rearrange("l b t s h d -> (l b t) (s h d)")
    diff_s = outs[7].rearrange("l b t s h d -> (l b t) s (h d)")
    win_s = [o.rearrange("l b t s h d -> (l b t) (s h d)") for o in outs[8:11]]
    y_p = outs[0].rearrange("a t d -> (a t) d")
    y_s = outs[1].rearrange("b t d -> (b t) d")

    ctx = ExitStack()
    early = ExitStack()
    with ctx:
        def sb(name, shape, dt=f32, where=ctx):
            return where.enter_context(nc.sbuf_tensor(name, shape, dt))

        def sem(name):
            return ctx.enter_context(nc.semaphore(name))

        xh = sb("xh", [128, KT, TT], f32r)
        xl = sb("xl", [128, KT, TT], f32r)
        w_raw = sb("w_raw", [128, 3, 4, CW])
        w_hi = sb("w_hi", [128, 2, KT, CW], f32r)
        w_lo = sb("w_lo", [128, 2, KT, CW], f32r)
        oz = sb("oz", [128, KT, TT])
        ident = sb("ident_sb", [128, 128])
        ones = sb("ones", [128, 128])
        ssq = sb("ssq", [128, 16])
        rstd = sb("rstd", [128, 16])
        eps = sb("eps", [128, 1])
        lamv = sb("lamv", [128, 8])
        gs = sb("gs", [128, 2])

        prod = sb("prod", [128, 1024], f32, early)
        stage = sb("stage", [128, 2, 512], f32, early)
        qs = sb("qs", [40, 1536], f32r, early)
        early.close()
        gate = sb("gate", [128, 3, 2, TT])
        g_fin = sb("g_fin", [128, D])

        memh = sb("memh", [128, KT, NMEM], f32r, early)
        meml = sb("meml", [128, KT, NMEM], f32r, early)
        early.close()
        rsq_split = sb("rsq_split", [36, 512], f32r, early)
        early.close()
        work = sb("work", [128, 4 * KT * NMEM // 2], f32, early)
        region = sb("region", [128, 16 * TT], f32, early)
        v_b = sb("v_b", [128, 3, QT, 256], f32, early)
        bias_b = sb("bias_b", [128, 4, 771], f32, early)
        vT = sb("vT", [128, 4, TT], f32, early)
        ring = sb("ring", [128, 2, 2, 512], f32, early)
        kmT = sb("kmT", [128, 2, NMEM], f32, early)
        vm = sb("vm", [128, 2, 256], f32, early)
        small = sb("small", [128, 1100], f32, early)
        pages = sb("pages", [1, 16], i32, early)
        pick = sb("pick", [40, NS], f32r, early)
        pick_in = sb("pick_in", [40, NS], f32, early)
        sel_h = sb("sel_h", [128, 4, 4], f32, early)
        early.close()

        mixh = sb("mixh", [128, KT, TT], f32r, early)
        mixl = sb("mixl", [128, KT, TT], f32r, early)
        oh = sb("oh", [128, KT, TT], f32r, early)
        ol = sb("ol", [128, KT, TT], f32r, early)
        mix_t = sb("mix_t", [128, 2, 3, HALF], f32, early)
        y_nat = sb("y_nat", [128, 5, D], f32, early)
        early.close()

        xin = [region[:, 1024 * t:1024 * t + 1024] for t in range(7)]
        qaT = region[:, 0:4 * TT].rearrange("p (h t) -> p h t", h=4)
        kaT = region[:, 4 * TT:8 * TT].rearrange("p (h t) -> p h t", h=4)
        v_a = region[:, 8 * TT:8 * TT + 2048].rearrange("p (t c) -> p t c", t=4)
        bias_a = region[:, 8 * TT + 2048:8 * TT + 4096].rearrange("p (h c) -> p h c", h=4)
        qbT = region[:, 0:6 * TT].rearrange("p (g h t) -> p g h t", g=3, h=2)
        kbT = region[:, 6 * TT:12 * TT].rearrange("p (g h t) -> p g h t", g=3, h=2)
        qmT = region[:, 12 * TT:14 * TT].rearrange("p (h t) -> p h t", h=2)
        g_row = ring[:, 0, :, :].rearrange("p a b -> p (a b)")
        g_row_m = ring[:, 1, :, :].rearrange("p a b -> p (a b)")
        sc = {"A": [work[:, 1024 * i:1024 * i + 1024] for i in range(3)],
              "B": [work[:, 768 * i:768 * i + 768] for i in range(3)]}
        pt = {"A": [work[:, 3072 + 512 * i:3584 + 512 * i] for i in range(2)],
              "B": [work[:, 2304 + 768 * i:3072 + 768 * i] for i in range(2)]}
        sc["M"], pt["M"] = sc["B"], pt["B"]
        oraw = vT
        oraw_sq = [work[:, 512 * h:512 * h + 512] for h in range(4)]
        rsq = work[0:4, 2048:2560]

        o = 0

        def cut(n):
            nonlocal o
            o += n
            return small[:, o - n:o]
        mx = cut(8)
        nm = cut(8)
        sm = cut(8)
        rs = cut(8)
        smx, snm, ssm, srs = cut(4), cut(4), cut(4), cut(4)
        lam_in = cut(256)
        s_a = cut(128)
        s_m = cut(64)
        s_1 = cut(32)
        s_23 = cut(32)
        vn_a = cut(32)
        vn_b = cut(48)
        pm_a = cut(64)
        pm_b = cut(96)
        bias_sa = work[0:64, 2560:2560 + W_A]
        e_a = work[0:64, 2832:2832 + W_A]
        e_m = work[0:32, 3104:3360]
        g_a = work[0:64, 3360:3392]
        g_m = work[0:32, 3392:3424]
        swork = vT[:, :, :].rearrange("p a b -> p (a b)")
        g_b = swork[0:32, 1792:1824]
        aT = swork[:, 1040:1360]
        t_a = swork[:, 1360:1392]
        o_as = swork[:, 1392:1424]
        sq_s = swork[:, 1424:1456]
        r_s = swork[:, 1456:1488]
        t_b = swork[:, 1488:1536]
        t_b2 = swork[:, 1536:1568]
        bias_sb = swork[0:32, 1568:1568 + W_B]
        e_b = swork[0:32, 1840:1840 + W_B]
        OWN_A, OWN_M = 14 * TT, 14 * TT + 512
        own_a, own_m = region[:, OWN_A:OWN_A + 512], region[:, OWN_M:OWN_M + 512]
        own_b = swork[:, 0:512]
        ov_sa = swork[0:32, 512:1024]
        ov_sb = swork[64:96, 512:1024]

        pj = [ctx.enter_context(nc.psum_tensor(f"pj{i}", [128, 512], f32)) for i in range(2)]
        ps = [ctx.enter_context(nc.psum_tensor(f"ps{i}", [128, 1024], f32)) for i in range(2)]
        pt_bank = ctx.enter_context(nc.psum_tensor("pt_bank", [128, 512], f32))
        po_bank = ctx.enter_context(nc.psum_tensor("po_bank", [128, 512], f32))
        bank = [ps[0][:, 0:512], ps[0][:, 512:1024], ps[1][:, 0:512], ps[1][:, 512:1024],
                pt_bank[:, :], po_bank[:, :]]

        s_raw = [sem(f"raw_loaded{i}") for i in range(3)]
        s_hi = sem("half_hi")
        s_lo = sem("half_lo")
        s_const = sem("const_loaded")
        s_ident = sem("ident_loaded")
        s_gain = [sem(f"gain_loaded{i}") for i in range(2)]
        s_vn = sem("new_values_kept")
        s_ob = sem("o_bm_gated")
        s_biasa = sem("bias_a_loaded")
        s_biasb = sem("bias_b_loaded")
        s_xin = [sem(f"x_loaded{i}") for i in range(7)]
        s_init = sem("init_done")
        s_qz = sem("q_rows_zeroed")
        s_qh = sem("q_rows_high")
        s_dv = sem("dve_step")
        s_sq = sem("x_squared")
        s_std = sem("x_std")
        s_xn = sem("x_normed")
        s_xt = sem("x_transposed")
        s_xh = sem("x_hi")
        s_xl = sem("x_lo")
        s_pj = sem("proj_done")
        s_ev = sem("proj_evacuated")
        s_nat = sem("nat_done")
        s_stage = sem("nat_staged")
        s_qrow = sem("q_rows_split")
        s_pc = sem("nat_copied")
        s_out = [sem(f"stage_stored{i}") for i in range(2)]
        s_S = sem("scores")
        s_bm = sem("biased_max")
        s_nm = sem("neg_max")
        s_ex = sem("exps")
        s_cb = sem("probs")
        s_T = sem("probs_transposed")
        s_te = sem("probsT_copied")
        s_pv = sem("pv_done")
        s_oe = sem("o_evacuated")
        s_lexp = sem("lambda_exp")
        s_lsum = sem("lambda_sum")
        s_osq = sem("o_squared")
        s_ov = sem("o_var")
        s_ostd = sem("o_std")
        s_orc = sem("o_rstd")
        s_orh = sem("o_rstd_hi")
        s_orl = sem("o_rstd_lo")
        s_obc = sem("o_rstd_bc")
        s_oa = sem("o_a_done")
        s_kr = [sem(f"ring_loaded{i}") for i in range(2)]
        s_qb = sem("q_broadcast")
        s_km = sem("k_multiplied")
        s_kd = sem("sample_scores")
        s_new = sem("new_products")
        s_sT = sem("samples_transposed")
        s_snm = sem("samples_neg_max")
        s_sex = sem("samples_exp")
        s_sG = sem("samples_norm")
        s_saT = sem("samples_probsT")
        s_sev = sem("samples_probsT_copied")
        s_spv = sem("samples_pv")
        s_own = sem("samples_masked_zeroed")
        s_ownb = sem("samples_masked_b_zeroed")
        s_sov = sem("samples_pv_copied")
        s_sot = sem("samples_o_transposed")
        s_silu = sem("silu_done")
        s_sig = sem("sigmoid_done")
        s_so = sem("samples_o")
        s_sbl = [sem(f"sample_bias_loaded{i}") for i in range(2)]
        s_oh = sem("o_hi")
        s_ol = sem("o_lo")
        s_pp = sem("branch_projected")
        s_mx = sem("mix_read")
        s_mix = sem("mixed")
        s_mh = sem("mixed_hi")
        s_ml = sem("mixed_lo")
        s_po = sem("out_projected")
        s_y = sem("y_added")
        s_ysq = sem("y_squared")
        s_ystd = sem("y_std")
        s_yo = sem("y_normed")
        s_yl = sem("residual_loaded")
        s_gf = sem("g_final_loaded")
        s_ys = sem("y_stored")
        s_pg = sem("pages_loaded")

        def units_of(kind):
            return {"mem": 2, "in": 4}.get(kind, 0)

        def pj_of(u):
            return pj[0] if U0[N_BM] <= u < U0[N_THIRD] else pj[u % 2]

        def sole_bank(u):
            return U0[N_BM] <= u <= U0[N_THIRD]
        U0 = [0]
        for kind, _ in SEQ:
            U0.append(U0[-1] + units_of(kind))

        def ev_of(key):
            return U0[POS[key] + 1]

        JOBS = []

        def job(need, rows, srcs, stores, copies):
            JOBS.append((POS[need], rows, srcs, stores, copies))

        def tok(ap, t):
            return ap[:, 128 * t:128 * t + (128 if t < 4 else NS)]

        for t in range(2):
            job(("mem", 1), 128, [kmT[:, 0, 128 * t:128 * t + 128], kmT[:, 1, 128 * t:128 * t + 128],
                                  vT[:, 2, 128 * t:128 * t + 128], vT[:, 3, 128 * t:128 * t + 128]],
                [(mem_p[128 * t:128 * t + 128, :], 0, 512)], [(vm[:, t, :], 256, 512)])
        J_MEM = len(JOBS)
        for t in range(5):
            dst = diff_p[128 * t:128 * t + 128, 1, :] if t < 4 else diff_s[:, 1, :]
            job(("in", 5), 128 if t < 4 else NS, [tok(vT[:, h, :], t) for h in range(4)],
                [(dst, 0, 512)], [(v_a[:, t, :], 0, 512)] if t < 4 else [])
        for t in range(5):
            dst = diff_p[128 * t:128 * t + 128, 0, :] if t < 4 else diff_s[:, 0, :]
            job(("in", 3), 128 if t < 4 else NS, [tok(kaT[:, h, :], t) for h in range(4)],
                [(dst, 0, 512)], [])
        J_A = len(JOBS)
        job(("in", 17), NS, [tok(qaT[:, h, :], 4) for h in range(4)], [], [])
        J_QA = len(JOBS)
        job(("in", 18), NS, [tok(qmT[:, h, :], 4) for h in range(2)], [], [])
        J_QM = len(JOBS)
        for g in range(3):
            job(("in", 8 + 3 * g), NS, [tok(qbT[:, g, h, :], 4) for h in range(2)], [], [])
        J_QB = len(JOBS)
        QS_COLS = {J_QA - 1: 0, J_QM - 1: 512, J_QM: 768, J_QM + 1: 1024, J_QM + 2: 1280}
        J_G = []
        for g in range(3):
            vt = [vT[:, (2 * g) % 4 + h, :] for h in range(2)]
            need = ("in", 9 + 3 * g)
            for t in range(4):
                if g == 0 and t < 3:
                    job(need, 128, [tok(v, t) for v in vt], [], [(v_b[:, 0, t, :], 0, 256)])
                    continue
                if g == 0:
                    srcs = [tok(kbT[:, 0, h, :], t) for h in range(2)] + [tok(v, t) for v in vt]
                    dst = win1_p
                else:
                    srcs = [kbT[:, g, h, t:T:4] for h in range(2)] + [v[:, t:T:4] for v in vt]
                    dst = (win2_p, win3_p)[g - 1][t]
                job(need, 128, srcs, [(dst, 0, 512)], [(v_b[:, g, t, :], 256, 512)])
            job(need, NS, [tok(kbT[:, g, h, :], 4) for h in range(2)] + [tok(v, 4) for v in vt],
                [(win_s[g], 0, 512)], [])
            J_G.append(len(JOBS))
        NJ = len(JOBS)
        PC = [0]
        OUTC = [0, 0]
        OUT_AT = []
        for J, (_, _, _, stores, copies) in enumerate(JOBS):
            PC.append(PC[-1] + len(copies))
            OUTC[J % 2] += 16 * len(stores)
            OUT_AT.append(OUTC[J % 2])

        def wait_staged(eng, J):
            q = sum(i in QS_COLS for i in range(J + 1))
            eng.wait_ge(s_stage, J + 1 - q)
            if q:
                eng.wait_ge(s_qrow, q)

        V_GUARD = {("in", 5): J_MEM, ("in", 10): J_A, ("in", 13): J_A, ("in", 16): J_G[0]}

        RINGS = [(k, b) for b in range(4) for k in "AM"]
        for b in range(4):
            RINGS += [("A", 4 + b), ("M", 4 + b), ("B", b)]
        K_AM = len(RINGS) - 1
        RINGS += [("B", b) for b in range(4, NS)]
        NK = len(RINGS)
        RINGS += [(k, b) for k in "BAM" for b in range(NS)]

        BESIDE = {}
        seen = [0] * len(SEQ)
        for J, (n, *_) in enumerate(JOBS):
            BESIDE.setdefault((n + 1, seen[n] // 2), []).append(("job", J))
            seen[n] += 1
        for k in range(NK):
            if k < 8:
                at = (N_SECOND + 1 + k // 2, k % 2)
            elif k < 20:
                at = (N_SECOND + 5 + (k - 8) // 3, (k - 8) % 3)
            else:
                at = (N_BM - 2, k - 20)
            BESIDE.setdefault(at, []).append(("ring", k))
        for h in range(4):
            BESIDE.setdefault((N_SECOND + 3, h), []).append(("rstd", h))
        BESIDE.setdefault((N_BM - 1, 0), []).append(("probs_am", 0))
        BESIDE.setdefault((N_BM - 1, 2), []).append(("rows_b", 0))

        def beside(n, k=None):
            return [e for i in (range(4) if k is None else [k]) for e in BESIDE.get((n, i), [])]

        LOADS = {"A": 2, "M": 1, "B": 3}
        KR = []
        cum = [0, 0]
        for k, (kind, _) in enumerate(RINGS):
            cum[k % 2] += 16 * LOADS[kind]
            KR.append(cum[k % 2])
        OA_UNITS = 4 * QT
        OB_UNITS = 4 * 4
        OM_UNITS = QT * 2
        NU = OA_UNITS + OB_UNITS + OM_UNITS

        SLOTS = {"A": [0, 1, 2, 4, 6, 7, 9, 10, 12, 13, 15, 17], "BM": [1, 3, 8, 12, 19, 21, 23, 24]}
        LAST_SLOT = {"A": OA_UNITS + 2, "BM": OB_UNITS + OM_UNITS + 2}
        FILL, SPLIT, SPLIT_LO = {}, {}, {}
        for which, n0 in (("A", N_A), ("BM", N_BM)):
            FILL[which] = {s: (n0 + i // 4, i % 4) for i, s in enumerate(SLOTS[which])}
            SPLIT[which], SPLIT_LO[which] = {}, {}
            if which == "BM":
                SPLIT_LO[which] = {2: [(n0 + 1, 0)], 3: [(n0 + 1, 1)]}
            for s, (n, k) in FILL[which].items():
                if k == 3:
                    for half in range(2):
                        SPLIT[which].setdefault(s + half, []).append((n + 2, half))
                        SPLIT_LO[which].setdefault(min(s + half + 1, LAST_SLOT[which]), []).append((n + 2, half))

        OUT_TILES = [4, 0, 1, 2, 3]
        OUT_ORDER = [(m, t) for m in range(2) for t in range(5)] + [(m, t) for t in OUT_TILES for m in (2, 3)]

        RAWC = [0, 0, 0]
        RAW_AT = []
        for m in range(2 * len(SEQ)):
            RAWC[m % 3] += 32 if (SEQ[m // 2][0] == "proj" and m % 2) else 16
            RAW_AT.append(RAWC[m % 3])

        block = ctx.enter_context(nc.Block())

        @block.sync
        def _(sp):
            def load_weights(m):
                n, s = divmod(m, 2)
                kind, j = SEQ[n]
                if m >= 3:
                    sp.wait_ge(s_lo, m - 2)
                if kind == "proj" and s == 1:
                    sp.dma_start(w_raw[:, m % 3, 0:2, :], w_pb[:, :, CW * j:CW * j + CW]).then_inc(s_raw[m % 3], 16)
                    sp.dma_start(w_raw[:, m % 3, 2:4, :], w_pm[:, :, CW * j:CW * j + CW]).then_inc(s_raw[m % 3], 16)
                    return
                src = {"mem": w_mem, "in": w_in, "proj": w_pa, "out": w_out}[kind]
                sp.dma_start(w_raw[:, m % 3, :, :],
                             src[:, 4 * s:4 * s + 4, CW * j:CW * j + CW]).then_inc(s_raw[m % 3], 16)

            def load_rows(t):
                src = x_m[128 * (t - 5):128 * (t - 4), :] if t >= 5 else x_s if t == 4 else x_p[128 * t:128 * t + 128, :]
                sp.dma_start(xin[t][0:(NS if t == 4 else 128), :], src).then_inc(s_xin[t], 16)

            load_rows(5)
            sp.dma_start(g_row_m, ins["g_mem"].partition_broadcast(128).rearrange("p a d -> p (a d)")).then_inc(s_gain[1], 16)
            sp.dma_start(ident[:, :], ins["c_ident"]).then_inc(s_ident, 16)
            load_rows(6)
            load_weights(0)
            load_weights(1)
            load_rows(0)
            sp.dma_start(g_row, ins["g_norm"].partition_broadcast(128).rearrange("p a d -> p (a d)")).then_inc(s_gain[0], 16)
            load_rows(1)
            load_weights(2)
            load_rows(2)
            load_weights(3)
            load_rows(3)
            load_rows(4)
            def store_rows(n):
                for J in (i for what, i in beside(n) if what == "job"):
                    _, rows, _, stores, _ = JOBS[J]
                    for dst, a, b in stores:
                        wait_staged(sp, J)
                        sp.dma_start(dst, stage[0:rows, J % 2, a:b]).then_inc(s_out[J % 2], 16)

            for m in range(4, 2 * len(SEQ)):
                if m % 2 and m >= 7:
                    store_rows((m - 7) // 2)
                load_weights(m)
            for j, t in enumerate(OUT_TILES):
                for c in range(2):
                    sp.wait_ge(s_yo, 2 * j + c + 1)
                    cols = slice(512 * c, 512 * c + 512)
                    dst = y_p[128 * t:128 * t + 128, cols] if t < 4 else y_s[:, cols]
                    sp.dma_start(dst, y_nat[0:(128 if t < 4 else NS), t, cols]).then_inc(s_ys, 16)
            sp.wait_ge(s_ys, 160)

        @block.gpsimd
        def _(pool):
            pool.memset(eps[:, :], EPS).then_inc(s_init, 1)
            pool.memset(ssq[:, :], 1.0).then_inc(s_init, 1)
            pool.memset(ones[:, :], 1.0).then_inc(s_init, 1)
            pool.memset(pm_a, 0.0).then_inc(s_init, 1)
            pool.memset(pm_b, 0.0).then_inc(s_init, 1)
            for i, n in enumerate(("lambda_q1", "lambda_k1", "lambda_q2", "lambda_k2")):
                pool.dma_start(lam_in[:, 64 * i:64 * i + 64],
                               ins[n].partition_broadcast(128).rearrange("p a d -> p (a d)")).then_inc(s_const, 16)
            pool.dma_start(gs[:, 0:1], ins["g_subln"].rearrange("l d -> d l")).then_inc(s_const, 16)
            pool.dma_start(sel_h[:, :, :], ins["c_selh"]).then_inc(s_const, 16)
            pool.dma_start(pick_in[:, :], ins["c_pick"]).then_inc(s_const, 16)
            pool.dma_start(pages[:, :], ins["page_table"].rearrange("b n -> (b n)").unsqueeze(0)).then_inc(s_pg, 16)

            def copy_job(J):
                _, rows, _, _, copies = JOBS[J]
                if not copies:
                    return
                wait_staged(pool, J)
                for dst, a, b in copies:
                    pool.tensor_copy(dst, stage[0:rows, J % 2, a:b]).then_inc(s_pc, 1)

            def load_ring(k):
                kind, b = RINGS[k]
                s = 0 if k < NK else 1
                if k >= 2 and k - 2 < NK:
                    pool.wait_ge(s_km, k - 1)
                elif k >= 2:
                    pool.wait_ge(s_spv, k - 2 - NK + 1)
                slot = ring[:, k % 2, :, :]
                if kind == "A":
                    for t in range(2):
                        page = pool.value_load(pages[0:1, 2 * b + t:2 * b + t + 1], min_val=0,
                                               max_val=cache_a.shape[0] - 1)
                        pool.dma_start(slot[:, t, :], cache_a[bass.ds(page, 1), :, s, :].rearrange("a p c -> (a p) c")).then_inc(s_kr[k % 2], 16)
                elif kind == "M":
                    pool.dma_start(slot[:, :, 0:256], cache_m[b, :, :, s, :]).then_inc(s_kr[k % 2], 16)
                else:
                    pool.dma_start(slot[:, 0, 0:256], cache_1[b, :, s, :]).then_inc(s_kr[k % 2], 16)
                    pool.dma_start(slot[0:64, 1, 0:256], cache_2[b, :, 0, s, :]).then_inc(s_kr[k % 2], 16)
                    pool.dma_start(slot[64:80, 1, 0:256], cache_3[b, :, 0, s, :]).then_inc(s_kr[k % 2], 16)

            def run_beside(n):
                for what, i in beside(n):
                    if what == "job":
                        copy_job(i)
                    elif what == "ring":
                        load_ring(i + 2)

            for n in range(N_SECOND):
                if n == 3:
                    pool.wait_ge(s_xt, 14)
                    pool.dma_start(bias_a, ins["c_bias_a"]).then_inc(s_biasa, 16)
                run_beside(n)
            pool.dma_start(bias_b[:, :, :], ins["c_bias_b"]).then_inc(s_biasb, 16)
            pool.wait_ge(s_pg, 16)
            pool.wait_ge(s_xn, 7)
            load_ring(0)
            load_ring(1)
            pool.wait_ge(s_pv, OA_UNITS)
            pool.dma_start(bias_sa, ins["c_bias_sa"]).then_inc(s_sbl[0], 16)
            for n in range(N_SECOND, N_BM):
                run_beside(n)
                if n == N_BM - 2:
                    pool.wait_ge(s_nat, J_G[1])
                    pool.wait_ge(s_vn, 10)
                    pool.dma_start(bias_sb, ins["c_bias_sb"]).then_inc(s_sbl[1], 16)
            pool.wait_ge(s_nat, NJ)
            pool.memset(own_b, 0.0).then_inc(s_ownb, 1)
            for k in range(NK + 2, 2 * NK):
                load_ring(k)
            pool.wait_ge(s_so, 2)
            for i in range(2):
                pool.wait_ge(s_out[i], OUTC[i])
            for t in range(4):
                pool.dma_start(y_nat[:, t, :], x_p[128 * t:128 * t + 128, :]).then_inc(s_yl, 16)
            pool.dma_start(y_nat[0:NS, 4, :], x_s).then_inc(s_yl, 16)
            pool.dma_start(g_fin[:, :], ins["g_final"].unsqueeze(0).partition_broadcast(128).rearrange("p a d -> p (a d)")).then_inc(s_gf, 16)

        XORDER = [5, 6, 0, 1, 2, 3, 4]

        def rows_of(t):
            return NS if t == 4 else 128

        def x_dst(buf_x, buf_m, t, kg):
            if t < 5:
                return buf_x[:, 4 * kg:4 * kg + 4, 128 * t:128 * t + rows_of(t)]
            return buf_m[:, 4 * kg:4 * kg + 4, 128 * (t - 5):128 * (t - 5) + 128]

        def attn_slot(u):
            if u < OA_UNITS:
                return "A", u // QT, u % QT
            u -= OA_UNITS
            if u < OB_UNITS:
                return "B", u // 4, u % 4
            u -= OB_UNITS
            return "M", u // 2, u % 2

        def pairs_through(u):
            v = u - OA_UNITS + 1
            return max(0, v // 2 if v <= OB_UNITS else v - OB_UNITS // 2)

        RANGES = {"A": (0, OA_UNITS), "BM": (OA_UNITS, NU)}

        @block.tensor
        def _(pe):
            def transpose_input(i):
                t = XORDER[i]
                pe.wait_ge(s_xn, i + 1)
                for kg in range(2):
                    g = 2 * i + kg
                    if g >= 4:
                        pe.wait_ge(s_xl, g - 3)
                    for c in range(4):
                        last = pe.transpose(bank[g % 4][:, 128 * c:128 * c + rows_of(t)],
                                            xin[t][0:rows_of(t), 512 * kg + 128 * c:512 * kg + 128 * c + 128],
                                            ident[0:rows_of(t), 0:rows_of(t)])
                    last.then_inc(s_xt, 1)

            def product(out, parts, hi_m, lo_m):
                n = len(parts)
                for i, (slot, kt, c0, cn, kx, a, b) in enumerate(parts):
                    wh = w_hi[:, slot, kt, c0:c0 + cn]
                    wl = w_lo[:, slot, kt, c0:c0 + cn]
                    mh, ml = hi_m[:, kx, a:b], lo_m[:, kx, a:b]
                    pe.matmul(out, wh, mh, start=(i == 0), stop=False)
                    pe.matmul(out, wl, mh, start=False, stop=False)
                    last = pe.matmul(out, wh, ml, start=False, stop=(i == n - 1))
                return last

            def nat_job(J):
                need, rows, srcs, _, _ = JOBS[J]
                pe.wait_ge(s_ev, U0[need + 1])
                if J >= 2:
                    wait_staged(pe, J - 2)
                for c, src in enumerate(srcs):
                    last = pe.transpose(bank[J % 2][0:rows, 128 * c:128 * c + 128], src, ident[:, :])
                last.then_inc(s_nat, 1)

            def project_unit(n, k):
                kind, j = SEQ[n]
                if k == 0:
                    pe.wait_ge(s_lo, 2 * n + 2)
                hi_m, lo_m = (memh, meml) if kind == "mem" else (xh, xl)
                tile, (a, b) = (k, (0, NMEM)) if kind == "mem" else (k // 2, ((0, HALF), (HALF, TT))[k % 2])
                u = U0[n] + k
                if u >= 2:
                    pe.wait_ge(s_ev, u if sole_bank(u) else u - 1)
                product(pj_of(u)[:, 0:b - a],
                        [(n % 2, kt, 128 * tile, 128, kt, a, b) for kt in range(KT)], hi_m, lo_m).then_inc(s_pj, 1)

            def project_chunk(n):
                for k in range(units_of(SEQ[n][0])):
                    project_unit(n, k)
                    for what, i in beside(n, k):
                        if what == "job":
                            nat_job(i)
                        elif what == "ring":
                            broadcast_q(i)
                        elif what == "rstd":
                            broadcast_rstd(i)
                        elif what == "probs_am":
                            samples_probs_am()
                        else:
                            samples_rows_b()

            def broadcast_rstd(h):
                if h == 0:
                    pe.wait_ge(s_orl, 1)
                if h >= 2:
                    pe.wait_ge(s_oa, h - 1)
                dst = (pt_bank, po_bank)[h % 2][:, 0:512]
                pe.matmul(dst, pick[0:36, h:h + 1].to_broadcast([36, 128]), rsq_split[:, :],
                          start=True, stop=True).then_inc(s_obc, 1)

            def broadcast_q(k):
                kind, b = RINGS[k]
                wait_staged(pe, {"A": J_QA, "M": J_QM, "B": J_QB}[kind] - 1)
                if k >= 2:
                    pe.wait_ge(s_km, k - 1)
                out = bank[2 + k % 2]
                one = pick[:, b:b + 1]
                if kind == "A":
                    last = pe.matmul(out, one.to_broadcast([40, 128]), qs[:, 0:512], start=True, stop=True)
                elif kind == "M":
                    last = pe.matmul(out[:, 0:256], one.to_broadcast([40, 128]), qs[:, 512:768], start=True, stop=True)
                else:
                    pe.matmul(out[:, 0:256], one.to_broadcast([40, 128]), qs[:, 768:1024], start=True, stop=True)
                    pe.matmul(out[0:64, 256:512], one.to_broadcast([40, 64]), qs[:, 1024:1280], start=True, stop=True)
                    last = pe.matmul(out[64:80, 256:512], pick_in[:, b:b + 1].to_broadcast([40, 16]),
                                     qs[:, 1280:1536].bitcast(f32), start=True, stop=True)
                last.then_inc(s_qb, 1)

            def scores(u):
                br, p, q = attn_slot(u)
                S = ps[u % 2]
                if u >= 2:
                    pe.wait_ge(s_bm, u - 1)
                    if attn_slot(u - 2)[0] == "M":
                        pe.wait_ge(s_ex, u - 1)
                if br == "A":
                    for c in range(2):
                        rows = slice(64 * c, 64 * c + 64)
                        last = pe.matmul(S[:, 512 * c:512 * c + 128 * (q + 1)],
                                         qaT[rows, p, 128 * q:128 * q + 128],
                                         kaT[rows, p, 0:128 * (q + 1)], start=True, stop=True)
                elif br == "B":
                    hp, hh = divmod(q, 2)
                    rows = slice(64 * hh, 64 * hh + 64)
                    pe.matmul(S[:, 0:512], qbT[rows, 0, hp, p:T:4], kbT[rows, 0, hp, 0:T], start=True, stop=True)
                    pe.matmul(S[:, 512:640], qbT[rows, 1, hp, p:T:4], kbT[rows, 1, hp, p:T:4], start=True, stop=True)
                    last = pe.matmul(S[:, 640:768], qbT[rows, 2, hp, p:T:4], kbT[rows, 2, hp, p:T:4],
                                     start=True, stop=True)
                else:
                    for hh in range(2):
                        rows = slice(64 * hh, 64 * hh + 64)
                        last = pe.matmul(S[:, 512 * hh:512 * hh + 256], qmT[rows, q, 128 * p:128 * p + 128],
                                         kmT[rows, q, :], start=True, stop=True)
                last.then_inc(s_S, 1)

            def transposes(u):
                br, p, q = attn_slot(u)
                pe.wait_ge(s_cb, u + 1)
                pe.wait_ge(s_te, u)
                if u == OA_UNITS:
                    pe.wait_ge(s_sev, 3)
                if u > OA_UNITS:
                    pe.wait_ge(s_ob, pairs_through(u - 1))
                blocks = {"A": q + 1, "B": 6, "M": 4}[br]
                for k in range(blocks):
                    dst = pt_bank[:, 128 * k:128 * k + 128] if k < 4 else po_bank[:, 128 * k - 512:128 * k - 384]
                    last = pe.transpose(dst, sc[br][u % 3][:, 128 * k:128 * k + 128], ident[:, :])
                last.then_inc(s_T, 1)

            def values(u):
                br, p, q = attn_slot(u)
                pe.wait_ge(s_te, u + 1)
                P = pt[br][u % 2]
                if br == "A":
                    out = po_bank[:, 128 * q:128 * q + 128]
                    if q == 0 and p > 0:
                        pe.wait_ge(s_oe, p)
                    for k in range(q + 1):
                        last = pe.matmul(out, v_a[:, k, 128 * p:128 * p + 128], P[:, 128 * k:128 * k + 128],
                                         start=(k == 0), stop=(k == q))
                else:
                    v = u - OA_UNITS
                    pair = v // 2 if br == "B" else OB_UNITS // 2 + (v - OB_UNITS)
                    heads = [(q // 2, q % 2)] if br == "B" else [(q, 0), (q, 1)]
                    if v == 0:
                        pe.wait_ge(s_pc, PC[NJ])
                    if pair and (br == "M" or q % 2 == 0):
                        pe.wait_ge(s_ob, pair)
                    for hp, hh in heads:
                        out = po_bank[64 * hh:64 * hh + 64, 256:384]
                        cols = slice(128 * hp + 64 * hh, 128 * hp + 64 * hh + 64)
                        if br == "B":
                            parts = [(v_b[:, 1, p, cols], 4, 0, 128), (v_b[:, 2, p, cols], 5, 0, 128)]
                            parts += [(v_b[:, 0, k, cols], k, 32 * k, min(32 * k + 64, 128)) for k in range(4)]
                        else:
                            parts = [(vm[:, k, cols], 2 * hh + k, 0, 128) for k in range(2)]
                        for i, (v, k, q0, q1) in enumerate(parts):
                            last = pe.matmul(out[:, q0:q1], v, P[:, 128 * k + q0:128 * k + q1],
                                             start=(i == 0), stop=(i == len(parts) - 1))
                last.then_inc(s_pv, 1)

            def attention(which):
                a, b = RANGES[which]
                for s in range(a, b + 3):
                    if s < b:
                        scores(s)
                    if which == "BM" and s == a + 1:
                        samples_probs_b()
                    if which == "BM" and s >= a + 3:
                        sample_values(NK + s - a - 3)
                    if a <= s - 3:
                        values(s - 3)
                    if s - a in FILL[which]:
                        project_unit(*FILL[which][s - a])
                    if a <= s - 2 < b:
                        transposes(s - 2)

            sa = s_a.rearrange("p (t r) -> p t r", t=2)
            smt = s_m.rearrange("p (t r) -> p t r", t=2)

            def samples_rows_am():
                pe.wait_ge(s_kd, K_AM)
                pe.wait_ge(s_new, 2)
                pe.wait_ge(s_oa, 4)
                for t in range(2):
                    pe.transpose(pt_bank[0:64, 128 * t:128 * t + 128], sa[:, t, :], ident[:, :])
                pe.matmul(pt_bank[0:64, 256:257], pm_a, ones[:, 0:1], start=True, stop=True).then_inc(s_sT, 1)
                for t in range(2):
                    last = pe.transpose(po_bank[0:32, 128 * t:128 * t + 128], smt[:, t, :], ident[:, :])
                last.then_inc(s_sT, 1)

            def samples_probs_am():
                pe.wait_ge(s_sG, 2)
                out = pt_bank[:, 288:448]
                for t in range(2):
                    pe.matmul(out[:, 32 * t:32 * t + 32], e_a[:, 128 * t:128 * t + 128], g_a, start=True, stop=True)
                pe.matmul(out[:, 64:96], e_a[:, 256:257].to_broadcast([64, 128]), g_a, start=True, stop=True)
                for t in range(2):
                    last = pe.matmul(out[:, 96 + 32 * t:128 + 32 * t], e_m[:, 128 * t:128 * t + 128], g_m,
                                     start=True, stop=True)
                last.then_inc(s_saT, 1)

            def samples_rows_b():
                pe.wait_ge(s_kd, NK)
                pe.wait_ge(s_new, 4)
                pe.wait_ge(s_sex, 2)
                pe.transpose(po_bank[0:32, 0:128], s_1, ident[:, :])
                pe.transpose(po_bank[0:32, 128:208], s_23[0:80, :], ident[0:80, 0:80])
                for g in range(3):
                    last = pe.matmul(po_bank[0:32, 208 + g:209 + g], pm_b[:, 32 * g:32 * g + 32], ones[:, 0:1],
                                     start=True, stop=True)
                last.then_inc(s_sT, 1)

            def samples_probs_b():
                pe.wait_ge(s_sG, 3)
                out = po_bank[:, 256:416]
                pe.matmul(out[:, 0:32], e_b[:, 0:128], g_b, start=True, stop=True)
                for g in range(3):
                    pe.matmul(out[:, 32 + 32 * g:64 + 32 * g], e_b[:, 208 + g:209 + g].to_broadcast([32, 128]), g_b,
                              start=True, stop=True)
                pe.matmul(out[0:80, 128:160], e_b[:, 128:208], g_b, start=True, stop=True).then_inc(s_saT, 1)

            def sample_values(k):
                kind, b = RINGS[k]
                pe.wait_ge(s_kr[k % 2], KR[k])
                if k == NK:
                    pe.wait_ge(s_sev, 3)
                slot = ring[:, k % 2, :, :]
                for t in range(2):
                    cols = slice(256 * t + 32 * b, 256 * t + 32 * b + 32)
                    first, end = b == 0 and t == 0, b == NS - 1 and t == 1
                    if kind == "A":
                        last = pe.matmul(pj[1][0:32, 0:512], own_a[:, cols], slot[:, t, :], start=first, stop=end)
                    elif kind == "M":
                        last = pe.matmul(pj[1][64:96, 0:256], own_m[:, cols], slot[:, t, 0:256], start=first, stop=end)
                    else:
                        r = 128 if t == 0 else 80
                        last = pe.matmul(pj[1][64:96, 256:512], own_b[0:r, cols], slot[0:r, t, 0:256],
                                         start=first, stop=end)
                last.then_inc(s_spv, 1)

            def samples_outputs():
                pe.wait_ge(s_sov, 2)
                pe.wait_ge(s_pv, NU)
                for h in range(4):
                    last = pe.transpose(po_bank[:, 32 * h:32 * h + 32], ov_sa[:, 128 * h:128 * h + 128], ident[0:32, 0:32])
                last.then_inc(s_sot, 1)
                for c in range(4):
                    last = pe.transpose(pt_bank[:, 32 * c:32 * c + 32], ov_sb[:, 128 * c:128 * c + 128],
                                        ident[64:96, 64:96])
                last.then_inc(s_sot, 1)

            pe.wait_ge(s_ident, 16)
            pe.wait_ge(s_init, 5)
            for i in range(3):
                transpose_input(i)
            pe.wait_ge(s_xl, 4)
            for i in range(4):
                if i:
                    transpose_input(2 + i)
                if i == 3:
                    transpose_input(6)
                project_unit(i // 2, i % 2)
            pe.wait_ge(s_xl, 14)
            for n in range(2, N_A):
                project_chunk(n)
            wait_staged(pe, J_A - 1)
            pe.wait_ge(s_pc, PC[J_A])
            pe.wait_ge(s_ev, U0[N_A])
            attention("A")
            pe.wait_ge(s_bm, OA_UNITS)
            pe.wait_ge(s_te, OA_UNITS)
            for n in range(N_SECOND, N_BM):
                if n == N_SECOND + 1:
                    pe.wait_ge(s_const, 16 * 7)
                    for h in range(4):
                        pe.wait_ge(s_osq, h + 1)
                        last = pe.matmul(pt_bank[0:4, 0:512], sel_h[:, h, :], oraw_sq[h], start=(h == 0), stop=(h == 3))
                    last.then_inc(s_ov, 1)
                if n == N_BM - 2:
                    samples_rows_am()
                project_chunk(n)
            wait_staged(pe, NJ - 1)
            pe.wait_ge(s_ev, U0[N_BM])
            pe.wait_ge(s_km, NK)
            attention("BM")
            pe.wait_ge(s_bm, NU)
            pe.wait_ge(s_ex, NU)

            for m in range(4):
                for g in range(3):
                    if m == 0 and g < 2:
                        continue
                    for k in range(4):
                        project_unit(POS["in", 20 + 4 * g + m], k)
                        if m == 0 and k == 0:
                            samples_outputs()
                        if m == 0 and k == 1:
                            pe.wait_ge(s_so, 1)
                            pe.matmul(bank[3][:, 0:32], ones[:, :], sq_s, start=True, stop=True).then_inc(s_saT, 1)
                n = POS["proj", m]
                pe.wait_ge(s_lo, 2 * n + 2)
                for tile in range(2):
                    for hf in range(2):
                        i = 4 * m + 2 * tile + hf
                        a, b = HALF * hf, HALF * hf + HALF
                        if i >= 2:
                            pe.wait_ge(s_mx, i - 1)
                        else:
                            pe.wait_ge(s_ol, 2 + i)
                        for br, kts in enumerate(((0, 1, 2, 3), (4, 5), (6, 7))):
                            last = product(bank[3 * (i % 2) + br][:, 0:HALF],
                                           [(n % 2, kt, 128 * tile, 128, kt, a, b) for kt in kts], oh, ol)
                        last.then_inc(s_pp, 1)
            pe.wait_ge(s_ev, U0[-1])
            for i, (m, t) in enumerate(OUT_ORDER):
                n = N_OUT + m
                pe.wait_ge(s_lo, 2 * n + 2)
                rows = rows_of(t)
                if i >= 2:
                    pe.wait_ge(s_y, i - 1)
                out = pj[i % 2][0:rows, 0:CW]
                for kt in range(KT):
                    if m == 0 and t < 3:
                        pe.wait_ge(s_ml, 2 * kt + (1 if t < 2 else 2))
                    mh = mixh[:, kt, 128 * t:128 * t + rows]
                    ml = mixl[:, kt, 128 * t:128 * t + rows]
                    pe.matmul(out, mh, w_hi[:, n % 2, kt, :], start=(kt == 0), stop=False)
                    pe.matmul(out, ml, w_hi[:, n % 2, kt, :], start=False, stop=False)
                    last = pe.matmul(out, mh, w_lo[:, n % 2, kt, :], start=False, stop=(kt == KT - 1))
                last.then_inc(s_po, 1)

        def wait_chunk_used(eng, n):
            kind, j = SEQ[n]
            if kind == "proj":
                eng.wait_ge(s_pp, 4 * (j + 1))
            elif kind == "out":
                eng.wait_ge(s_po, 5 * (j + 1))
            else:
                eng.wait_ge(s_pj, U0[n + 1])

        @block.scalar
        def _(act):
            def hi_split(n, halves=(0, 1)):
                if n >= len(SEQ):
                    return
                if n >= 2:
                    wait_chunk_used(act, n - 2)
                for s in halves:
                    m = 2 * n + s
                    act.wait_ge(s_raw[m % 3], RAW_AT[m])
                    act.activation(w_hi[:, n % 2, 4 * s:4 * s + 4, :], w_raw[:, m % 3, :, :], ACT.Copy).then_inc(s_hi, 1)

            def evac_dest(key, tile, a, b):
                kind, j = key
                if kind == "mem":
                    return kmT[:, tile, a:b] if j == 0 else vT[:, 2 + tile, a:b]
                c = 2 * j + tile
                if j < 2:
                    return qaT[:, c, a:b]
                if j < 4:
                    return kaT[:, c - 4, a:b]
                if j < 6:
                    return vT[:, c - 8, a:b]
                if j < 8:
                    return oz[:, c - 12, a:b]
                if j < 17:
                    g, r = divmod(j - 8, 3)
                    if r == 2:
                        return vT[:, (2 * g) % 4 + tile, a:b]
                    return (qbT, kbT)[r][:, g, tile, a:b]
                if j == 17:
                    return oz[:, 4 + tile, a:b]
                if j == 18:
                    return qmT[:, tile, a:b]
                if j == 19:
                    return oz[:, 6 + tile, a:b]
                return gate[:, (j - 20) // 4, tile, a:b]

            def evacuate_unit(n, k):
                key = SEQ[n]
                kind, j = key
                if N_A <= n < N_SECOND or N_BM <= n < N_THIRD:
                    func = ACT.Copy
                elif kind == "in" and j >= 20:
                    func = ACT.Sigmoid
                elif kind == "in" and j in (6, 7, 17, 19):
                    func = ACT.Silu
                else:
                    func = ACT.Copy
                if k == 0:
                    if key in V_GUARD:
                        act.wait_ge(s_nat, V_GUARD[key])
                    if key == ("in", 10):
                        act.wait_ge(s_oa, 4)
                    if key == ("in", 8):
                        act.wait_ge(s_new, 2)
                        act.wait_ge(s_nat, J_QA)
                    if key == ("in", 20):
                        act.wait_ge(s_kd, NK)
                        act.wait_ge(s_qb, NK)
                        for i in range(2):
                            act.wait_ge(s_out[i], OUTC[i])
                tile, (a, b) = (k, (0, NMEM)) if kind == "mem" else (k // 2, ((0, HALF), (HALF, TT))[k % 2])
                u = U0[n] + k
                act.wait_ge(s_pj, u + 1)
                if kind == "in" and j >= 20 and (j - 20) % 4:
                    act.wait_ge(s_mx, 4 * ((j - 21) % 4) + 2 * tile + (1 if a else 0) + 1)
                act.activation(evac_dest(key, tile, a, b), pj_of(u)[:, 0:b - a], func).then_inc(s_ev, 1)
                if kind == "in" and a and (j in (4, 5) or j in (10, 13, 16)):
                    if j < 6:
                        dst = vn_a[:, 8 * (2 * j - 8 + tile):8 * (2 * j - 8 + tile) + 8]
                    else:
                        g = (j - 10) // 3
                        dst = vn_b[:, 16 * g + 8 * tile:16 * g + 8 * tile + 8]
                    act.wait_ge(s_ev, u + 1)
                    act.activation(dst, evac_dest(key, tile, 512, TT), ACT.Copy).then_inc(s_vn, 1)

            def evacuate(n):
                for k in range(units_of(SEQ[n][0])):
                    evacuate_unit(n, k)

            def stage_job(J):
                _, rows, srcs, _, _ = JOBS[J]
                act.wait_ge(s_nat, J + 1)
                w = 128 * len(srcs)
                if J in QS_COLS:
                    c = QS_COLS[J]
                    act.activation(qs[0:NS, c:c + w], bank[J % 2][0:NS, 0:w], ACT.Copy).then_inc(s_qh, 1)
                    return
                if J >= 2:
                    act.wait_ge(s_out[J % 2], OUT_AT[J - 2])
                    act.wait_ge(s_pc, PC[J - 1])
                act.activation(stage[0:rows, J % 2, 0:w], bank[J % 2][0:rows, 0:w], ACT.Copy).then_inc(s_stage, 1)

            def run_beside(n, k):
                for what, i in beside(n, k):
                    if what == "job":
                        stage_job(i)

            def exps(u):
                br, p, q = attn_slot(u)
                act.wait_ge(s_nm, u + 1)
                k4 = 2 * (u % 4)
                buf = sc[br][u % 3]
                if br == "A":
                    kn = 128 * (q + 1)
                    act.activation(buf[:, 0:kn], buf[:, 0:kn], ACT.Exp, bias=nm[:, k4:k4 + 1],
                                   accum_out=sm[:, k4:k4 + 1])
                    act.activation(buf[:, 512:512 + kn], buf[:, 512:512 + kn], ACT.Exp, bias=nm[:, k4 + 1:k4 + 2],
                                   accum_out=sm[:, k4 + 1:k4 + 2]).then_inc(s_ex, 1)
                elif br == "B":
                    act.activation(buf[:, 0:768], buf[:, 0:768], ACT.Exp, bias=nm[:, k4:k4 + 1],
                                   accum_out=sm[:, k4:k4 + 1]).then_inc(s_ex, 1)
                else:
                    for hh in range(2):
                        last = act.activation(buf[:, 256 * hh:256 * hh + 256], ps[u % 2][:, 512 * hh:512 * hh + 256],
                                              ACT.Exp, bias=nm[:, k4 + hh:k4 + hh + 1], scale=SCALE,
                                              accum_out=sm[:, k4 + hh:k4 + hh + 1])
                    last.then_inc(s_ex, 1)

            def copy_probs(u):
                br, p, q = attn_slot(u)
                act.wait_ge(s_T, u + 1)
                if u >= 2:
                    act.wait_ge(s_pv, u - 1)
                P = pt[br][u % 2]
                if br == "B":
                    act.activation(P[:, 0:512], pt_bank[:, :], ACT.Copy)
                    act.activation(P[:, 512:768], po_bank[:, 0:256], ACT.Copy).then_inc(s_te, 1)
                else:
                    w = 128 * (q + 1) if br == "A" else 512
                    act.activation(P[:, 0:w], pt_bank[:, 0:w], ACT.Copy).then_inc(s_te, 1)

            def attention(which):
                a, b = RANGES[which]
                for s in range(a, b + 4):
                    v = s - 4
                    if which == "A" and a <= v < b and attn_slot(v)[2] == QT - 1:
                        h = attn_slot(v)[1]
                        act.wait_ge(s_pv, v + 1)
                        act.activation(oraw[:, h, 0:T], po_bank[:, :], ACT.Copy).then_inc(s_oe, 1)
                    fill = FILL[which].get(s - a)
                    if a <= s - 2 < b and not fill:
                        copy_probs(s - 2)
                    if s < b:
                        exps(s)
                    if fill:
                        evacuate_unit(*fill)
                        if a <= s - 2 < b:
                            copy_probs(s - 2)
                    for n, half in SPLIT[which].get(s - a, ()):
                        hi_split(n, (half,))

            def samples_exp_am():
                act.wait_ge(s_snm, 1)
                act.activation(e_a, e_a, ACT.Exp, bias=snm[0:64, 0:1], accum_out=ssm[0:64, 0:1]).then_inc(s_sex, 1)
                act.wait_ge(s_snm, 2)
                act.activation(e_m, po_bank[0:32, 0:256], ACT.Exp, bias=snm[0:32, 1:2], scale=SCALE,
                               accum_out=ssm[0:32, 1:2]).then_inc(s_sex, 1)

            def samples_exp_b():
                act.wait_ge(s_snm, 3)
                act.activation(e_b, e_b, ACT.Exp, bias=snm[0:32, 2:3], accum_out=ssm[0:32, 2:3]).then_inc(s_sex, 1)

            act.wait_ge(s_init, 2)
            act.activation(rstd[:, 15:16], eps[:, :], ACT.Sqrt)
            def square_root(i):
                t = XORDER[i]
                r = rows_of(t)
                act.wait_ge(s_xin[t], 16)
                if i:
                    act.wait_ge(s_sq, i)
                act.activation(prod[0:r, :], xin[t][0:r, :], ACT.Square,
                               accum_out=ssq[0:r, t:t + 1]).then_inc(s_sq, 1)
                act.wait_ge(s_sq, i + 1)
                act.activation(rstd[0:r, t:t + 1], ssq[0:r, t:t + 1], ACT.Sqrt, scale=1.0 / D,
                               bias=eps[0:r, :]).then_inc(s_std, 1)

            def high_x(i):
                t = XORDER[i]
                for g in (2 * i, 2 * i + 1):
                    act.wait_ge(s_xt, g + 1)
                    src = bank[g % 4].rearrange("p (c t) -> p c t", c=4)[:, :, 0:rows_of(t)]
                    act.activation(x_dst(xh, memh, t, g % 2), src, ACT.Copy).then_inc(s_xh, 1)

            square_root(0)
            square_root(1)
            hi_split(0)
            high_x(0)
            square_root(2)
            high_x(1)
            square_root(3)
            high_x(2)
            square_root(4)
            hi_split(1)
            high_x(3)
            evacuate_unit(0, 0)
            square_root(5)
            square_root(6)
            evacuate_unit(0, 1)
            high_x(4)
            hi_split(2)
            high_x(5)
            high_x(6)
            evacuate_unit(1, 0)
            evacuate_unit(1, 1)
            act.wait_ge(s_init, 5)
            act.activation(qs.rearrange("p (a b) -> p a b", b=64),
                           pm_a[0:40, :].unsqueeze(1).to_broadcast([40, 24, 64]), ACT.Copy).then_inc(s_qz, 1)
            act.wait_ge(s_const, 16 * 7)
            act.activation(pick[:, :], pick_in[:, :], ACT.Copy).then_inc(s_qz, 1)
            act.wait_ge(s_lsum, 1)
            act.activation(lamv[:, 2:4], lamv[:, 0:2], ACT.Exp).then_inc(s_lexp, 1)
            hi_split(3)
            for n in range(2, N_A):
                for k in range(4):
                    evacuate_unit(n, k)
                    run_beside(n, k)
                hi_split(n + 2)
            act.wait_ge(s_nat, J_A)
            attention("A")
            act.wait_ge(s_oe, 4)
            for h in range(4):
                act.activation(oraw_sq[h], oraw[:, h, 0:T], ACT.Square).then_inc(s_osq, 1)
            for n in range(N_SECOND, N_BM):
                for k in range(4):
                    evacuate_unit(n, k)
                    run_beside(n, k)
                    if n == N_SECOND + 2 and k == 1:
                        act.wait_ge(s_orc, 1)
                        act.wait_ge(s_orh, 1)
                        act.activation(rsq_split[0:4, :], rsq, ACT.Copy).then_inc(s_orh, 1)
                    if n == N_BM - 2 and k == 1:
                        samples_exp_am()
                if n == N_BM - 1:
                    samples_exp_b()
                hi_split(n + 2)
                if n == N_SECOND:
                    act.wait_ge(s_ev, U0[N_SECOND])
                    act.activation(oz[:, 0:6, :], oz[:, 0:6, :], ACT.Silu).then_inc(s_silu, 1)
                if n == N_SECOND + 1:
                    act.wait_ge(s_ov, 1)
                    act.activation(rsq, pt_bank[0:4, 0:512], ACT.Sqrt, bias=eps[0:4, :]).then_inc(s_ostd, 1)
                    act.activation(rsq_split[:, :].rearrange("p (a b) -> p a b", b=64),
                                   pm_b[0:36, 0:64].unsqueeze(1).to_broadcast([36, 8, 64]), ACT.Copy).then_inc(s_orh, 1)
            attention("BM")

            evacuate_unit(N_THIRD, 0)
            act.wait_ge(s_ob, OB_UNITS // 2 + OM_UNITS)
            act.wait_ge(s_spv, 3 * NS)
            for i in range(2):
                act.activation(oh[:, 4 * i:4 * i + 4, 0:T], oz[:, 4 * i:4 * i + 4, 0:T], ACT.Copy).then_inc(s_oh, 1)
                evacuate_unit(N_THIRD, 1 + i)
            evacuate_unit(N_THIRD, 3)
            act.wait_ge(s_saT, 3)
            act.activation(r_s, bank[3][:, 0:32], ACT.Sqrt, scale=1.0 / 128, bias=eps[:, :]).then_inc(s_sex, 1)
            hi_split(N_THIRD + 2, (0,))
            act.wait_ge(s_so, 2)
            act.activation(oh[:, :, T:TT], oz[:, :, T:TT], ACT.Copy).then_inc(s_oh, 1)
            hi_split(N_THIRD + 2, (1,))
            for tile in range(2):
                act.activation(gate[:, 0:2, tile, :], gate[:, 0:2, tile, :], ACT.Sigmoid).then_inc(s_sig, 1)
            for m in range(4):
                for g in range(3 if m else 0):
                    n = POS["in", 20 + 4 * g + m]
                    evacuate(n)
                    hi_split(n + 2)
                for i in range(4 * m, 4 * m + 4):
                    c, hf = divmod(i, 2)
                    act.wait_ge(s_mix, i + 1)
                    act.activation(mixh[:, c, HALF * hf:HALF * hf + HALF], mix_t[:, i % 2, 0, :], ACT.Copy).then_inc(s_mh, 1)
                hi_split(POS["proj", m] + 2)
            for m in range(4):
                hi_split(N_OUT + m + 2)
            for j, t in enumerate(OUT_TILES):
                r = rows_of(t)
                act.wait_ge(s_y, 12 + 2 * j)
                if j:
                    act.wait_ge(s_ysq, j)
                act.activation(gate[0:r, 0:2, :, 0:256].rearrange("p a b c -> p (a b) c"),
                               y_nat[0:r, t, :].rearrange("p (a c) -> p a c", c=256), ACT.Square,
                               accum_out=ssq[0:r, 8 + t:9 + t]).then_inc(s_ysq, 1)
                act.wait_ge(s_ysq, j + 1)
                act.activation(rstd[0:r, 8 + t:9 + t], ssq[0:r, 8 + t:9 + t], ACT.Sqrt, scale=1.0 / D,
                               bias=eps[0:r, :]).then_inc(s_ystd, 1)

        @block.vector
        def _(dve):
            own = [0]

            def link(ins):
                own[0] += 1
                ins.then_inc(s_dv, 1)
                dve.wait_ge(s_dv, own[0])

            def lo_split(n, halves=(0, 1)):
                if n >= len(SEQ):
                    return
                for s in halves:
                    m = 2 * n + s
                    dve.wait_ge(s_hi, m + 1)
                    dve.tensor_tensor(w_lo[:, n % 2, 4 * s:4 * s + 4, :], w_raw[:, m % 3, :, :],
                                      w_hi[:, n % 2, 4 * s:4 * s + 4, :].bitcast(f32), ALU.subtract).then_inc(s_lo, 1)

            def split_x(i):
                t = XORDER[i]
                for kg in range(2):
                    g = 2 * i + kg
                    dve.wait_ge(s_xh, g + 1)
                    src = bank[g % 4].rearrange("p (c t) -> p c t", c=4)[:, :, 0:rows_of(t)]
                    dve.tensor_tensor(x_dst(xl, meml, t, kg), src, x_dst(xh, memh, t, kg).bitcast(f32),
                                      ALU.subtract).then_inc(s_xl, 1)

            def normalise_x(i):
                t = XORDER[i]
                r = rows_of(t)
                dve.wait_ge(s_std, i + 1)
                link(dve.reciprocal(rstd[0:r, t:t + 1], rstd[0:r, t:t + 1]))
                dve.wait_ge(s_gain[t // 5], 16)
                dve.scalar_tensor_tensor(xin[t][0:r, :], xin[t][0:r, :], rstd[0:r, t:t + 1],
                                         (g_row if t < 5 else g_row_m)[0:r, :], ALU.mult, ALU.mult).then_inc(s_xn, 1)

            normalise_x(0)
            normalise_x(1)
            lo_split(0)
            split_x(0)
            normalise_x(2)
            split_x(1)
            normalise_x(3)
            split_x(2)
            normalise_x(4)
            lo_split(1)
            split_x(3)
            normalise_x(5)
            normalise_x(6)
            split_x(4)
            lo_split(2)
            split_x(5)
            split_x(6)
            dve.wait_ge(s_const, 16 * 7)
            for i in range(2):
                link(dve.tensor_tensor(s_a[:, 64 * i:64 * i + 64], lam_in[:, 128 * i:128 * i + 64],
                                       lam_in[:, 128 * i + 64:128 * i + 128], ALU.mult))
            dve.tensor_reduce(lamv[:, 0:2], s_a.rearrange("p (i d) -> p i d", i=2), AXX, ALU.add).then_inc(s_lsum, 1)
            dve.tensor_scalar(gs[:, 1:2], gs[:, 0:1], 1.0 - LAM_INIT, None, ALU.mult)
            lo_split(3)
            dve.wait_ge(s_lexp, 1)
            link(dve.tensor_tensor(lamv[:, 4:5], lamv[:, 3:4], lamv[:, 2:3], ALU.subtract))
            link(dve.tensor_scalar(lamv[:, 5:6], lamv[:, 4:5], -LAM_INIT, None, ALU.add))

            def split_q(J):
                c, w = QS_COLS[J], 128 * len(JOBS[J][2])
                dve.wait_ge(s_qh, J - J_A + 1)
                dve.tensor_tensor(qs[32:40, c:c + w], bank[J % 2][0:NS, 0:w],
                                  qs[0:NS, c:c + w].bitcast(f32), ALU.subtract).then_inc(s_qrow, 1)

            def sample_scores(k):
                kind, b = RINGS[k]
                dve.wait_ge(s_kr[k % 2], KR[k])
                dve.wait_ge(s_qb, k + 1)
                if k:
                    dve.wait_ge(s_kd, k)
                slot = ring[:, k % 2, :, :]
                q = bank[2 + k % 2]
                if kind == "A":
                    dve.tensor_tensor(prod.rearrange("p (t c) -> p t c", t=2), slot,
                                      q.unsqueeze(1).to_broadcast([128, 2, 512]), ALU.mult).then_inc(s_km, 1)
                    dve.wait_ge(s_km, k + 1)
                    dve.tensor_reduce(s_a.rearrange("p (t c h b) -> p b t h c", t=2, c=2, h=4)[:, b],
                                      prod.rearrange("p (t h c d) -> p t h c d", t=2, h=4, c=2), AXX,
                                      ALU.add).then_inc(s_kd, 1)
                elif kind == "M":
                    dve.tensor_tensor(prod[:, 0:512].rearrange("p (t c) -> p t c", t=2), slot[:, :, 0:256],
                                      q[:, 0:256].unsqueeze(1).to_broadcast([128, 2, 256]), ALU.mult).then_inc(s_km, 1)
                    dve.wait_ge(s_km, k + 1)
                    dve.tensor_reduce(s_m.rearrange("p (t h b) -> p b t h", t=2, h=4)[:, b],
                                      prod[:, 0:512].rearrange("p (t h d) -> p t h d", t=2, h=4), AXX,
                                      ALU.add).then_inc(s_kd, 1)
                else:
                    dve.tensor_tensor(prod[:, 0:256], slot[:, 0, 0:256], q[:, 0:256], ALU.mult)
                    dve.tensor_tensor(prod[0:80, 256:512], slot[0:80, 1, 0:256], q[0:80, 256:512],
                                      ALU.mult).then_inc(s_km, 1)
                    dve.wait_ge(s_km, k + 1)
                    dve.tensor_reduce(s_1.rearrange("p (h b) -> p b h", h=4)[:, b],
                                      prod[:, 0:256].rearrange("p (h d) -> p h d", h=4), AXX, ALU.add)
                    dve.tensor_reduce(s_23[0:80, :].rearrange("p (h b) -> p b h", h=4)[:, b],
                                      prod[0:80, 256:512].rearrange("p (h d) -> p h d", h=4), AXX,
                                      ALU.add).then_inc(s_kd, 1)

            LOWEST = -3.0e38

            def biased_max(u):
                br, p, q = attn_slot(u)
                dve.wait_ge(s_S, u + 1)
                if u >= 3:
                    dve.wait_ge(s_T, u - 2)
                buf, S, k4 = sc[br][u % 3], ps[u % 2], 2 * (u % 4)
                if br == "A":
                    kn = 128 * (q + 1)
                    for c in range(2):
                        last = dve.tensor_tensor_reduce(
                            out=buf[:, 512 * c:512 * c + kn], in0=S[:, 512 * c:512 * c + kn],
                            in1=bias_a[:, p, 512 - kn:512], scale=SCALE, scalar=LOWEST, op0=ALU.add, op1=ALU.max,
                            accum_out=mx[:, k4 + c:k4 + c + 1])
                    last.then_inc(s_bm, 1)
                    n, f = 2, -1.0
                elif br == "B":
                    link(dve.tensor_tensor_reduce(
                        out=buf[:, 0:512], in0=S[:, 0:512], in1=bias_b[:, q, 3 - p:515 - p], scale=SCALE,
                        scalar=LOWEST, op0=ALU.add, op1=ALU.max, accum_out=mx[:, k4 + 1:k4 + 2]))
                    dve.tensor_tensor_reduce(
                        out=buf[:, 512:768], in0=S[:, 512:768], in1=bias_b[:, q, 515:771], scale=SCALE,
                        scalar=mx[:, k4 + 1:k4 + 2], op0=ALU.add, op1=ALU.max,
                        accum_out=mx[:, k4:k4 + 1]).then_inc(s_bm, 1)
                    n, f = 1, -1.0
                else:
                    dve.tensor_reduce(mx[:, k4:k4 + 2], S[:, :].rearrange("p (h c) -> p h c", h=2)[:, :, 0:256], AXX,
                                      ALU.max).then_inc(s_bm, 1)
                    n, f = 2, -SCALE
                dve.wait_ge(s_bm, u + 1)
                dve.tensor_scalar(nm[:, k4:k4 + n], mx[:, k4:k4 + n], f, None, ALU.mult).then_inc(s_nm, 1)

            def normalise(u):
                br, p, q = attn_slot(u)
                buf, k4 = sc[br][u % 3], 2 * (u % 4)
                n = 1 if br == "B" else 2
                dve.wait_ge(s_ex, u + 1)
                link(dve.reciprocal(rs[:, k4:k4 + n], sm[:, k4:k4 + n]))
                if br == "A":
                    kn = 128 * (q + 1)
                    link(dve.tensor_scalar(buf[:, 512:512 + kn], buf[:, 512:512 + kn], rs[:, k4 + 1:k4 + 2],
                                           lamv[:, 5:6], ALU.mult, ALU.mult))
                    dve.scalar_tensor_tensor(buf[:, 0:kn], buf[:, 0:kn], rs[:, k4:k4 + 1], buf[:, 512:512 + kn],
                                             ALU.mult, ALU.add).then_inc(s_cb, 1)
                elif br == "B":
                    dve.tensor_scalar(buf[:, 0:768], buf[:, 0:768], rs[:, k4:k4 + 1], None, ALU.mult).then_inc(s_cb, 1)
                else:
                    for hh in range(2):
                        w = buf[:, 256 * hh:256 * hh + 256]
                        last = dve.tensor_scalar(w, w, rs[:, k4 + hh:k4 + hh + 1], None, ALU.mult)
                    last.then_inc(s_cb, 1)

            def gate_output(u):
                br, p, q = attn_slot(u)
                if br == "A" or (br == "B" and q % 2 == 0):
                    return
                v = u - OA_UNITS
                pair = v // 2 if br == "B" else OB_UNITS // 2 + (v - OB_UNITS)
                dve.wait_ge(s_pv, u + 1)
                z = oz[:, 4 + q // 2, p:T:4] if br == "B" else oz[:, 6 + q, 128 * p:128 * p + 128]
                dve.tensor_tensor(z, po_bank[:, 256:384], z, ALU.mult).then_inc(s_ob, 1)

            def attention(which):
                a, b = RANGES[which]
                for s in range(a, b + 3):
                    if a <= s - 3:
                        gate_output(s - 3)
                    if s < b:
                        biased_max(s)
                    if a <= s - 1 < b:
                        normalise(s - 1)
                    if which == "BM" and s == a + 1:
                        dve.wait_ge(s_saT, 2)
                        dve.tensor_copy(aT[:, 192:288], po_bank[:, 288:384]).then_inc(s_sev, 1)
                        dve.wait_ge(s_ownb, 1)
                        own_columns(swork, 0, 0, po_bank[:, 256:288])
                        own_columns(swork, 0, 1, po_bank[:, 384:416], 80).then_inc(s_sev, 1)
                    for n, half in SPLIT_LO[which].get(s - a, ()):
                        lo_split(n, (half,))

            def samples_max(i, e, scores_, bias, rows):
                m1 = smx[0:rows, i:i + 1]
                if bias is None:
                    link(dve.tensor_reduce(m1, scores_, AXX, ALU.max))
                else:
                    link(dve.tensor_tensor_reduce(out=e, in0=scores_, in1=bias, scale=SCALE, scalar=LOWEST,
                                                  op0=ALU.add, op1=ALU.max, accum_out=m1))
                dve.tensor_scalar(snm[0:rows, i:i + 1], m1, -1.0 if bias is not None else -SCALE, None,
                                  ALU.mult).then_inc(s_snm, 1)

            def own_columns(buf, at, t, src, rows=128):
                w = buf[0:rows, at + 256 * t:at + 256 * t + 264]
                return dve.tensor_copy(w.rearrange("p (b x) -> p b x", x=33)[:, :, 0:32:8],
                                       src[0:rows, :].rearrange("p (h b) -> p b h", h=4))

            def samples_norm(i, g):
                dve.wait_ge(s_sex, i + 1)
                link(dve.reciprocal(srs[0:32, i:i + 1], ssm[0:32, i:i + 1]))
                dve.tensor_scalar(g, ident[0:32, 0:32], srs[0:32, i:i + 1], None, ALU.mult).then_inc(s_sG, 1)

            def run_beside(n, k=None):
                for what, i in beside(n, k):
                    if what == "job":
                        if i in QS_COLS:
                            split_q(i)
                    elif what == "ring":
                        sample_scores(i)
                    elif what == "rstd":
                        norm_head(i)
                    elif what == "probs_am":
                        samples_own_am()
                    else:
                        samples_max_b()

            def norm_head(h):
                dve.wait_ge(s_obc, h + 1)
                dve.wait_ge(s_silu, 1)
                link(dve.scalar_tensor_tensor(oraw[:, h, 0:T], oraw[:, h, 0:T], gs[:, 1:2],
                                              (pt_bank, po_bank)[h % 2][:, 0:512], ALU.mult, ALU.mult))
                dve.tensor_tensor(oz[:, h, 0:T], oz[:, h, 0:T], oraw[:, h, 0:T], ALU.mult).then_inc(s_oa, 1)

            def samples_norm_am():
                dve.wait_ge(s_sex, 1)
                link(dve.reciprocal(srs[0:64, 0:1], ssm[0:64, 0:1]))
                dve.tensor_scalar(g_a[0:32, :], ident[0:32, 0:32], srs[0:32, 0:1], None, ALU.mult)
                dve.tensor_scalar(g_a[32:64, :], ident[32:64, 32:64], srs[32:64, 0:1], lamv[32:64, 5:6],
                                  ALU.mult, ALU.mult).then_inc(s_sG, 1)
                samples_norm(1, g_m)

            def samples_own_am():
                dve.wait_ge(s_saT, 1)
                dve.wait_ge(s_own, 2)
                dve.tensor_copy(aT[:, 64:96], pt_bank[:, 352:384])
                for t in range(2):
                    own_columns(region, OWN_A, t, pt_bank[:, 288 + 32 * t:320 + 32 * t])
                own_columns(region, OWN_M, 0, pt_bank[:, 384:416])
                own_columns(region, OWN_M, 1, pt_bank[:, 416:448]).then_inc(s_sev, 1)
                dve.wait_ge(s_ev, U0[N_BM - 1])
                for hh in range(2):
                    r = slice(64 * hh, 64 * hh + 64)
                    dve.tensor_tensor(pm_b[r, :].rearrange("p (g k h b) -> p g k h b", g=3, k=2, h=2)[:, :, :, hh, :],
                                      qbT[r, :, :, T:TT], kbT[r, :, :, T:TT], ALU.mult).then_inc(s_new, 1)

            def samples_max_b():
                dve.wait_ge(s_sbl[1], 16)
                dve.wait_ge(s_sT, 3)
                samples_max(2, e_b, po_bank[0:32, 0:W_B], bias_sb, 32)

            for n in range(2, N_A):
                run_beside(n)
                lo_split(n + 2)
            dve.wait_ge(s_ev, ev_of(("in", 1)))
            for c in range(2):
                r = slice(64 * c, 64 * c + 64)
                dve.tensor_tensor(pm_a[r, 32 * c:32 * c + 32].rearrange("p (h b) -> p h b", h=4),
                                  qaT[r, :, T:TT], kaT[r, :, T:TT], ALU.mult).then_inc(s_new, 1)
            dve.wait_ge(s_biasa, 16)
            attention("A")
            for n in range(N_SECOND, N_BM):
                if n == N_BM - 2:
                    dve.wait_ge(s_sbl[0], 16)
                    dve.wait_ge(s_sT, 1)
                    samples_max(0, e_a, pt_bank[0:64, 0:W_A], bias_sa, 64)
                    dve.wait_ge(s_sT, 2)
                    samples_max(1, e_m, po_bank[0:32, 0:256], None, 32)
                for k in range(4):
                    run_beside(n, k)
                    if n == N_BM - 2 and k == 2:
                        samples_norm_am()
                if n == N_SECOND + 2:
                    dve.wait_ge(s_orh, 2)
                    dve.tensor_tensor(rsq_split[32:36, :], rsq, rsq_split[0:4, :].bitcast(f32),
                                      ALU.subtract).then_inc(s_orl, 1)
                if n == N_BM - 1:
                    samples_norm(2, g_b)
                else:
                    lo_split(n + 2)
                if n == N_BM - 3:
                    dve.memset(own_a, 0.0).then_inc(s_own, 1)
                    dve.memset(own_m, 0.0).then_inc(s_own, 1)
                if n == N_SECOND + 1:
                    dve.wait_ge(s_ostd, 1)
                    dve.reciprocal(rsq, rsq).then_inc(s_orc, 1)
            dve.wait_ge(s_biasb, 16)
            attention("BM")

            def split_outputs(i):
                dve.wait_ge(s_oh, i + 1)
                dve.tensor_tensor(ol[:, 4 * i:4 * i + 4, 0:T], oz[:, 4 * i:4 * i + 4, 0:T],
                                  oh[:, 4 * i:4 * i + 4, 0:T].bitcast(f32), ALU.subtract).then_inc(s_ol, 1)

            dve.wait_ge(s_spv, 3 * NS)
            dve.tensor_copy(ov_sa, pj[1][0:32, :]).then_inc(s_sov, 1)
            dve.tensor_copy(ov_sb, pj[1][64:96, :]).then_inc(s_sov, 1)
            link(dve.tensor_tensor(t_a, vn_a, aT[:, 64:96], ALU.mult))
            for hh in range(2):
                r = slice(64 * hh, 64 * hh + 64)
                link(dve.tensor_tensor(t_b[r, :].rearrange("p (g k b) -> p g k b", g=3, k=2),
                                       aT[r, 192:288].rearrange("p (g k h b) -> p g k h b", g=3, k=2, h=2)[:, :, :, hh, :],
                                       vn_b[r, :].rearrange("p (g k b) -> p g k b", g=3, k=2), ALU.mult))
            link(dve.tensor_reduce(t_b2[:, 0:16], t_b.rearrange("p (g x) -> p x g", g=3), AXX, ALU.add))
            dve.wait_ge(s_sot, 1)
            link(dve.tensor_tensor(o_as.rearrange("p (h b) -> p h b", h=4),
                                   po_bank[:, 0:160].rearrange("p (h x) -> p h x", x=40)[:, :, 0:8],
                                   t_a.rearrange("p (h b) -> p h b", h=4), ALU.add))
            dve.tensor_tensor(sq_s, o_as, o_as, ALU.mult).then_inc(s_so, 1)
            split_outputs(0)
            dve.wait_ge(s_sot, 2)
            for hh in range(2):
                r = slice(64 * hh, 64 * hh + 64)

                def heads(c):
                    return pt_bank[r, c:c + 96].rearrange("p (k x) -> p k x", x=48)[:, :, 8 * hh:8 * hh + 8]
                z = oz[r, 6:8, T:TT]
                dve.tensor_tensor(z, heads(0), z, ALU.mult)
                w = t_b2[r, 0:16].rearrange("p (k b) -> p k b", k=2)
                link(dve.tensor_tensor(w, heads(64), w, ALU.add))
            z = oz[:, 4:6, T:TT]
            dve.tensor_tensor(z, z, t_b2[:, 0:16].rearrange("p (k b) -> p k b", k=2), ALU.mult)
            split_outputs(1)
            dve.wait_ge(s_sex, 4)
            link(dve.reciprocal(r_s, r_s))
            link(dve.scalar_tensor_tensor(t_a, o_as, gs[:, 1:2], r_s, ALU.mult, ALU.mult))
            z = oz[:, 0:4, T:TT]
            dve.tensor_tensor(z, z, t_a.rearrange("p (h b) -> p h b", h=4), ALU.mult).then_inc(s_so, 1)
            dve.wait_ge(s_oh, 3)
            dve.tensor_tensor(ol[:, :, T:TT], oz[:, :, T:TT], oh[:, :, T:TT].bitcast(f32), ALU.subtract).then_inc(s_ol, 1)
            lo_split(N_THIRD + 2)

            def mixed_lo(i):
                c, hf = divmod(i, 2)
                dve.wait_ge(s_mh, i + 1)
                cols = slice(HALF * hf, HALF * hf + HALF)
                dve.tensor_tensor(mixl[:, c, cols], mix_t[:, i % 2, 0, :], mixh[:, c, cols].bitcast(f32),
                                  ALU.subtract).then_inc(s_ml, 1)

            for m in range(4):
                for g in range(3 if m else 0):
                    lo_split(POS["in", 20 + 4 * g + m] + 2)
                dve.wait_ge(s_ev, ev_of(("in", 28 + m)))
                for i in range(4 * m, 4 * m + 4):
                    tile, hf = (i // 2) % 2, i % 2
                    cols = slice(HALF * hf, HALF * hf + HALF)
                    dve.wait_ge(s_pp, i + 1)
                    if i in (0, 2):
                        dve.wait_ge(s_sig, 1 + i // 2)
                    if i >= 2:
                        dve.wait_ge(s_ml, i - 1)
                    for br in range(3):
                        last = dve.tensor_tensor(mix_t[:, i % 2, br, :], bank[3 * (i % 2) + br][:, 0:HALF],
                                                 gate[:, br, tile, cols], ALU.mult)
                    last.then_inc(s_mx, 1)
                    dve.wait_ge(s_mx, i + 1)
                    t0 = mix_t[:, i % 2, 0, :]
                    link(dve.tensor_tensor(t0, t0, mix_t[:, i % 2, 1, :], ALU.add))
                    dve.tensor_tensor(t0, t0, mix_t[:, i % 2, 2, :], ALU.add).then_inc(s_mix, 1)
                    if i % 4:
                        mixed_lo(i - 1)
                mixed_lo(4 * m + 3)
                lo_split(POS["proj", m] + 2)
            dve.wait_ge(s_yl, 80)
            dve.wait_ge(s_gf, 16)

            def final_norm(j):
                t = OUT_TILES[j]
                r = rows_of(t)
                dve.wait_ge(s_ystd, j + 1)
                link(dve.reciprocal(rstd[0:r, 8 + t:9 + t], rstd[0:r, 8 + t:9 + t]))
                for c in range(2):
                    cols = slice(512 * c, 512 * c + 512)
                    dve.scalar_tensor_tensor(y_nat[0:r, t, cols], y_nat[0:r, t, cols], rstd[0:r, 8 + t:9 + t],
                                             g_fin[0:r, cols], ALU.mult, ALU.mult).then_inc(s_yo, 1)

            for i, (m, t) in enumerate(OUT_ORDER):
                r = rows_of(t)
                dve.wait_ge(s_po, i + 1)
                y = y_nat[0:r, t, CW * m:CW * m + CW]
                dve.tensor_tensor(y, pj[i % 2][0:r, 0:CW], y, ALU.add).then_inc(s_y, 1)
                if i in (4, 9):
                    lo_split(N_OUT + m + 2)
                if i > 11 and m == 3:
                    final_norm((i - 13) // 2)
            final_norm(4)


def constants():
    f = np.float32
    slope = [2.0 ** (-2.0 * (h + 1)) for h in range(4)]
    neg = -1e30 / SCALE

    def bias(dist, ok, h):
        return np.where(ok, -slope[h] * dist / SCALE, neg)

    p = np.arange(128)[:, None]
    y = np.arange(512)[None, :] - 384
    bias_a = np.stack([bias(p - y, p >= y, h) for h in range(4)], 1)
    d1 = 4 * p - (np.arange(515)[None, :] - 3)
    d2 = 4 * (p - np.arange(128)[None, :])
    bias_b = np.stack([np.concatenate([bias(d1, (d1 >= 0) & (d1 <= 128), h), bias(d2, d2 >= 0, h),
                                       bias(d2, (d2 >= 0) & (d2 % 16 == 0), h)], 1) for h in range(4)], 1)
    rows = np.arange(64)
    ha = (rows // 8) % 4
    bias_sa = np.stack([bias(256 - np.arange(W_A), np.ones(W_A, bool), h) for h in ha])
    cached = [d * (n - np.arange(n)) for n, d in zip(G_ROWS, DIL)]
    dist_b = np.concatenate(cached + [np.zeros(3)])
    bias_sb = np.stack([bias(dist_b, np.ones(W_B, bool), h) for h in ha[:32]])
    sel = np.zeros((128, 4, 4))
    pick = np.zeros((40, NS))
    pick[np.arange(NS), np.arange(NS)] = pick[32 + np.arange(NS), np.arange(NS)] = 1.0
    for h in range(4):
        sel[:, h, h] = 1.0 / 128
    return {"c_ident": np.eye(128, dtype=f), "c_bias_a": bias_a.astype(f), "c_bias_b": bias_b.astype(f),
            "c_bias_sa": bias_sa.astype(f), "c_bias_sb": bias_sb.astype(f), "c_selh": sel.astype(f),
            "c_pick": pick.astype(f)}


_INS = ["x_prompt", "x_sample", "mem_prompt", "cache_diff_kv", "page_table", "cache_win1_kv", "cache_win2_kv",
        "cache_win3_kv", "cache_mem_kv", "g_norm", "w_in", "g_mem", "w_mem_kv", "lambda_q1", "lambda_k1",
        "lambda_q2", "lambda_k2", "g_subln", "w_proj_a", "w_proj_b", "w_proj_m", "w_out", "g_final"]
_OUTS = [(1, 512, 1024), (8, 1, 1024), (1, 1, 512, 2, 4, 128), (1, 1, 128, 2, 4, 64), (1, 1, 512, 2, 4, 64),
         (1, 1, 512, 2, 4, 64), (1, 1, 256, 2, 4, 64), (1, 8, 1, 2, 4, 128), (1, 8, 1, 2, 4, 64),
         (1, 8, 1, 2, 4, 64), (1, 8, 1, 2, 4, 64)]


def kernel(**inputs):
    import concourse.bacc as bacc
    from concourse.bass_utils import run_bass_kernel_spmd

    nc = bacc.Bacc("TRN2", target_bir_lowering=False, num_devices=1)
    arrays = {f"in_{n}": np.ascontiguousarray(inputs[n]) for n in _INS}
    arrays.update({f"in_{n}": a for n, a in constants().items()})
    ins = {n[3:]: nc.dram_tensor(n, a.shape, mybir.dt.from_np(a.dtype), kind="ExternalInput").ap()
           for n, a in arrays.items()}
    outs = [nc.dram_tensor(f"out_{i}", s, mybir.dt.float32, kind="ExternalOutput").ap() for i, s in enumerate(_OUTS)]
    build_kernel(nc, ins, outs)
    r = run_bass_kernel_spmd(nc, [arrays], core_ids=[0])
    return tuple(r.results[0][f"out_{i}"] for i in range(len(_OUTS)))
```
